# Optimizing a Trainium2 kernel written in Bass

```python
import jax, jax.numpy as jnp
from jax import lax
import numpy as np

D_MODEL = 1024
BATCH = 1
SEQ = 1024
DEPTH = 1

CTX_LEN = 256
GRID_W = 64
EPS = 1e-6
N_MOD = 6

A_WIDTH = D_MODEL
A_GROUPS = 8
A_GROUP_DIM = A_WIDTH // A_GROUPS
A_CHUNK = 128

B_HEADS = 4
B_DK = D_MODEL // 2 // B_HEADS
B_DV = D_MODEL // B_HEADS
B_QK_WIDTH = B_HEADS * B_DK
B_V_WIDTH = B_HEADS * B_DV
GATE_RANK = 16
GATE_TEMP = 16.0
GLA_CHUNK = 64

D_FF = ((8 * D_MODEL // 3 + 255) // 256) * 256

IN_SIZES = (A_WIDTH, A_WIDTH, B_QK_WIDTH, B_QK_WIDTH, B_V_WIDTH, B_V_WIDTH,
            GATE_RANK, GATE_RANK, D_MODEL, D_MODEL)


def _split_offsets():
    offs, acc = [], 0
    for s in IN_SIZES[:-1]:
        acc += s
        offs.append(acc)
    return offs

def _rmsnorm(x, g):
    xf = x.astype(jnp.float32)
    y = xf * lax.rsqrt(jnp.mean(xf * xf, axis=-1, keepdims=True) + EPS)
    return (y * g.astype(jnp.float32)).astype(x.dtype)

def _layernorm(x, g, b):
    xf = x.astype(jnp.float32)
    mu = jnp.mean(xf, axis=-1, keepdims=True)
    xc = xf - mu
    y = xc * lax.rsqrt(jnp.mean(xc * xc, axis=-1, keepdims=True) + EPS)
    return (y * g.astype(jnp.float32) + b.astype(jnp.float32)).astype(x.dtype)

def _modulate(xn, shift, scale):
    return xn * (1 + scale) + shift

def _chunk_mlp(u, v, n_chunks, ln_v_g, ln_v_b, w_spatial, b_spatial):
    B, T, _ = u.shape
    u = jax.nn.gelu(u, approximate=False)
    v = _layernorm(jax.nn.gelu(v, approximate=False), ln_v_g, ln_v_b)
    vc = v.reshape(B, n_chunks, A_CHUNK, A_GROUPS, A_GROUP_DIM)
    mixed = jnp.einsum('gpq,bnqgc->bnpgc', w_spatial, vc) + jnp.transpose(b_spatial)[:, :, None]
    return u * mixed.reshape(B, T, A_WIDTH)

def _gla_heads(q, k, v, af, ab, w_af, b_af, w_ab, b_ab):
    B, T, _ = q.shape
    f32 = jnp.float32
    q = q.astype(f32).reshape(B, T, B_HEADS, B_DK) * (B_DK ** -0.5)
    k = k.astype(f32).reshape(B, T, B_HEADS, B_DK)
    v = v.astype(f32).reshape(B, T, B_HEADS, B_DV)
    lf = (jax.nn.log_sigmoid((af @ w_af + b_af).astype(f32)) / GATE_TEMP).reshape(B, T, B_HEADS, B_DK)
    lb = (jax.nn.log_sigmoid((ab @ w_ab + b_ab).astype(f32)) / GATE_TEMP).reshape(B, T, B_HEADS, B_DK)
    return q, k, v, lf, lb

def _gla_scan(q, k, v, log_a, s0):
    B, T, H, DK = q.shape
    DV = v.shape[-1]
    n = T // GLA_CHUNK

    def to_chunks(t):
        return jnp.moveaxis(t.reshape(B, n, GLA_CHUNK, H, t.shape[-1]), 1, 0)

    mask = jnp.tril(jnp.ones((GLA_CHUNK, GLA_CHUNK), dtype=bool))

    def step(s, xs):
        qc, kc, vc, gc = xs
        b = jnp.cumsum(gc, axis=1)
        b_last = b[:, -1]
        q_dec = qc * jnp.exp(b)
        k_inv = kc * jnp.exp(-b)
        k_state = kc * jnp.exp(b_last[:, None] - b)
        o_inter = jnp.einsum('bchk,bhkv->bchv', q_dec, s)
        att = jnp.where(mask, jnp.einsum('bihk,bjhk->bhij', q_dec, k_inv), 0.0)
        o_intra = jnp.einsum('bhij,bjhv->bihv', att, vc)
        s_new = jnp.exp(b_last)[..., None] * s + jnp.einsum('bchk,bchv->bhkv', k_state, vc)
        return s_new, o_inter + o_intra

    s_fin, o = lax.scan(step, s0, (to_chunks(q), to_chunks(k), to_chunks(v), to_chunks(log_a)))
    o = jnp.moveaxis(o, 0, 1).reshape(B, T, H, DV)
    return o, s_fin

def _gla_out(o, r, gla_norm_g, dtype):
    B, T = o.shape[0], o.shape[1]
    o = o * lax.rsqrt(jnp.mean(o * o, axis=-1, keepdims=True) + EPS)
    o = o.reshape(B, T, B_V_WIDTH) * gla_norm_g.astype(jnp.float32)
    return o.astype(dtype) * jax.nn.silu(r)

def _token_mixer(h_lat, h_ctx, w_in, ln_v_g, ln_v_b, w_spatial, b_spatial,
                 w_alpha_f, b_alpha_f, w_alpha_b, b_alpha_b, gla_norm_g,
                 w_branch_a, w_branch_b, w_out, with_ctx_out):
    offs = _split_offsets()
    u_l, v_l, q_l, k_l, vv_l, r_l, af_l, ab_l, ga_l, gb_l = jnp.split(h_lat @ w_in, offs, axis=-1)
    u_c, v_c, q_c, k_c, vv_c, r_c, af_c, ab_c, ga_c, gb_c = jnp.split(h_ctx @ w_in, offs, axis=-1)
    B = h_lat.shape[0]

    ql, kl, vl, lfl, lbl = _gla_heads(q_l, k_l, vv_l, af_l, ab_l, w_alpha_f, b_alpha_f, w_alpha_b, b_alpha_b)
    qc, kc, vc, lfc, lbc = _gla_heads(q_c, k_c, vv_c, af_c, ab_c, w_alpha_f, b_alpha_f, w_alpha_b, b_alpha_b)
    s0 = jnp.zeros((B, B_HEADS, B_DK, B_DV), jnp.float32)
    fl = lambda t: jnp.flip(t, axis=1)
    o_cf, s_cf = _gla_scan(qc, kc, vc, lfc, s0)
    o_lf, _ = _gla_scan(ql, kl, vl, lfl, s_cf)
    o_cb, s_cb = _gla_scan(fl(qc), fl(kc), fl(vc), fl(lbc), s0)
    o_lb, _ = _gla_scan(fl(ql), fl(kl), fl(vl), fl(lbl), s_cb)
    b_lat = _gla_out(o_lf + fl(o_lb), r_l, gla_norm_g, h_lat.dtype)

    rows = h_lat.shape[1] // GRID_W
    a_lat = _chunk_mlp(u_l, v_l, rows // (A_CHUNK // GRID_W), ln_v_g, ln_v_b, w_spatial, b_spatial)

    def merge(a_out, b_out, ga, gb):
        y = jax.nn.sigmoid(ga) * (a_out @ w_branch_a) + jax.nn.sigmoid(gb) * (b_out @ w_branch_b)
        return y @ w_out

    out_lat = merge(a_lat, b_lat, ga_l, gb_l)
    if not with_ctx_out:
        return out_lat, None
    b_ctx = _gla_out(o_cf + fl(o_cb), r_c, gla_norm_g, h_ctx.dtype)
    a_ctx = _chunk_mlp(u_c, v_c, h_ctx.shape[1] // A_CHUNK, ln_v_g, ln_v_b, w_spatial, b_spatial)
    return out_lat, merge(a_ctx, b_ctx, ga_c, gb_c)

def _swiglu(h, w_ffn_in, w_ffn_out):
    a, g = jnp.split(h @ w_ffn_in, 2, axis=-1)
    return (jax.nn.silu(g) * a) @ w_ffn_out

def first_inputs(seed: int = 0) -> dict:
    key = jax.random.key(seed)
    ks = jax.random.split(key, 24)
    f32 = jnp.float32
    nrm = lambda k, shape, s: jax.random.normal(k, shape, f32) * s
    L, D = DEPTH, D_MODEL
    return {
        "x": nrm(ks[0], (BATCH, SEQ, D), 1.0),
        "c": nrm(ks[1], (BATCH, D), 1.0),
        "ctx": nrm(ks[2], (BATCH, CTX_LEN, D), 1.0),
        "c_ctx": nrm(ks[3], (D,), 1.0),
        "w_ada": nrm(ks[4], (L, D, N_MOD * D), 0.5 * D ** -0.5),
        "b_ada": nrm(ks[5], (L, N_MOD * D), 0.02),
        "norm1_g": 1.0 + nrm(ks[6], (L, D), 0.02),
        "w_in": nrm(ks[7], (L, D, sum(IN_SIZES)), D ** -0.5),
        "ln_v_g": 1.0 + nrm(ks[8], (L, A_WIDTH), 0.02),
        "ln_v_b": nrm(ks[9], (L, A_WIDTH), 0.02),
        "w_spatial": nrm(ks[10], (L, A_GROUPS, A_CHUNK, A_CHUNK), A_CHUNK ** -0.5),
        "b_spatial": 1.0 + nrm(ks[11], (L, A_GROUPS, A_CHUNK), 0.02),
        "w_alpha_f": nrm(ks[12], (L, GATE_RANK, B_QK_WIDTH), GATE_RANK ** -0.5),
        "b_alpha_f": nrm(ks[13], (L, B_QK_WIDTH), 0.02),
        "w_alpha_b": nrm(ks[14], (L, GATE_RANK, B_QK_WIDTH), GATE_RANK ** -0.5),
        "b_alpha_b": nrm(ks[15], (L, B_QK_WIDTH), 0.02),
        "gla_norm_g": 1.0 + nrm(ks[16], (L, B_V_WIDTH), 0.02),
        "w_branch_a": nrm(ks[17], (L, A_WIDTH, D), A_WIDTH ** -0.5),
        "w_branch_b": nrm(ks[18], (L, B_V_WIDTH, D), B_V_WIDTH ** -0.5),
        "w_out": nrm(ks[19], (L, D, D), D ** -0.5),
        "norm2_g": 1.0 + nrm(ks[20], (L, D), 0.02),
        "w_ffn_in": nrm(ks[21], (L, D, 2 * D_FF), D ** -0.5),
        "w_ffn_out": nrm(ks[22], (L, D_FF, D), D_FF ** -0.5),
        "final_norm_g": 1.0 + nrm(ks[23], (D,), 0.02),
    }

def first_block(x, c, ctx, c_ctx, w_ada, b_ada, norm1_g, w_in, ln_v_g, ln_v_b, w_spatial, b_spatial,
              w_alpha_f, b_alpha_f, w_alpha_b, b_alpha_b, gla_norm_g, w_branch_a, w_branch_b,
              w_out, norm2_g, w_ffn_in, w_ffn_out, final_norm_g):
    for l in range(DEPTH):
        update_ctx = l < DEPTH - 1
        mod = jnp.split((jax.nn.silu(c) @ w_ada[l] + b_ada[l])[:, None, :], N_MOD, axis=-1)
        mod_c = jnp.split(jax.nn.silu(c_ctx) @ w_ada[l] + b_ada[l], N_MOD, axis=-1)
        sh1, sc1, g1, sh2, sc2, g2 = mod
        sh1c, sc1c, g1c, sh2c, sc2c, g2c = mod_c

        h_lat = _modulate(_rmsnorm(x, norm1_g[l]), sh1, sc1)
        h_ctx = _modulate(_rmsnorm(ctx, norm1_g[l]), sh1c, sc1c)
        mix_l, mix_c = _token_mixer(h_lat, h_ctx, w_in[l], ln_v_g[l], ln_v_b[l], w_spatial[l], b_spatial[l],
                                    w_alpha_f[l], b_alpha_f[l], w_alpha_b[l], b_alpha_b[l], gla_norm_g[l],
                                    w_branch_a[l], w_branch_b[l], w_out[l], update_ctx)
        x = x + g1 * mix_l
        x = x + g2 * _swiglu(_modulate(_rmsnorm(x, norm2_g[l]), sh2, sc2), w_ffn_in[l], w_ffn_out[l])
        if update_ctx:
            ctx = ctx + g1c * mix_c
            ctx = ctx + g2c * _swiglu(_modulate(_rmsnorm(ctx, norm2_g[l]), sh2c, sc2c), w_ffn_in[l], w_ffn_out[l])
    return _rmsnorm(x, final_norm_g)


_first_inputs = first_inputs


def first_inputs(seed=0):
    import zlib

    import numpy as np

    out = dict(_first_inputs(seed))
    spreads = {}
    factors = {}
    for name, (base, spread) in spreads.items():
        noise = np.random.default_rng([zlib.crc32(name.encode()), seed]).standard_normal(out[name].shape)
        drawn = base * np.exp(spread * noise) if base else spread * noise
        out[name] = __import__('jax').numpy.asarray(drawn.astype(out[name].dtype))
    for name, factor in factors.items():
        out[name] = (out[name] * factor).astype(out[name].dtype)
    return out


_narrow_inputs = first_inputs


def first_inputs(seed=0):

    out = dict(_narrow_inputs(seed))
    wider = {'ctx': 6.61,
     'c_ctx': 9.99,
     'norm1_g': 9.94,
     'ln_v_g': 12.0,
     'ln_v_b': 12.0,
     'b_spatial': 12.0,
     'w_alpha_f': 4.15,
     'b_alpha_f': 12.0,
     'w_alpha_b': 5.21,
     'b_alpha_b': 12.0,
     'gla_norm_g': 12.0,
     'norm2_g': 10.64,
     'final_norm_g': 3.26}
    for name, times in wider.items():
        mean = out[name].mean()
        out[name] = (mean + times * (out[name] - mean)).astype(out[name].dtype)
    return out


LRU_WIDTH = D_MODEL
LRU_HEADS = 16
LRU_BLOCK = LRU_WIDTH // LRU_HEADS
CONV_WIDTH = 4
CONV_LEFT = 2
RGLRU_C = 8.0
N_DIR = 2
N_HEADS = 16
N_KV_HEADS = 4
HEAD_DIM = 64
GROUP = N_HEADS // N_KV_HEADS
WINDOW = 128
BLOCK = 128
D_FF_2 = ((8 * D_MODEL // 3 + 255) // 256) * 256
N_BRANCH = 2
Q_W = N_HEADS * HEAD_DIM
KV_W = N_KV_HEADS * HEAD_DIM
IN_W = 2 * LRU_WIDTH + Q_W + 2 * KV_W + N_BRANCH * D_MODEL
NEG_INF = -1e30


def rmsnorm(x, g):
    xf = x.astype(jnp.float32)
    y = xf * lax.rsqrt(jnp.mean(xf * xf, axis=-1, keepdims=True) + EPS)
    return (y * g.astype(jnp.float32)).astype(x.dtype)

def centred_depthwise_conv(u, w, b):
    s = u.shape[1]
    up = jnp.pad(u, ((0, 0), (CONV_LEFT, CONV_WIDTH - 1 - CONV_LEFT), (0, 0)))
    out = up[:, 0:s] * w[0]
    for k in range(1, CONV_WIDTH):
        out = out + up[:, k:k + s] * w[k]
    return out + b

def _linear_combine(left, right):
    a1, b1 = left
    a2, b2 = right
    return a1 * a2, a2 * b1 + b2

def rg_lru(u, lam, wa, ba, wx, bx, reverse):
    bsz, s, c = u.shape
    ub = u.reshape(bsz, s, LRU_HEADS, LRU_BLOCK)
    r = jax.nn.sigmoid(jnp.einsum("bshi,hij->bshj", ub, wa.astype(jnp.float32)).reshape(bsz, s, c) + ba.astype(jnp.float32))
    i = jax.nn.sigmoid(jnp.einsum("bshi,hij->bshj", ub, wx.astype(jnp.float32)).reshape(bsz, s, c) + bx.astype(jnp.float32))
    log_a = -RGLRU_C * r * jax.nn.softplus(-lam.astype(jnp.float32))
    a = jnp.exp(log_a)
    beta = jnp.sqrt(jnp.maximum(-jnp.expm1(2.0 * log_a), 0.0))
    _, h = lax.associative_scan(_linear_combine, (a, beta * (i * u)), axis=1, reverse=reverse)
    return h

def banded_alibi_sink_attention(q, k, v, sink):
    bsz, s = q.shape[0], q.shape[1]
    nb = s // BLOCK
    qb = (q.astype(jnp.float32) * (HEAD_DIM ** -0.5)).reshape(bsz, nb, BLOCK, N_KV_HEADS, GROUP, HEAD_DIM)

    def key_blocks(t):
        tp = jnp.pad(t.astype(jnp.float32), ((0, 0), (BLOCK, BLOCK), (0, 0), (0, 0)))
        tp = tp.reshape(bsz, nb + 2, BLOCK, N_KV_HEADS, HEAD_DIM)
        return jnp.concatenate([tp[:, j:j + nb] for j in range(3)], axis=2)

    kb = key_blocks(k)
    vb = key_blocks(v)
    scores = jnp.einsum("bnqkgd,bnskd->bnkgqs", qb, kb)

    q_loc = jnp.arange(BLOCK)
    k_loc = jnp.arange(3 * BLOCK)
    dist = q_loc[:, None] + BLOCK - k_loc[None, :]
    kpos = jnp.arange(nb)[:, None] * BLOCK - BLOCK + k_loc[None, :]
    valid = (jnp.abs(dist) <= WINDOW)[None] & ((kpos >= 0) & (kpos < s))[:, None, :]

    slopes = jnp.exp2(-8.0 * (jnp.arange(N_HEADS, dtype=jnp.float32) + 1.0) / N_HEADS)
    alibi = -slopes.reshape(N_KV_HEADS, GROUP, 1, 1) * jnp.abs(dist).astype(jnp.float32)
    scores = jnp.where(valid[None, :, None, None], scores + alibi, NEG_INF)

    sink_l = sink.astype(jnp.float32).reshape(1, 1, N_KV_HEADS, GROUP, 1, 1)
    m = jnp.maximum(jnp.max(scores, axis=-1, keepdims=True), sink_l)
    p = jnp.exp(scores - m)
    denom = jnp.sum(p, axis=-1, keepdims=True) + jnp.exp(sink_l - m)
    o = jnp.einsum("bnkgqs,bnskd->bnqkgd", p / denom, vb)
    return o.reshape(bsz, s, Q_W)

def second_inputs(seed: int = 0) -> dict:
    key = jax.random.key(seed)
    ks = jax.random.split(key, 20)
    f32 = jnp.float32
    x = jax.random.normal(ks[0], (BATCH, SEQ, D_MODEL), f32)
    norm_mix_g = 1.0 + 0.05 * jax.random.normal(ks[1], (DEPTH, D_MODEL), f32)
    w_in = jax.random.normal(ks[2], (DEPTH, D_MODEL, IN_W), f32) * D_MODEL ** -0.5
    b_gate = 0.01 * jax.random.normal(ks[3], (DEPTH, N_BRANCH * D_MODEL), f32)
    conv_w = jax.random.normal(ks[4], (DEPTH, CONV_WIDTH, LRU_WIDTH), f32) * CONV_WIDTH ** -0.5
    conv_b = 0.01 * jax.random.normal(ks[5], (DEPTH, LRU_WIDTH), f32)
    u = jax.random.uniform(ks[6], (DEPTH, N_DIR, LRU_WIDTH), f32, minval=0.9, maxval=0.999)
    p = u ** (1.0 / RGLRU_C)
    lru_lambda = jnp.log(p) - jnp.log1p(-p)
    lru_wa = jax.random.normal(ks[7], (DEPTH, N_DIR, LRU_HEADS, LRU_BLOCK, LRU_BLOCK), f32) * LRU_BLOCK ** -0.5
    lru_ba = 0.01 * jax.random.normal(ks[8], (DEPTH, N_DIR, LRU_WIDTH), f32)
    lru_wx = jax.random.normal(ks[9], (DEPTH, N_DIR, LRU_HEADS, LRU_BLOCK, LRU_BLOCK), f32) * LRU_BLOCK ** -0.5
    lru_bx = 0.01 * jax.random.normal(ks[10], (DEPTH, N_DIR, LRU_WIDTH), f32)
    attn_sink = 0.5 * jax.random.normal(ks[11], (DEPTH, N_HEADS), f32)
    w_out = jax.random.normal(ks[12], (DEPTH, D_MODEL, D_MODEL), f32) * D_MODEL ** -0.5
    norm_ffn_g = 1.0 + 0.05 * jax.random.normal(ks[13], (DEPTH, D_MODEL), f32)
    w_ffn_in = jax.random.normal(ks[14], (DEPTH, D_MODEL, 2 * D_FF_2), f32) * D_MODEL ** -0.5
    w_ffn_out = jax.random.normal(ks[15], (DEPTH, D_FF_2, D_MODEL), f32) * D_FF_2 ** -0.5
    norm_final_g = 1.0 + 0.05 * jax.random.normal(ks[16], (D_MODEL,), f32)
    return {"x": x, "norm_mix_g": norm_mix_g, "w_in": w_in, "b_gate": b_gate,
            "conv_w": conv_w, "conv_b": conv_b, "lru_lambda": lru_lambda,
            "lru_wa": lru_wa, "lru_ba": lru_ba, "lru_wx": lru_wx, "lru_bx": lru_bx,
            "attn_sink": attn_sink, "w_out": w_out, "norm_ffn_g": norm_ffn_g,
            "w_ffn_in": w_ffn_in, "w_ffn_out": w_ffn_out, "norm_final_g": norm_final_g}

def second_block(x, norm_mix_g, w_in, b_gate, conv_w, conv_b, lru_lambda, lru_wa, lru_ba,
              lru_wx, lru_bx, attn_sink, w_out, norm_ffn_g, w_ffn_in, w_ffn_out, norm_final_g):
    bsz, s, _ = x.shape
    splits = [LRU_WIDTH, 2 * LRU_WIDTH, 2 * LRU_WIDTH + Q_W, 2 * LRU_WIDTH + Q_W + KV_W,
              2 * LRU_WIDTH + Q_W + 2 * KV_W]
    for l in range(DEPTH):
        xn = rmsnorm(x, norm_mix_g[l])
        proj = xn @ w_in[l]
        u, g_lru, q, k, v, z = jnp.split(proj, splits, axis=-1)

        uc = centred_depthwise_conv(u, conv_w[l], conv_b[l]).astype(jnp.float32)
        h_fwd = rg_lru(uc, lru_lambda[l, 0], lru_wa[l, 0], lru_ba[l, 0], lru_wx[l, 0], lru_bx[l, 0], False)
        h_bwd = rg_lru(uc, lru_lambda[l, 1], lru_wa[l, 1], lru_ba[l, 1], lru_wx[l, 1], lru_bx[l, 1], True)
        y_a = ((h_fwd + h_bwd) * jax.nn.gelu(g_lru.astype(jnp.float32))).astype(x.dtype)

        y_b = banded_alibi_sink_attention(
            q.reshape(bsz, s, N_HEADS, HEAD_DIM),
            k.reshape(bsz, s, N_KV_HEADS, HEAD_DIM),
            v.reshape(bsz, s, N_KV_HEADS, HEAD_DIM),
            attn_sink[l]).astype(x.dtype)

        gates = jax.nn.sigmoid(z + b_gate[l]).reshape(bsz, s, N_BRANCH, D_MODEL)
        merged = gates[:, :, 0] * y_a + gates[:, :, 1] * y_b
        x = x + merged @ w_out[l]

        xn2 = rmsnorm(x, norm_ffn_g[l])
        gu = xn2 @ w_ffn_in[l]
        ff_gate, ff_up = jnp.split(gu, [D_FF_2], axis=-1)
        x = x + (jax.nn.silu(ff_gate) * ff_up) @ w_ffn_out[l]
    return rmsnorm(x, norm_final_g)


def setup_inputs(seed=0):
    out = dict(first_inputs(seed))
    for name, value in second_inputs(seed + 1).items():
        if name != "x":
            out[name + "_2"] = value
    return out


def reference(
    x, c, ctx, c_ctx, w_ada, b_ada, norm1_g, w_in, ln_v_g, ln_v_b, w_spatial, b_spatial,
    w_alpha_f, b_alpha_f, w_alpha_b, b_alpha_b, gla_norm_g, w_branch_a, w_branch_b, w_out,
    norm2_g, w_ffn_in, w_ffn_out, final_norm_g, norm_mix_g_2, w_in_2, b_gate_2, conv_w_2,
    conv_b_2, lru_lambda_2, lru_wa_2, lru_ba_2, lru_wx_2, lru_bx_2, attn_sink_2, w_out_2,
    norm_ffn_g_2, w_ffn_in_2, w_ffn_out_2, norm_final_g_2,
):
    x = first_block(
        x, c, ctx, c_ctx, w_ada, b_ada, norm1_g, w_in, ln_v_g, ln_v_b, w_spatial, b_spatial,
        w_alpha_f, b_alpha_f, w_alpha_b, b_alpha_b, gla_norm_g, w_branch_a, w_branch_b, w_out,
        norm2_g, w_ffn_in, w_ffn_out, final_norm_g,
    )
    return second_block(
        x, norm_mix_g_2, w_in_2, b_gate_2, conv_w_2, conv_b_2, lru_lambda_2, lru_wa_2, lru_ba_2,
        lru_wx_2, lru_bx_2, attn_sink_2, w_out_2, norm_ffn_g_2, w_ffn_in_2, w_ffn_out_2,
        norm_final_g_2,
    )


_drawn_inputs = setup_inputs


def setup_inputs(seed=0):
    import zlib

    import numpy as np

    out = dict(_drawn_inputs(seed))
    spreads = {}
    factors = {'b_alpha_f': 7.525,
     'b_alpha_b': 5.873,
     'b_gate_2': 33.739,
     'lru_ba_2': 61.502,
     'lru_bx_2': 42.102,
     'attn_sink_2': 8.0}
    for name, (base, spread) in spreads.items():
        noise = np.random.default_rng([zlib.crc32(name.encode()), seed]).standard_normal(out[name].shape)
        drawn = base * np.exp(spread * noise) if base else spread * noise
        out[name] = __import__('jax').numpy.asarray(drawn.astype(out[name].dtype))
    for name, factor in factors.items():
        out[name] = (out[name] * factor).astype(out[name].dtype)
    return out
```

```python
from contextlib import ExitStack

import numpy as np

import concourse.bass as bass
from concourse import mybir

F = mybir.dt.float32
R = mybir.dt.float32r
I32 = mybir.dt.int32
ALU = mybir.AluOpType
ACT = mybir.ActivationFunctionType
AX = mybir.AxisListType

T = 1024
TC = 256
NF = 22
EPS = 1e-6
NW = 5
NS = 2
NST = 4


class Engine:

    def __init__(self, name, eng, sems):
        self.name, self.eng, self.sems, self.n, self.seen = name, eng, sems, 0, {}

    def wait(self, *tokens):
        for t in tokens:
            if t is None:
                continue
            if isinstance(t, list):
                self.wait(*t)
            elif self.seen.get(t[0], 0) < t[1]:
                self.seen[t[0]] = t[1]
                self.eng.wait_ge(self.sems(t[0]), t[1])

    def do(self, fn, *tokens):
        self.wait(*tokens)
        self.n += 1
        fn(self.eng).then_inc(self.sems(self.name), 1)
        return (self.name, self.n)

    def quiet(self, fn, *tokens):
        self.wait(*tokens)
        fn(self.eng)


class Dma:

    def __init__(self, eng):
        self.eng, self.n = eng, {}

    def __call__(self, key, out, in_, *tokens):
        self.eng.wait(*tokens)
        self.n[key] = self.n.get(key, 0) + 16
        self.eng.eng.dma_start(out, in_).then_inc(self.eng.sems(key), 16)
        return (key, self.n[key])


def weight_order():
    order = [("al", 0)]
    order += [("k", m) for m in range(4)] + [("vv", m) for m in range(8)] + [("q", m) for m in range(4)]
    for n in ("v", "u", "r", "ga", "gb"):
        order += [(n, m) for m in range(8)]
    for n in ("wa", "wb", "wo"):
        order += [(n, m) for m in range(8)]
    order += ffn_order("f1", "f2")
    for m in range(8):
        order += [("u2", m), ("g2", m), ("z0", m)]
    order += [("k2", 0), ("k2", 1), ("v2", 0), ("v2", 1)]
    order += [("q2", m) for m in range(4)] + [("z1", m) for m in range(4)]
    order += [("q2", m) for m in range(4, 8)] + [("z1", m) for m in range(4, 8)]
    order += [("wo2", m) for m in range(8)]
    order += ffn_order("f12", "f22")
    return order


GROUPS = [(2 * i, 2 * i + 1) for i in range(NF // 2)]


def ffn_order(one, two):
    order = []
    for i, g in enumerate(GROUPS):
        for t in g:
            order += [(one, t), (one, NF + t)]
        if i:
            order += [(two, t) for t in GROUPS[i - 1]]
    return order + [(two, t) for t in GROUPS[-1]]


def program(nc, D, out):
    top = ExitStack()
    with top:
        held = {}

        def sems(key):
            if key not in held:
                held[key] = nc.alloc_semaphore("q_" + key)
            return held[key]

        PE, AC, DV, PO, SP = (Engine(n, e, sems) for n, e in (("pe", nc.tensor), ("ac", nc.scalar), ("dv", nc.vector), ("po", nc.gpsimd), ("sp", nc.sync)))
        dma = Dma(SP)
        cnt = [0]

        def alloc(stack, shape, dt, name="t"):
            cnt[0] += 1
            return stack.enter_context(nc.sbuf_tensor(f"s_{name}{cnt[0]}", shape, dt))

        def A(shape, dt, name="t"):
            return alloc(top, shape, dt, name)

        def scratch(name, shape):
            return nc.dram_tensor("d_" + name, shape, F, kind="Internal").ap()

        XH = A([128, 8, T], R, "xh")
        XL = A([128, 8, T], R, "xl")
        WH = A([128, NW, 1024], R, "wh")
        WL = A([128, NW, 1024], R, "wl")
        WS = A([128, NS, 1024], F, "ws")
        RES = A([128, 8, T], F, "res")
        ident = A([128, 128], F, "ident")
        ones = A([128, 128], F, "ones")
        MOD = A([128, 48], F, "mod")
        MODC = A([128, 16], F, "modc")
        VEC = A([128, 240], F, "vec")
        GS = A([128, 32], F, "gs")
        eps = A([128, 1], F, "eps")
        B = [top.enter_context(nc.psum_tensor(f"p_{i}", [128, 512], F)) for i in range(8)]
        bfree = [None] * 8

        t_vec = dma("vec", VEC[:], D["vec"])
        t_id = dma("ident", ident[:], D["ident"])
        t_ones = DV.do(lambda e: e.memset(ones[:], 1.0))
        t_eps = DV.do(lambda e: e.memset(eps[:], EPS))

        V = {}
        at = 0
        for name, n in VECTORS:
            V[name] = at
            at += n

        def vec(name, m):
            return VEC[:, V[name] + m:V[name] + m + 1]

        def everything():
            return [(e.name, e.n) for e in (PE, AC, DV, PO) if e.n] + [(k, v) for k, v in dma.n.items() if not k.startswith("ws")]

        def barrier():
            t = everything()
            for e in (AC, DV, PO, SP):
                e.wait(t)

        order = weight_order()
        wsplit = {}
        wfree = {}
        wload = {}
        state = {"next": 0, "loaded": 0, "split": 0}

        def wload_to(n):
            while state["loaded"] < min(n, len(order)):
                i = state["loaded"]
                name, m = order[i]
                src = D["W" + name][m]
                cols = src.shape[1]
                wload[i] = dma(f"ws{i % NS}", WS[:, i % NS, 0:cols], src, wsplit.get(i - NS))
                state["loaded"] += 1

        def wsplit_to(n):
            while state["split"] < min(n, len(order)):
                i = state["split"]
                wload_to(i + 1)
                s, w = i % NS, i % NW
                cols = D["W" + order[i][0]][order[i][1]].shape[1]
                hi, lo, src = WH[:, w, 0:cols], WL[:, w, 0:cols], WS[:, s, 0:cols]
                t1 = AC.do(lambda e: e.activation(hi, src, ACT.Copy), wload[i], wfree.get(i - NW))
                t2 = DV.do(lambda e: e.tensor_tensor(lo, src, hi.bitcast(F), ALU.subtract), wload[i], t1)
                wsplit[i] = [t1, t2]
                state["split"] += 1

        def wget(name, m):
            i = state["next"]
            assert order[i] == (name, m), (order[i], name, m)
            state["next"] += 1
            wsplit_to(i + 3)
            wload_to(i + 5)
            return i

        def wdone(i, token):
            wfree[i] = token

        banks = {"use": [0, 1, 2], "n": 0}

        def bank():
            b = banks["use"][banks["n"] % len(banks["use"])]
            banks["n"] += 1
            return b

        xtok = [[None] * 8, [None] * 8]

        def product(i, half, M=128, X=None, n=512, tok=None):
            H, L = X or (XH, XL)
            tok = tok or xtok[half]
            b = bank()
            PE.wait(bfree[b], wsplit[i])
            w = i % NW
            for k in range(8):
                PE.wait(tok[k])
                o = B[b][0:M, 0:n]
                wh, wl = WH[:, w, k * M:(k + 1) * M], WL[:, w, k * M:(k + 1) * M]
                xh, xl = H[:, k, half * n:half * n + n], L[:, k, half * n:half * n + n]
                PE.quiet(lambda e, o=o, a=wh, x=xh, k=k: e.matmul(o, a, x, start=(k == 0), stop=False))
                PE.quiet(lambda e, o=o, a=wh, x=xl: e.matmul(o, a, x, start=False, stop=False))
                f = (lambda e, o=o, a=wl, x=xh, k=k: e.matmul(o, a, x, start=False, stop=(k == 7)))
                if k < 7:
                    PE.quiet(f)
                else:
                    t = PE.do(f)
            return b, t

        def split_to(hi, lo, src, *tokens):
            t1 = AC.do(lambda e: e.activation(hi, src, ACT.Copy), *tokens)
            t2 = DV.do(lambda e: e.tensor_tensor(lo, src, hi.bitcast(F), ALU.subtract), t1, *tokens)
            return [t1, t2]

        later = []

        def run_later():
            todo, later[:] = later[:], []
            for f in todo:
                f()

        def rms_scale(acc, n, rb, tacc):
            toks = []
            for c in range(0, n, 512):
                w = min(512, n - c)
                b = bank()
                t = PE.do(lambda e, b=b, c=c, w=w: e.matmul(B[b][:, 0:w], ones[:], acc[:, c:c + w], start=True, stop=True),
                          bfree[b], tacc, t_ones)
                t2 = AC.do(lambda e, b=b, c=c, w=w: e.activation(rb[:, c:c + w], B[b][:, 0:w], ACT.Sqrt, bias=eps[:, 0:1], scale=1.0 / 1024), t, t_eps)
                bfree[b] = t2
                toks.append(DV.do(lambda e, c=c, w=w: e.reciprocal(rb[:, c:c + w], rb[:, c:c + w]), t2))
            return toks

        def norm_mod(src, n, rb, trb, hs, scale, shift, H, L, tmp, ready, free):
            outs = []
            ttmp = [None] * tmp.shape[1]
            for k in range(8):
                q = k % tmp.shape[1]
                x, r = src[:, k, 0:n], rb[:, 0:n]
                s = tmp[:, q, 0:n]
                t1 = DV.do(lambda e, s=s, x=x, r=r: e.tensor_tensor(s, x, r, ALU.mult), trb, ready[k], ttmp[q])
                t2 = AC.do(lambda e, s=s, k=k: e.activation(s, s, ACT.Identity, bias=shift(k), scale=scale(k)), t1, hs)
                h, l = H[:, k, 0:n], L[:, k, 0:n]
                t3 = AC.do(lambda e, h=h, s=s: e.activation(h, s, ACT.Copy), t2, free)
                t4 = DV.do(lambda e, h=h, l=l, s=s: e.tensor_tensor(l, s, h.bitcast(F), ALU.subtract), t3, free)
                ttmp[q] = [t3, t4]
                outs.append([t3, t4])
            return outs

        def sum_squares(acc, sq, x, k, tx, tsq, tacc):
            if k == 0:
                t = AC.do(lambda e: e.activation(acc, x, ACT.Square), tx, tacc)
                return tsq, t
            t1 = AC.do(lambda e: e.activation(sq, x, ACT.Square), tx, tsq)
            t2 = DV.do(lambda e: e.tensor_tensor(acc, acc, sq, ALU.add), t1, tacc)
            return t2, t2

        ph = ExitStack()
        written = {}

        class Stage:

            def __init__(self, stack, n, name):
                self.buf, self.n, self.i, self.name = alloc(stack, [128, n, 512], F, name), n, 0, name
                self.free = [None] * n

            def take(self):
                s = self.i % self.n
                self.i += 1
                return s, self.free[s]

            def store(self, s, dst, src, name, *tokens):
                t = dma(f"{self.name}{s}", dst, src, *tokens)
                self.free[s] = t
                written.setdefault(name, []).append(t)
                return t

        ST = Stage(ph, NST, "st")
        VF = alloc(ph, [128, 2, 512], F, "vf")
        vf = {"i": 0, "free": [None, None]}
        pc = ExitStack()
        CH = alloc(pc, [128, 8, TC], R, "ch")
        CL = alloc(pc, [128, 8, TC], R, "cl")
        p0 = ExitStack()
        Q = lambda shape, dt, name="t": alloc(p0, shape, dt, name)
        sc2 = Q([128, 8, 2], F, "sc2")
        AD = Q([128, 2, 2048], F, "ad")
        mrow = AD[0:2, 0, :]
        acc = Q([128, T], F, "acc")
        sq = Q([128, T], F, "sq")
        XC = AD[:, 1, :].rearrange("p (k t) -> p k t", k=8)

        t_cc = dma("cc", sc2[:], D["cc"])
        t_sc = AC.do(lambda e: e.activation(sc2[:, :, :], sc2[:, :, :], ACT.Silu), t_cc)
        banks["use"] = [4, 5, 6, 7]
        tad = [None, None]
        tx = [None] * 8
        for k in range(8):
            t = dma(f"ad{k % 2}", AD[:, k % 2, :], D["ada"][k], tad[k % 2])
            for c in range(4):
                f = (lambda e, k=k, c=c: e.matmul(B[c][0:2, :], sc2[:, k, :], AD[:, k % 2, c * 512:c * 512 + 512], start=(k == 0), stop=(k == 7)))
                if c < 3:
                    PE.quiet(f, t, t_sc)
                else:
                    tad[k % 2] = PE.do(f)
        for k in range(8):
            tx[k] = dma(f"x{k}", RES[:, k, :], D["xT"][k])
        tmr = AC.do(lambda e: e.activation(mrow[:, 0:512], B[0][0:2, :], ACT.Copy), tad[0], tad[1])
        for c in range(1, 4):
            tmr = AC.do(lambda e, c=c: e.activation(mrow[:, c * 512:c * 512 + 512], B[c][0:2, :], ACT.Copy))
        for m in range(16):
            f = (lambda e, m=m: e.matmul(B[4][:, 2 * m:2 * m + 2], mrow[:, m * 128:m * 128 + 128], ident[0:2, 0:2], start=True, stop=True))
            if m < 15:
                PE.quiet(f, tmr, t_id)
            else:
                t = PE.do(f)
        mp = B[4][:, 0:32].rearrange("p (m j) -> p j m", j=2)
        t_m1 = DV.do(lambda e: e.tensor_tensor(MOD[:, 0:16], mp[:, 0, :], VEC[:, V["b_ada"]:V["b_ada"] + 16], ALU.add), t, t_vec)
        t_m2 = DV.do(lambda e: e.tensor_tensor(MODC[:, 0:16], mp[:, 1, :], VEC[:, V["b_ada"]:V["b_ada"] + 16], ALU.add))
        bfree[4] = t_m2
        t_g1 = DV.do(lambda e: e.scalar_tensor_tensor(out=GS[:, 0:8], in0=MOD[:, 8:16], scalar=1.0, in1=VEC[:, V["n1"]:V["n1"] + 8], op0=ALU.add, op1=ALU.mult), t_m1)
        t_g2 = DV.do(lambda e: e.scalar_tensor_tensor(out=GS[:, 8:16], in0=MODC[:, 8:16], scalar=1.0, in1=VEC[:, V["n1"]:V["n1"] + 8], op0=ALU.add, op1=ALU.mult), t_m2)

        txc = dma("ad1", XC, D["ctxT"], tad[1])
        tsq = tacc = None
        for k in range(8):
            tsq, tacc = sum_squares(acc[:, :], sq[:, :], RES[:, k, :], k, tx[k], tsq, tacc)
        rb = sq
        trb = rms_scale(acc, T, rb, [tacc, tsq])
        tmp = Q([128, 1, T], F, "tmp")
        xt = norm_mod(RES, T, rb, trb, [t_g1], lambda k: GS[:, k:k + 1], lambda k: MOD[:, k:k + 1], XH, XL, tmp, tx, None)
        xtok[0], xtok[1] = xt, xt
        tsq2 = xt[7]
        tacc = xt[7]
        tsq = xt[7]
        accc, sqc = acc[:, 0:TC], sq[:, 0:TC]
        for k in range(8):
            tsq, tacc = sum_squares(accc, sqc, XC[:, k, :], k, txc, tsq, tacc)
        trb = rms_scale(acc, TC, sq, [tacc, tsq])
        ctok = norm_mod(XC, TC, sq, trb, [t_g2], lambda k: GS[:, 8 + k:9 + k], lambda k: MODC[:, k:k + 1], CH, CL, tmp, [txc] * 8, None)
        wsplit_to(2)
        wload_to(3)
        barrier()
        p0.close()

        dB = [scratch("bf", [4, 128, T + TC]), scratch("bb", [4, 128, T + TC])]
        dK = scratch("k", [4, 128, T + TC])
        dQ = scratch("q", [4, 128, T])
        dV = scratch("v", [10, 128, 1024])
        dVm = scratch("vm", [8, 128, 1024])
        dU = scratch("u", [8, 128, T])
        dR = scratch("r", [8, 128, T])
        dGA = scratch("ga", [8, 128, T])
        dGB = scratch("gb", [8, 128, T])
        dA = scratch("a", [8, 128, T])
        dBo = scratch("bo", [8, 128, T])
        p1 = ExitStack()
        banks["use"] = [0, 1, 2]
        banks["n"] = 0

        def parts(ctx):
            p = [(TC, 0, 512, (XH, XL), None), (TC + 512, 1, 512, (XH, XL), None)]
            if ctx:
                p.append((0, 0, 256, (CH, CL), ctok))
            return p

        AL = alloc(p1, [32, T + TC], F, "al")
        WAL = alloc(p1, [32, 2, 512], F, "wal")
        LG = alloc(p1, [128, 2, 4, 512], F, "lg")
        cmask = alloc(p1, [128, 512], F, "cmask")
        t_wal = dma("wal", WAL[:], D["walpha"])
        t_cm = dma("cmask", cmask[:], D["cmask"])
        i = wget("al", 0)
        tal = []
        for col, h, n, X, tok in parts(True):
            b, t = product(i, h, M=32, X=X, n=n, tok=tok)
            t2 = AC.do(lambda e, b=b, n=n, col=col: e.activation(AL[:, col:col + n], B[b][0:32, 0:n], ACT.Copy), t)
            bfree[b] = t2
            tal.append((col, n, t2))
        wdone(i, t)
        tlg = [None, None]
        j = 0
        for d in range(2):
            for h in range(4):
                for col, n, ta in tal:
                    b = bank()
                    t = PE.do(lambda e, b=b, d=d, h=h, n=n, col=col: e.matmul(B[b][:, 0:n], WAL[:, d, h * 128:h * 128 + 128], AL[:, col:col + n], start=True, stop=True),
                              bfree[b], ta, t_wal)
                    q = j % 2
                    j += 1
                    bias = vec("b_al", 4 * d + h)
                    g = [LG[:, q, c, 0:n] for c in range(3)]
                    ps = B[b][:, 0:n]
                    t1 = AC.do(lambda e, g=g, ps=ps, bias=bias: e.activation(g[0], ps, ACT.Abs, bias=bias), t, tlg[q], t_vec)
                    t2 = DV.do(lambda e, g=g, ps=ps, bias=bias: e.tensor_scalar(g[1], ps, bias, 0.0, ALU.add, ALU.min), t1, tlg[q], t_vec)
                    bfree[b] = [t1, t2]
                    t3 = AC.do(lambda e, g=g: e.activation(g[0], g[0], ACT.Exp, scale=-1.0), t1)
                    t4 = AC.do(lambda e, g=g: e.activation(g[0], g[0], ACT.Ln, bias=ones[:, 0:1]), t3, t_ones)
                    t5 = DV.do(lambda e, g=g: e.tensor_tensor(g[1], g[1], g[0], ALU.subtract), t4, t2)
                    s, fr = ST.take()
                    o = ST.buf[:, s, 0:n]
                    if d == 0:
                        t6 = DV.do(lambda e, g=g, o=o, n=n: e.tensor_tensor_scan(o, cmask[:, 0:n], g[1], 0.0, ALU.mult, ALU.add), t5, t_cm, fr)
                    else:
                        t6 = DV.do(lambda e, g=g, o=o, n=n: e.tensor_tensor_scan(o[:, ::-1], cmask[:, 0:n], g[1][:, ::-1], 0.0, ALU.mult, ALU.add), t5, t_cm, fr)
                    tlg[q] = [t5, t6]
                    ST.store(s, dB[d][h][:, col:col + n], o, f"b{d}", t6)

        def turned(src, n, col, m, dst, name, ts, tbank):
            def go():
                c4 = n // 128
                for c in range(c4):
                    f = (lambda e, c=c: e.transpose(B[tbank][:, c * 128:c * 128 + 128], src[:, c * 128:c * 128 + 128], ident[:]))
                    if c < c4 - 1:
                        PE.quiet(f, bfree[tbank], ts, t_id)
                    else:
                        t = PE.do(f, bfree[tbank], ts, t_id)
                s, fr = ST.take()
                t2 = DV.do(lambda e: e.tensor_copy(ST.buf[:, s, 0:n], B[tbank][:, 0:n]), t, fr)
                bfree[tbank] = t2
                ST.store(s, dst[col // 128:col // 128 + c4, :, m * 128:m * 128 + 128].rearrange("c p f -> p c f"),
                         ST.buf[:, s, 0:n].rearrange("p (c f) -> p c f", f=128), name, t2)
                return t
            later.append(go)


        def project(name, m, ctx, put):
            i = wget(name, m)
            for col, h, n, X, tok in parts(ctx):
                b, t = product(i, h, X=X, n=n, tok=tok)
                run_later()
                put(m, col, n, B[b][:, 0:n], b, t)
                yield
            wdone(i, t)

        def put_plain(dst, name, off, func=ACT.Copy, scale=1.0):
            def put(m, col, n, ps, b, t):
                s, fr = ST.take()
                o = ST.buf[:, s, 0:n]
                t2 = AC.do(lambda e: e.activation(o, ps, func, scale=scale), t, fr)
                bfree[b] = t2
                ST.store(s, dst[m][:, col - off:col - off + n], o, name, t2)
            return put

        def put_turned(dst, name, off, func, tbank):
            def put(m, col, n, ps, b, t):
                q = vf["i"] % 2
                vf["i"] += 1
                o = VF[:, q, 0:n]
                t2 = AC.do(lambda e: e.activation(o, ps, func), t, vf["free"][q])
                bfree[b] = t2
                turned(o, n, col - off, m, dst, name, t2, tbank)
                f = later.pop()

                def go():
                    vf["free"][q] = f()
                later.append(go)
            return put

        def run(g):
            for _ in g:
                pass

        for m in range(4):
            run(project("k", m, True, put_plain(dK, "k", 0)))
        for m in range(8):
            run(project("vv", m, True, put_turned(dV, "v", 0, ACT.Copy, 3)))
        for m in range(4):
            run(project("q", m, False, put_plain(dQ, "q", TC, scale=float(128 ** -0.5))))
        run_later()
        barrier()
        p1.close()
        pc.close()

        p2 = ExitStack()
        S2 = lambda shape, dt, name="t": alloc(p2, shape, dt, name)
        banks["use"] = [0, 1]
        TB, AB, KB, VB = 2, 3, 4, 5
        OB = [6, 7]
        gb = [S2([128, 4, 128], F, "gb") for _ in range(2)]
        gk = [S2([128, 4, 128], F, "gk") for _ in range(2)]
        gq = [S2([128, 4, 128], F, "gq") for _ in range(2)]
        gv = [S2([128, 1024], F, "gv") for _ in range(2)]
        ee = S2([128, 4, 128], F, "ee")
        ki = S2([128, 4, 128], F, "ki")
        ks = S2([128, 4, 128], F, "ks")
        kT = S2([128, 4, 128], F, "kT")
        att = [S2([128, 4, 128], F, "att") for _ in range(2)]
        amask = [S2([128, 128], I32, "am") for _ in range(2)]
        SS = [S2([128, 4, 256], F, "S") for _ in range(2)]
        EB = S2([128, 2, 4, 2], F, "eb")
        EP = S2([128, 4], F, "ep")
        t_am = [dma(f"am{d}", amask[d][:], D[f"amask{d}"]) for d in range(2)]
        t_at0 = [DV.do(lambda e, d=d: e.memset(att[d][:], 0.0)) for d in range(2)]
        t_S = [DV.do(lambda e, d=d: e.memset(SS[d][:], 0.0)) for d in range(2)]
        g_free = [{}, {}]
        w_free = {}
        t_att = [t_at0[0], t_at0[1]]
        o_tok = {}

        def gla(d, pair, ctx):
            col = pair * 128
            fr = g_free[d]
            tb = dma(f"gb{d}", gb[d][:], dB[d][:, :, col:col + 128].rearrange("h p t -> p h t"), written[f"b{d}"], fr.get("b"))
            tk = dma(f"gk{d}", gk[d][:], dK[:, :, col:col + 128].rearrange("h p t -> p h t"), written["k"], fr.get("k"))
            tv = dma(f"gv{d}", gv[d][:], dV[pair], written["v"], fr.get("v"))
            tq = None
            if not ctx:
                tq = dma(f"gq{d}", gq[d][:], dQ[:, :, col - TC:col - TC + 128].rearrange("h p t -> p h t"), written["q"], fr.get("q"))
            yield
            first, second = (0, 1) if d == 0 else (1, 0)
            last = (lambda c: 64 * c + 63) if d == 0 else (lambda c: 64 * c)
            b, k, q, v = gb[d], gk[d], gq[d], gv[d]
            lastv = b[:, :, last(0):last(0) + 65:64]
            te = AC.do(lambda e: e.activation(EB[:, d, :, :], lastv, ACT.Exp, scale=1 / 16), tb, w_free.get(f"EB{d}"))
            tp = DV.do(lambda e: e.tensor_tensor(EP[:, :], EB[:, d, :, 0], EB[:, d, :, 1], ALU.mult), te, w_free.get("EP"))
            if not ctx:
                t1 = AC.do(lambda e: e.activation(ee[:, :, :], b[:, :, :], ACT.Exp, scale=1 / 16), tb, w_free.get("ee"))
                tq1 = DV.do(lambda e: e.tensor_tensor(q[:, :, :], q[:, :, :], ee[:, :, :], ALU.mult), t1, tq)
                t2 = AC.do(lambda e: e.activation(ee[:, :, :], b[:, :, :], ACT.Exp, scale=-1 / 16), tq1)
                tki = DV.do(lambda e: e.tensor_tensor(ki[:, :, :], k[:, :, :], ee[:, :, :], ALU.mult), t2, tk, w_free.get("ki"))
            else:
                tki = w_free.get("ee")
            b2 = b[:, :, :].rearrange("p h (c t) -> p h c t", c=2)
            for c in range(2):
                td = DV.do(lambda e, c=c: e.tensor_tensor(ee[:, :, 64 * c:64 * c + 64], b[:, :, last(c):last(c) + 1].to_broadcast([128, 4, 64]), b2[:, :, c, :], ALU.subtract), tki, tb)
            t3 = AC.do(lambda e: e.activation(ee[:, :, :], ee[:, :, :], ACT.Exp, scale=1 / 16), td)
            fr["b"] = [te, t3, td]
            tks = DV.do(lambda e: e.tensor_tensor(ks[:, :, :], k[:, :, :], ee[:, :, :], ALU.mult), t3, tk, w_free.get("ks"))
            w_free["ee"] = tks
            fr["k"] = tks
            yield
            tx1 = tks
            if not ctx:
                for h in range(4):
                    PE.quiet(lambda e, h=h: e.matmul(B[AB][:, h * 128:h * 128 + 128], ki[:, h, :], q[:, h, :], start=True, stop=True),
                             tki, tq1, bfree[AB])
                for h in range(4):
                    f = (lambda e, h=h: e.matmul(B[KB][64 * first:64 * first + 64, h * 64:h * 64 + 64], ks[:, h, 64 * first:64 * first + 64],
                                                 q[:, h, 64 * second:64 * second + 64], start=True, stop=True))
                    if h < 3:
                        PE.quiet(f, tks, bfree[KB])
                    else:
                        ta = PE.do(f)
                w_free["ki"] = ta
                tc = DV.do(lambda e: e.copy_predicated(att[d][:, :, :], amask[d][:].rearrange("p (o t) -> p o t", o=1).to_broadcast([128, 4, 128]),
                                                      B[AB][:, :].rearrange("p (h t) -> p h t", h=4)), ta, t_att[d], t_am[d])
                bfree[AB] = tc
                tc2 = DV.do(lambda e: e.tensor_copy(att[d][64 * first:64 * first + 64, :, 64 * second:64 * second + 64],
                                                    B[KB][64 * first:64 * first + 64, 0:256].rearrange("p (h t) -> p h t", h=4)), ta, tc)
                bfree[KB] = tc2
                tq2 = DV.do(lambda e: e.tensor_tensor(q[:, :, 64 * second:64 * second + 64], q[:, :, 64 * second:64 * second + 64],
                                                      EB[:, d, :, first:first + 1].to_broadcast([128, 4, 64]), ALU.mult), ta)
                tx1 = ta
            tks2 = DV.do(lambda e: e.tensor_tensor(ks[:, :, 64 * first:64 * first + 64], ks[:, :, 64 * first:64 * first + 64],
                                                   EB[:, d, :, second:second + 1].to_broadcast([128, 4, 64]), ALU.mult), tx1, te)
            w_free[f"EB{d}"] = tks2
            yield
            for h in range(4):
                f = (lambda e, h=h: e.transpose(B[KB][:, h * 128:h * 128 + 128], ks[:, h, :], ident[:]))
                if h < 3:
                    PE.quiet(f, tks2, bfree[KB])
                else:
                    tt = PE.do(f)
            w_free["ks"] = tt
            tkt = AC.do(lambda e: e.activation(kT[:, :, :], B[KB][:, :].rearrange("p (h t) -> p h t", h=4), ACT.Copy), tt, w_free.get("kT"))
            bfree[KB] = tkt
            to = None
            if not ctx:
                for h in range(4):
                    o = B[OB[h // 2]][:, (h % 2) * 256:(h % 2) * 256 + 256]
                    PE.quiet(lambda e, h=h, o=o: e.matmul(o, q[:, h, :], SS[d][:, h, :], start=True, stop=False),
                             tq2, t_S[d], bfree[OB[h // 2]])
                    f = (lambda e, h=h, o=o: e.matmul(o, att[d][:, h, :], v[:, h * 256:h * 256 + 256], start=False, stop=True))
                    if h % 2 == 0:
                        PE.quiet(f, tc, tc2, tv)
                    else:
                        to = PE.do(f, tc, tc2, tv)
                        P8 = pair - 2
                        dst = RES[:, P8, h // 2 * 512:h // 2 * 512 + 512]
                        bk = OB[h // 2]
                        if (P8, h) not in o_tok:
                            o_tok[(P8, h)] = AC.do(lambda e, dst=dst, bk=bk: e.activation(dst, B[bk][:, :], ACT.Copy), to)
                        else:
                            o_tok[(P8, h)] = DV.do(lambda e, dst=dst, bk=bk: e.tensor_tensor(dst, B[bk][:, :], dst, ALU.add), to, o_tok[(P8, h)])
                        bfree[bk] = o_tok[(P8, h)]
                t_att[d] = to
                fr["q"] = to
            yield
            for hh in range(2):
                for h in (2 * hh, 2 * hh + 1):
                    f = (lambda e, h=h: e.matmul(B[VB][:, (h % 2) * 256:(h % 2) * 256 + 256], kT[:, h, :], v[:, h * 256:h * 256 + 256], start=True, stop=True))
                    if h % 2 == 0:
                        PE.quiet(f, tkt, bfree[VB], tv)
                    else:
                        tkv = PE.do(f)
                for h in (2 * hh, 2 * hh + 1):
                    ts = DV.do(lambda e, h=h: e.scalar_tensor_tensor(out=SS[d][:, h, :], in0=SS[d][:, h, :], scalar=EP[:, h:h + 1],
                                                                     in1=B[VB][:, (h % 2) * 256:(h % 2) * 256 + 256], op0=ALU.mult, op1=ALU.add),
                               tkv, to, tp, t_S[d])
                bfree[VB] = ts
                if hh == 0:
                    yield
            t_S[d] = ts
            w_free["EP"] = ts
            w_free["kT"] = tkv
            fr["v"] = tkv
            yield

        def gla_all():
            for s in range(10):
                yield from gla(0, s, s < 2)
                yield from gla(1, (1 - s) if s < 2 else 11 - s, s < 2)

        def fill(names):
            table = {"v": (dVm, "vm", ACT.Gelu), "u": (dU, "u", ACT.Gelu), "r": (dR, "r", ACT.Silu), "ga": (dGA, "ga", ACT.Sigmoid), "gb": (dGB, "gb", ACT.Sigmoid)}
            for n in names:
                dst, key, func = table[n]
                put = put_turned(dst, key, TC, func, TB) if n == "v" else put_plain(dst, key, TC, func)
                for m in range(8):
                    yield from project(n, m, False, put)

        def together(a, na, b, nb):
            live_a = live_b = True
            x = 0
            while live_a or live_b:
                if live_a and (x * nb >= 0) :
                    live_a = next(a, 0) is None
                x += nb
                while x >= na or not live_a:
                    x -= na
                    if not live_b:
                        break
                    live_b = next(b, 0) is None
                if not live_b and not live_a:
                    break

        cb = S2([128, 1024], F, "cb")
        aw = [S2([128, 1024], F, "aw") for _ in range(1)]
        t_cb = dma("cb", cb[:], D["crow"])
        t_cb = AC.do(lambda e: e.activation(cb[:, :], cb[:, :], ACT.Silu), t_cb)
        mt = {"ops": None}

        def mods():
            for m in range(16, 48):
                t = dma("aw", aw[0][:], D["adaT"][m - 16], mt["ops"])
                yield
                mt["ops"] = DV.do(lambda e, m=m: e.tensor_tensor_reduce(out=aw[0][:], in0=aw[0][:], in1=cb[:], scale=1.0, scalar=0.0,
                                                                       op0=ALU.mult, op1=ALU.add, accum_out=MOD[:, m:m + 1]), t, t_cb)
                yield
            mt["ops"] = DV.do(lambda e: e.tensor_tensor(MOD[:, 16:48], MOD[:, 16:48], VEC[:, V["b_ada"] + 16:V["b_ada"] + 48], ALU.add), mt["ops"])
            mt["gs"] = DV.do(lambda e: e.scalar_tensor_tensor(out=GS[:, 16:24], in0=MOD[:, 32:40], scalar=1.0, in1=VEC[:, V["n2"]:V["n2"] + 8], op0=ALU.add, op1=ALU.mult), mt["ops"])

        both = mods()

        def fill_mods(names):
            for _ in fill(names):
                next(both, 0)
                next(both, 0)
                yield

        together(fill_mods(["v", "u", "r"]), 48, gla_all(), 120)
        run_later()
        run(both)
        barrier()
        p2.close()

        p3 = ExitStack()
        S3 = lambda shape, dt, name="t": alloc(p3, shape, dt, name)
        vn = S3([128, 4, 1024], F, "vn")
        lg = S3([128, 2, 1024], F, "lng")
        bs = S3([128, 1024], F, "bs")
        wsp = S3([128, 1024], F, "wsp")
        ld = S3([128, 2, 512], F, "ld")
        st6 = S3([128, 2, 6], F, "st6")
        mv = S3([128, 2], F, "mv")
        ss = S3([128, 32], F, "ss")
        t_lg = dma("lg", lg[:], D["lnvb"])
        t_bs = dma("bs", bs[:], D["bspb"])
        t_wsp = dma("wsp", wsp[:], D["wspT"])

        def mlp():
            ldf = [None, None]
            j = 0
            tvf = [None] * 4
            for half in range(2):
                tn = []
                for c in range(4):
                    n = 4 * half + c
                    x = vn[:, c, :]
                    t = dma(f"vn{c}", x, dVm[n], written["vm"], tvf[c])
                    yield
                    for s in range(2):
                        t1 = DV.do(lambda e, s=s, x=x: e.bn_stats(st6[:, s, :], x[:, s * 512:s * 512 + 512]), t)
                    t2 = DV.do(lambda e: e.bn_aggr(mv[:, :], st6[:, :, :].rearrange("p a b -> p (a b)")), t1)
                    t3 = AC.do(lambda e: e.activation(mv[:, 1:2], mv[:, 1:2], ACT.Sqrt, bias=eps[:, 0:1]), t2)
                    t4 = DV.do(lambda e: e.reciprocal(mv[:, 1:2], mv[:, 1:2]), t3)
                    t5 = DV.do(lambda e, x=x: e.tensor_scalar(x, x, mv[:, 0:1], mv[:, 1:2], ALU.subtract, ALU.mult), t4)
                    t6 = DV.do(lambda e, x=x: e.tensor_tensor(x, x, lg[:, 0, :], ALU.mult), t5, t_lg)
                    t7 = DV.do(lambda e, x=x: e.tensor_tensor(x, x, lg[:, 1, :], ALU.add), t6)
                    tn.append(t7)
                    yield
                for g in range(8):
                    q = j % 2
                    j += 1
                    tu = dma(f"ld{q}", ld[:, q, :], dU[g][:, half * 512:half * 512 + 512], written["u"], ldf[q])
                    bk = [3, 4][g % 2]
                    for c in range(4):
                        f = (lambda e, c=c, g=g, bk=bk: e.matmul(B[bk][:, c * 128:c * 128 + 128], vn[:, c, g * 128:g * 128 + 128], wsp[:, g * 128:g * 128 + 128], start=True, stop=True))
                        if c < 3:
                            PE.quiet(f, tn[c], t_wsp, bfree[bk])
                        else:
                            t = PE.do(f, tn[c])
                    yield
                    s, fr = ST.take()
                    o = ST.buf[:, s, :]
                    bsg = bs[:, g * 128:g * 128 + 128].rearrange("p (o t) -> p o t", o=1).to_broadcast([128, 4, 128])
                    t1 = DV.do(lambda e, o=o, bk=bk, bsg=bsg: e.tensor_tensor(o.rearrange("p (c t) -> p c t", c=4), B[bk][:, :].rearrange("p (c t) -> p c t", c=4), bsg, ALU.add), t, t_bs, fr)
                    bfree[bk] = t1
                    t2 = DV.do(lambda e, o=o, q=q: e.tensor_tensor(o, o, ld[:, q, :], ALU.mult), t1, tu)
                    ldf[q] = t2
                    ST.store(s, dA[g][:, half * 512:half * 512 + 512], o, "a", t2)
                tvf = [t] * 4

            for p8 in range(8):
                for h in range(4):
                    o = RES[:, p8, h * 256:h * 256 + 256]
                    c = 4 * p8 + h
                    t1 = AC.do(lambda e, o=o, c=c, q=h % 2: e.activation(ld[:, q, 0:256], o, ACT.Square, accum_out=ss[:, c:c + 1]),
                               o_tok[(p8, 1)], o_tok[(p8, 3)], ldf[h % 2])
                    ldf[h % 2] = t1
                if p8 % 2:
                    yield
            t2 = AC.do(lambda e: e.activation(ss[:, :], ss[:, :], ACT.Sqrt, bias=eps[:, 0:1], scale=1 / 256), t1)
            t3 = DV.do(lambda e: e.reciprocal(ss[:, :], ss[:, :]), t2)
            tr = []
            for p8 in range(8):
                for h in range(4):
                    o = RES[:, p8, h * 256:h * 256 + 256]
                    c = 4 * p8 + h
                    t4 = DV.do(lambda e, o=o, c=c: e.tensor_scalar(o, o, ss[:, c:c + 1], None, ALU.mult), t3)
                tr.append(t4)
                yield
            for half in range(2):
                for m in range(8):
                    q = j % 2
                    j += 1
                    tu = dma(f"ld{q}", ld[:, q, :], dR[m][:, half * 512:half * 512 + 512], written["r"], ldf[q])
                    bk = [3, 4][m % 2]
                    for c in range(4):
                        p8 = 4 * half + c
                        f = (lambda e, c=c, m=m, bk=bk, p8=p8: e.transpose(B[bk][:, c * 128:c * 128 + 128], RES[:, p8, m * 128:m * 128 + 128], ident[:]))
                        if c < 3:
                            PE.quiet(f, tr[p8], bfree[bk])
                        else:
                            t = PE.do(f, tr[p8])
                    yield
                    s, fr = ST.take()
                    o = ST.buf[:, s, :]
                    t1 = DV.do(lambda e, o=o, bk=bk, m=m, q=q: e.scalar_tensor_tensor(out=o, in0=B[bk][:, :], scalar=vec("gn", m), in1=ld[:, q, :], op0=ALU.mult, op1=ALU.mult), t, tu, fr)
                    bfree[bk] = t1
                    ldf[q] = t1
                    ST.store(s, dBo[m][:, half * 512:half * 512 + 512], o, "bo", t1)

        together(fill(["ga", "gb"]), 32, mlp(), 64)
        run_later()
        barrier()
        p3.close()
        ph.close()

        def load_split(src, name, after, pe_last):
            free = [None, None]
            outs = []
            for k in range(8):
                q = k % 2
                t = dma(f"lx{q}", LX[:, q, :], src[k], written[name] if name else None, free[q])
                s = split_to(XH[:, k, :], XL[:, k, :], LX[:, q, :], t, pe_last)
                free[q] = s
                outs.append(s)
            xtok[0], xtok[1] = outs, outs

        p4 = ExitStack()
        S4 = lambda shape, dt, name="t": alloc(p4, shape, dt, name)
        LX = S4([128, 2, T], F, "lx")
        lq = S4([128, 4, 512], F, "lq")
        acc = S4([128, T], F, "acc")
        sq = S4([128, T], F, "sq")
        lqf = [None] * 4
        banks["use"] = list(range(8))
        load_split(dA, "a", None, (PE.name, PE.n))
        ltok = {}

        def unit_load(j, src, key):
            q = j % 4
            ltok[j] = dma(f"lq{q}", lq[:, q, :], src, written[key] if key else None, lqf[q])

        def branch(w, gate, key, add):
            toks = {}
            for m in range(8):
                i = wget(w, m)
                for h in range(2):
                    j = 2 * m + h
                    q = j % 4
                    tl = dma(f"lq{q}", lq[:, q, :], gate[m][:, h * 512:h * 512 + 512], written[key], lqf[q])
                    b, t = product(i, h)
                    y = RES[:, m, h * 512:h * 512 + 512]
                    if not add:
                        t1 = DV.do(lambda e, y=y, b=b, q=q: e.tensor_tensor(y, B[b][:, :], lq[:, q, :], ALU.mult), t, tl)
                        bfree[b] = t1
                        lqf[q] = t1
                    else:
                        g = lq[:, q, :]
                        t0 = DV.do(lambda e, b=b, g=g: e.tensor_tensor(g, B[b][:, :], g, ALU.mult), t, tl)
                        bfree[b] = t0
                        t1 = DV.do(lambda e, y=y, g=g: e.tensor_tensor(y, y, g, ALU.add), t0)
                        lqf[q] = t1
                    toks[(m, h)] = t1
                wdone(i, t)
            return toks, t

        _, tl = branch("wa", dGA, "ga", False)
        load_split(dBo, "bo", None, tl)
        ty, tl = branch("wb", dGB, "gb", True)
        outs = []
        for k in range(8):
            outs.append(split_to(XH[:, k, :], XL[:, k, :], RES[:, k, :], ty[(k, 0)], ty[(k, 1)], tl))
        xtok[0], xtok[1] = outs, outs

        def out_branch(w, gain, xsrc, key, ygone, lq, lqf):
            tr = [[None, None] for _ in range(8)]
            tq = [None, None]
            ta = [None, None]
            for m in range(8):
                i = wget(w, m)
                for h in range(2):
                    j = 2 * m + h
                    q = j % 4
                    tl = dma(f"lq{q}", lq[:, q, :], xsrc[m][:, h * 512:h * 512 + 512], written[key] if key else None, lqf[q])
                    b, t = product(i, h)
                    y = RES[:, m, h * 512:h * 512 + 512]
                    t1 = DV.do(lambda e, y=y, b=b, q=q, m=m: e.scalar_tensor_tensor(out=y, in0=B[b][:, :], scalar=gain(m), in1=lq[:, q, :], op0=ALU.mult, op1=ALU.add), t, tl, ygone)
                    bfree[b] = t1
                    lqf[q] = t1
                    tr[m][h] = t1
                    tq[h], ta[h] = sum_squares(acc[:, h * 512:h * 512 + 512], sq[:, h * 512:h * 512 + 512], y, m, t1, tq[h], ta[h])
                wdone(i, t)
            return tr, tq + ta, t

        tr, ta, tl = out_branch("wo", lambda m: MOD[:, 16 + m:17 + m], D["xT"], None, outs, lq, lqf)
        trb = rms_scale(acc, T, sq, ta)
        outs = norm_mod(RES, T, sq, trb, None, lambda k: GS[:, 16 + k:17 + k], lambda k: MOD[:, 24 + k:25 + k], XH, XL, LX, tr, tl)
        xtok[0], xtok[1] = outs, outs
        barrier()
        p4.close()

        def ffn(one, two, gate_first, gain):
            p = ExitStack()
            FH = alloc(p, [128, 4, T], R, "fh")
            FL = alloc(p, [128, 4, T], R, "fl")
            tm = alloc(p, [128, 4, 512], F, "tm")
            tmf = [None] * 4
            ffree = [None] * 4
            ftok = {}
            rt = {}
            j = 0

            def second(g):
                ws = [wget(two, t) for t in g]
                for m in range(8):
                    for h in range(2):
                        b = bank()
                        for x, (i, tt) in enumerate(zip(ws, g)):
                            s = tt % 4
                            w = i % NW
                            o = B[b][:, :]
                            wh, wl = WH[:, w, m * 128:m * 128 + 128], WL[:, w, m * 128:m * 128 + 128]
                            xh, xl = FH[:, s, h * 512:h * 512 + 512], FL[:, s, h * 512:h * 512 + 512]
                            PE.quiet(lambda e, o=o, a=wh, x_=xh, x=x: e.matmul(o, a, x_, start=(x == 0), stop=False), bfree[b], wsplit[i], ftok[(tt, h)])
                            PE.quiet(lambda e, o=o, a=wh, x_=xl: e.matmul(o, a, x_, start=False, stop=False))
                            f = (lambda e, o=o, a=wl, x_=xh, x=x: e.matmul(o, a, x_, start=False, stop=(x == 1)))
                            if x < 1:
                                PE.quiet(f)
                            else:
                                t = PE.do(f)
                        y = RES[:, m, h * 512:h * 512 + 512]
                        rt[(m, h)] = DV.do(lambda e, y=y, b=b, m=m: e.scalar_tensor_tensor(out=y, in0=B[b][:, :], scalar=gain(m), in1=y, op0=ALU.mult, op1=ALU.add), t, rt.get((m, h)))
                        bfree[b] = rt[(m, h)]
                        last[(m, h)] = rt[(m, h)]
                for i in ws:
                    wdone(i, t)
                for tt in g:
                    ffree[tt % 4] = t

            last = {}
            for gi, g in enumerate(GROUPS):
                for tt in g:
                    i0 = wget(one, tt)
                    i1 = wget(one, NF + tt)
                    s = tt % 4
                    for h in range(2):
                        b0, t0 = product(i0, h)
                        b1, t1 = product(i1, h)
                        (bg, tg), (bu, tu) = ((b0, t0), (b1, t1)) if gate_first else ((b1, t1), (b0, t0))
                        q = j % 4
                        j += 1
                        y = tm[:, q, :]
                        t2 = AC.do(lambda e, y=y, bg=bg: e.activation(y, B[bg][:, :], ACT.Silu), tg, tmf[q])
                        t3 = DV.do(lambda e, y=y, bu=bu: e.tensor_tensor(y, B[bu][:, :], y, ALU.mult), tu, t2)
                        bfree[bg], bfree[bu] = t2, t3
                        ftok[(tt, h)] = split_to(FH[:, s, h * 512:h * 512 + 512], FL[:, s, h * 512:h * 512 + 512], y, t3, ffree[s])
                        tmf[q] = ftok[(tt, h)]
                    wdone(i0, t1)
                    wdone(i1, t1)
                if gi:
                    second(GROUPS[gi - 1])
            second(GROUPS[-1])
            barrier()
            p.close()
            return last

        last = ffn("f1", "f2", False, lambda m: MOD[:, 40 + m:41 + m])

        dX = scratch("x2", [8, 128, T])
        dZ1 = scratch("z1", [8, 128, T])
        dM = scratch("mg", [8, 128, T])
        dQ2 = scratch("q2", [8, 128, T])

        p5 = ExitStack()
        S5 = lambda shape, dt, name="t": alloc(p5, shape, dt, name)
        n5 = ExitStack()
        acc = alloc(n5, [128, T], F, "acc")
        sq = alloc(n5, [128, T], F, "sq")
        LX = alloc(n5, [128, 2, T], F, "lx")
        rbs = alloc(n5, [128, T], F, "rb")
        tsq = tacc = None
        for k in range(8):
            tsq, tacc = sum_squares(acc[:, :], sq[:, :], RES[:, k, :], k, [last[(k, 0)], last[(k, 1)]], tsq, tacc)
        trb = rms_scale(acc, T, rbs, [tsq, tacc])
        tfin = []
        for k in range(8):
            t = DV.do(lambda e, k=k: e.scalar_tensor_tensor(out=RES[:, k, :], in0=RES[:, k, :], scalar=vec("fin1", k), in1=rbs[:, :], op0=ALU.mult, op1=ALU.mult), trb)
            tfin.append(t)
            tsq, tacc = sum_squares(acc[:, :], sq[:, :], RES[:, k, :], k, t, [tsq, tacc], [tacc, trb])
            written.setdefault("x2", []).append(dma(f"x{k}", dX[k], RES[:, k, :], t))
        trb = rms_scale(acc, T, sq, [tsq, tacc])

        def norm_gain(src, rb, trb, name, H, L, ready, free):
            outs = []
            tt = [None, None]
            for k in range(8):
                q = k % 2
                s = LX[:, q, :]
                t1 = DV.do(lambda e, s=s, k=k: e.scalar_tensor_tensor(out=s, in0=src[:, k, :], scalar=vec(name, k), in1=rb[:, :], op0=ALU.mult, op1=ALU.mult), trb, ready[k], tt[q])
                tt[q] = split_to(H[:, k, :], L[:, k, :], s, t1, free)
                outs.append(tt[q])
            return outs

        outs = norm_gain(RES, sq, trb, "nm2", XH, XL, tfin, (PE.name, PE.n))
        xtok[0], xtok[1] = outs, outs
        wsplit_to(state["next"] + 3)
        barrier()
        n5.close()

        U = RES[:, 0, :]
        UC = RES[:, 1, :]
        Rg = [RES[:, 2, :], RES[:, 3, :]]
        Ig = [RES[:, 4, :], RES[:, 5, :]]
        HH = RES[:, 6, :]
        SQ = RES[:, 7, :]
        UP = S5([128, T + 3], F, "up")
        UH = S5([128, T], R, "uh")
        UL = S5([128, T], R, "ul")
        GL = S5([128, 2, T], F, "gl")
        Z0 = S5([128, 2, T], F, "z0")
        BD = S5([128, 2, 512], F, "bd")
        BH = S5([128, 2, 512], R, "bh")
        BL = S5([128, 2, 512], R, "bl")
        SPL = S5([128, 16], F, "spl")
        tm = S5([128, 2, T], F, "tm")
        lam = VEC[:, V["lam"]:V["lam"] + 16]
        s1, s2 = tm[:, 0, 0:16], tm[:, 1, 0:16]
        t1 = AC.do(lambda e: e.activation(s1, lam, ACT.Abs))
        t1 = AC.do(lambda e: e.activation(s1, s1, ACT.Exp, scale=-1.0), t1)
        t1 = AC.do(lambda e: e.activation(s1, s1, ACT.Ln, bias=ones[:, 0:1]), t1)
        t2 = DV.do(lambda e: e.tensor_scalar(s2, lam, -1.0, 0.0, ALU.mult, ALU.max))
        t2 = DV.do(lambda e: e.tensor_tensor(s2, s2, s1, ALU.add), t1, t2)
        t_spl = DV.do(lambda e: e.tensor_scalar(SPL[:, :], s2, -8.0, None, ALU.mult), t2)
        t_up = DV.do(lambda e: e.memset(UP[:], 0.0))
        banks["use"] = [0, 1, 2, 3]
        mid = {"n": 0}
        fr = {"tm": t_spl}
        gfree = [None] * 2
        bdf = [None, None]
        xbar = [(k, v) for k, v in dma.n.items()]

        def lru_tile(m, tg, tz, tu):
            g = m % 2
            tb = dma(f"bd{g}", BD[:, g, :], D["lruw"][m], bdf[g])
            tbs = split_to(BH[:, g, :], BL[:, g, :], BD[:, g, :], tb, fr.get(f"BH{g}"))
            bdf[g] = tbs
            t = DV.do(lambda e: e.tensor_scalar(UC, UP[:, 0:T], vec("cw", 4 * m), None, ALU.mult), tu, fr.get("UC"))
            for c in range(1, 4):
                t = DV.do(lambda e, c=c: e.scalar_tensor_tensor(out=UC, in0=UP[:, c:c + T], scalar=vec("cw", 4 * m + c), in1=UC, op0=ALU.mult, op1=ALU.add), t)
            t = DV.do(lambda e: e.tensor_scalar(UC, UC, vec("cb", m), None, ALU.add), t)
            fr["UP"] = t
            tuc = t
            tsp = split_to(UH[:, :], UL[:, :], UC, t, fr.get("UH"))
            yield
            gt = {}
            for d in range(2):
                for w in range(2):
                    for h in range(2):
                        b = 4 + mid["n"] % 4
                        mid["n"] += 1
                        c = (2 * d + w) * 128
                        o = B[b][:, :]
                        xh, xl = UH[:, h * 512:h * 512 + 512], UL[:, h * 512:h * 512 + 512]
                        PE.quiet(lambda e, o=o, c=c, x=xh: e.matmul(o, BH[:, g, c:c + 128], x, start=True, stop=False), bfree[b], tsp, tbs)
                        PE.quiet(lambda e, o=o, c=c, x=xl: e.matmul(o, BH[:, g, c:c + 128], x, start=False, stop=False))
                        t = PE.do(lambda e, o=o, c=c, x=xh: e.matmul(o, BL[:, g, c:c + 128], x, start=False, stop=True))
                        dst = (Rg if w == 0 else Ig)[d][:, h * 512:h * 512 + 512]
                        bias = vec("lba" if w == 0 else "lbx", 8 * d + m)
                        gt[(d, w, h)] = AC.do(lambda e, dst=dst, o=o, bias=bias: e.activation(dst, o, ACT.Sigmoid, bias=bias), t, fr.get(("G", d, w)))
                        bfree[b] = gt[(d, w, h)]
                    yield
            fr["UH"] = t
            fr[f"BH{g}"] = t
            for d in range(2):
                r, i = Rg[d], Ig[d]
                tr_ = [gt[(d, 0, 0)], gt[(d, 0, 1)]]
                tla = DV.do(lambda e, r=r, d=d: e.tensor_scalar(r, r, SPL[:, 8 * d + m:8 * d + m + 1], None, ALU.mult), tr_, t_spl)
                yield
                w0, w1 = tm[:, 0, :], tm[:, 1, :]
                ti = DV.do(lambda e, i=i: e.tensor_tensor(i, i, UC, ALU.mult), gt[(d, 1, 0)], gt[(d, 1, 1)], tuc)
                tt = AC.do(lambda e, r=r: e.activation(w0, r, ACT.Tanh, scale=-0.5), tla, fr.get("tm"))
                ta = AC.do(lambda e, r=r: e.activation(r, r, ACT.Exp), tla, tt)
                tb2 = DV.do(lambda e, r=r: e.tensor_scalar(w1, r, 1.0, None, ALU.add), ta, fr.get("tm"))
                ts = AC.do(lambda e: e.activation(w0, w0, ACT.Sqrt), tt)
                tb3 = DV.do(lambda e: e.tensor_tensor(w1, w1, w0, ALU.mult), tb2, ts)
                yield
                tin = DV.do(lambda e, i=i: e.tensor_tensor(i, i, w1, ALU.mult), ti, tb3)
                fr["tm"] = tin
                if d == 0:
                    th = DV.do(lambda e, r=r, i=i: e.tensor_tensor_scan(HH, r, i, 0.0, ALU.mult, ALU.add), tin, fr.get("HH"))
                else:
                    th2 = DV.do(lambda e, r=r, i=i: e.tensor_tensor_scan(SQ[:, ::-1], r[:, ::-1], i[:, ::-1], 0.0, ALU.mult, ALU.add), tin, fr.get("SQ"))
                fr[("G", d, 0)] = fr[("G", d, 1)] = th if d == 0 else th2
                fr["UC"] = ti
                yield
            t = DV.do(lambda e: e.tensor_tensor(HH, HH, SQ, ALU.add), th, th2)
            t = DV.do(lambda e: e.tensor_tensor(HH, HH, GL[:, g, :], ALU.mult), t, tg)
            fr["SQ"] = t
            t = DV.do(lambda e: e.tensor_tensor(HH, HH, Z0[:, g, :], ALU.mult), t, tz)
            gfree[g] = t
            t = dma("mg", dM[m], HH, t)
            fr["HH"] = t
            written.setdefault("mg", []).append(t)
            yield

        def run_beside(g, n):
            for _ in range(n):
                if next(g, 0) == 0:
                    return

        side = iter(())
        for m in range(8):
            g = m % 2
            i = wget("u2", m)
            tus, tgs, tzs = [], [], []
            for h in range(2):
                b, t = product(i, h)
                run_beside(side, 1)
                u = AC.do(lambda e, b=b, h=h: e.activation(UP[:, 2 + h * 512:2 + h * 512 + 512], B[b][:, :], ACT.Copy), t, fr.get("UP"), t_up)
                bfree[b] = u
                tus.append(u)
            wdone(i, t)
            i = wget("g2", m)
            for h in range(2):
                b, t = product(i, h)
                run_beside(side, 2)
                u = AC.do(lambda e, b=b, h=h, g=g: e.activation(GL[:, g, h * 512:h * 512 + 512], B[b][:, :], ACT.Gelu_apprx_tanh), t, gfree[g])
                bfree[b] = u
                tgs.append(u)
            wdone(i, t)
            i = wget("z0", m)
            for h in range(2):
                b, t = product(i, h)
                run_beside(side, 3)
                u = AC.do(lambda e, b=b, h=h, g=g, m=m: e.activation(Z0[:, g, h * 512:h * 512 + 512], B[b][:, :], ACT.Sigmoid, bias=vec("bg", m)), t, gfree[g])
                bfree[b] = u
                tzs.append(u)
            wdone(i, t)
            run(side)
            side = lru_tile(m, tgs, tzs, tus)
        run(side)
        barrier()
        p5.close()

        p6 = ExitStack()
        S6 = lambda shape, dt, name="t": alloc(p6, shape, dt, name)
        ST = Stage(p6, NST, "st")
        KT = RES[:, 0:2, :]
        Vt = S6([128, 8, 2, 192], F, "vt")
        PR = RES[:, 4:7, :].rearrange("p a t -> p (a t)").rearrange("p (h s) -> p h s", h=8)
        QB = RES[:, 2, 0:512].rearrange("p (a t) -> p a t", a=4)
        ZB = RES[:, 2, 512:1024].rearrange("p (a t) -> p a t", a=4)
        MB = RES[:, 3, 0:512].rearrange("p (a t) -> p a t", a=4)
        AD = RES[:, 3, 512:896]
        PT = S6([128, 8, 3, 128], F, "pt")
        mx = S6([128, 8], F, "mx")
        es = S6([128, 8], F, "es")
        dn = S6([128, 8], F, "dn")
        t_v0 = DV.do(lambda e: e.memset(Vt[:], 0.0))
        t_ad = dma("ad0", AD, D["alibi"])
        tK, tVv = [], []
        banks["use"] = [0, 1]
        VF = S6([128, 2, 512], F, "vf2")
        for m in range(2):
            i = wget("k2", m)
            for h in range(2):
                b, t = product(i, h)
                bfree[b] = AC.do(lambda e, b=b, h=h, m=m: e.activation(KT[:, m, h * 512:h * 512 + 512], B[b][:, :], ACT.Copy), t)
                tK.append(bfree[b])
            wdone(i, t)
        vff = [None, None]
        for m in range(2):
            i = wget("v2", m)
            for h in range(2):
                b, t = product(i, h)
                q = h
                t1 = AC.do(lambda e, b=b, q=q: e.activation(VF[:, q, :], B[b][:, :], ACT.Copy), t, vff[q])
                bfree[b] = t1
                for c in range(4):
                    f = (lambda e, c=c, q=q: e.transpose(B[2][:, c * 128:c * 128 + 128], VF[:, q, c * 128:c * 128 + 128], ident[:]))
                    if c < 3:
                        PE.quiet(f, t1, bfree[2])
                    else:
                        t2 = PE.do(f)
                vff[q] = t2
                src = B[2][:, :].rearrange("p (c f) -> p c f", c=4)
                t3 = DV.do(lambda e, src=src, h=h, m=m: e.tensor_copy(Vt[:, 4 * h:4 * h + 4, m, 0:64], src[:, :, 0:64]), t2, t_v0)
                t3 = DV.do(lambda e, src=src, h=h, m=m: e.tensor_copy(Vt[:, 4 * h:4 * h + 4, m, 128:192], src[:, :, 64:128]))
                bfree[2] = t3
                tVv.append(t3)
            wdone(i, t)

        def put2(dst, name, func, scale=1.0, bias=None):
            def put(m, h, b, t):
                s, f = ST.take()
                o = ST.buf[:, s, :]
                bb = bias(m) if bias else 0.0
                t2 = AC.do(lambda e: e.activation(o, B[b][:, :], func, scale=scale, bias=bb) if bias else e.activation(o, B[b][:, :], func, scale=scale), t, f)
                bfree[b] = t2
                ST.store(s, dst[m][:, h * 512:h * 512 + 512], o, name, t2)
            return put

        def project2(name, m, put):
            i = wget(name, m)
            for h in range(2):
                b, t = product(i, h)
                put(m, h, b, t)
                yield
            wdone(i, t)

        pq = put2(dQ2, "q2", ACT.Copy, scale=0.125)
        pz = put2(dZ1, "z1", ACT.Sigmoid, bias=lambda m: vec("bg", 8 + m))

        def fill2(a):
            for m in range(4 * a, 4 * a + 4):
                yield from project2("q2", m, pq)
            for m in range(4 * a, 4 * a + 4):
                yield from project2("z1", m, pz)

        af = {}
        slopes = [float(2.0 ** (-8.0 * (h + 1) / 16)) for h in range(16)]

        def attend(pair, blk):
            c0 = blk * 128
            tiles = slice(4 * pair, 4 * pair + 4)
            tq = dma("qb", QB, dQ2[tiles, :, c0:c0 + 128].rearrange("a p t -> p a t"), written["q2"], af.get("q"))
            k0, k1 = max(0, blk - 1), min(8, blk + 2)
            n = (k1 - k0) * 128
            a0 = (k0 - blk + 1) * 128
            yield
            tp = []
            for kv in range(2):
                for a in range(4):
                    x = kv * 4 + a
                    b = 3 + x % 2
                    head = 4 * (2 * pair + kv) + a
                    t = PE.do(lambda e, b=b, a=a, kv=kv: e.matmul(B[b][:, 0:n], QB[64 * kv:64 * kv + 64, a, :], KT[64 * kv:64 * kv + 64, pair, k0 * 128:k0 * 128 + n], start=True, stop=True),
                              bfree[b], tq, tK)
                    t1 = DV.do(lambda e, b=b, x=x, head=head: e.scalar_tensor_tensor(out=PR[:, x, 0:n], in0=AD[:, a0:a0 + n], scalar=-slopes[head], in1=B[b][:, 0:n], op0=ALU.mult, op1=ALU.add),
                               t, t_ad, af.get("p"))
                    bfree[b] = t1
                    af["q"] = t
                yield
            sink = VEC[:, V["sink"] + 8 * pair:V["sink"] + 8 * pair + 8]
            t2 = DV.do(lambda e: e.tensor_reduce(mx[:, :], PR[:, :, 0:n], AX.X, ALU.max), t1, af.get("mx"))
            t3 = DV.do(lambda e: e.tensor_tensor(mx[:, :], mx[:, :], sink, ALU.max), t2)
            t4 = DV.do(lambda e: e.tensor_tensor(es[:, :], sink, mx[:, :], ALU.subtract), t3, af.get("es"))
            t5 = DV.do(lambda e: e.tensor_scalar(mx[:, :], mx[:, :], -1.0, None, ALU.mult), t4)
            t6 = AC.do(lambda e: e.activation(es[:, :], es[:, :], ACT.Exp), t4)
            for x in range(8):
                t7 = AC.do(lambda e, x=x: e.activation(PR[:, x, 0:n], PR[:, x, 0:n], ACT.Exp, bias=mx[:, x:x + 1], accum_out=dn[:, x:x + 1]), t5, af.get("dn"))
            af["mx"] = t7
            t8 = DV.do(lambda e: e.tensor_tensor(dn[:, :], dn[:, :], es[:, :], ALU.add), t6, t7)
            af["es"] = t8
            t9 = DV.do(lambda e: e.reciprocal(dn[:, :], dn[:, :]), t8)
            yield
            tn = []
            for x in range(8):
                tn.append(DV.do(lambda e, x=x: e.tensor_scalar(PR[:, x, 0:n], PR[:, x, 0:n], dn[:, x:x + 1], None, ALU.mult), t9))
            af["dn"] = tn[-1]
            yield
            tpt = []
            for x in range(8):
                b = 5 + x % 2
                for c in range(n // 128):
                    f = (lambda e, b=b, c=c, x=x: e.transpose(B[b][:, c * 128:c * 128 + 128], PR[:, x, c * 128:c * 128 + 128], ident[:]))
                    if c < n // 128 - 1:
                        PE.quiet(f, tn[x], bfree[b])
                    else:
                        t = PE.do(f, tn[x], bfree[b])
                dst = PT[:, x, 0:n // 128, :]
                src = B[b][:, 0:n].rearrange("p (c t) -> p c t", t=128)
                if x % 2:
                    tc = DV.do(lambda e, dst=dst, src=src: e.tensor_copy(dst, src), t, af.get("pt"))
                else:
                    tc = AC.do(lambda e, dst=dst, src=src: e.activation(dst, src, ACT.Copy), t, af.get("pt"))
                bfree[b] = tc
                tpt.append(tc)
                if x == 3:
                    yield
            af["p"] = t
            yield
            tz = dma("zb", ZB, dZ1[tiles, :, c0:c0 + 128].rearrange("a p t -> p a t"), written["z1"], af.get("z"))
            tm_ = dma("mb", MB, dM[tiles, :, c0:c0 + 128].rearrange("a p t -> p a t"), written["mg"], af.get("m"))
            mms = []
            for kv in range(2):
                for c in range(n // 128):
                    mms.append((kv, c))
            for x, (kv, c) in enumerate(mms):
                f = (lambda e, kv=kv, c=c, x=x: e.matmul(B[7][:, :].rearrange("p (a t) -> p a t", a=4), Vt[:, k0 + c, pair, 64 * kv:64 * kv + 128], PT[:, 4 * kv:4 * kv + 4, c, :],
                                                         start=(x == 0), stop=(x == len(mms) - 1)))
                if x < len(mms) - 1:
                    PE.quiet(f, tpt, tVv, bfree[7])
                else:
                    t = PE.do(f)
            af["pt"] = t
            o = B[7][:, :].rearrange("p (a t) -> p a t", a=4)
            t1 = DV.do(lambda e: e.tensor_tensor(ZB, o, ZB, ALU.mult), t, tz)
            bfree[7] = t1
            s, f = ST.take()
            so = ST.buf[:, s, :].rearrange("p (a t) -> p a t", a=4)
            t2 = DV.do(lambda e: e.tensor_tensor(so, ZB, MB, ALU.add), t1, tm_, f)
            af["z"] = af["m"] = t2
            ST.store(s, dY[tiles, :, c0:c0 + 128].rearrange("a p t -> p a t"), so, "y", t2)
            yield

        dY = scratch("y", [8, 128, T])

        def attend_all(pair):
            for blk in range(8):
                yield from attend(pair, blk)

        run(fill2(0))
        together(fill2(1), 16, attend_all(0), 72)
        run(attend_all(1))
        barrier()
        p6.close()

        p7 = ExitStack()
        LX = alloc(p7, [128, 2, T], F, "lx")
        lq = alloc(p7, [128, 4, 512], F, "lq")
        acc = alloc(p7, [128, T], F, "acc")
        sq = alloc(p7, [128, T], F, "sq")
        banks["use"] = list(range(8))
        load_split(dY, "y", None, (PE.name, PE.n))
        tr, ta, tl = out_branch("wo2", lambda m: ones[:, 0:1], dX, "x2", None, lq, [None] * 4)
        trb = rms_scale(acc, T, sq, ta)
        outs = norm_gain(RES, sq, trb, "nf2", XH, XL, tr, tl)
        xtok[0], xtok[1] = outs, outs
        barrier()
        p7.close()
        last = ffn("f12", "f22", True, lambda m: ones[:, 0:1])

        acc = A([128, T], F, "acc")
        sq = A([128, T], F, "sq")
        tsq = tacc = None
        for k in range(8):
            tsq, tacc = sum_squares(acc[:, :], sq[:, :], RES[:, k, :], k, [last[(k, 0)], last[(k, 1)]], tsq, tacc)
        trb = rms_scale(acc, T, sq, [tsq, tacc])
        for k in range(8):
            t = DV.do(lambda e, k=k: e.scalar_tensor_tensor(out=RES[:, k, :], in0=RES[:, k, :], scalar=vec("nfin", k), in1=sq[:, :], op0=ALU.mult, op1=ALU.mult), trb)
            dma(f"x{k}", out[k], RES[:, k, :], t)
        assert state["next"] == len(order)
        SP.wait([(k, v) for k, v in dma.n.items()])


VECTORS = [("b_ada", 48), ("n1", 8), ("n2", 8), ("b_al", 8), ("gn", 8), ("nm2", 8), ("lam", 16), ("lba", 16), ("lbx", 16),
           ("cw", 32), ("cb", 8), ("bg", 16), ("sink", 16), ("nf2", 8), ("nfin", 8), ("fin1", 8)]
assert sum(n for _, n in VECTORS) <= 240


def layout(x, c, ctx, c_ctx, w_ada, b_ada, norm1_g, w_in, ln_v_g, ln_v_b, w_spatial, b_spatial,
           w_alpha_f, b_alpha_f, w_alpha_b, b_alpha_b, gla_norm_g, w_branch_a, w_branch_b, w_out,
           norm2_g, w_ffn_in, w_ffn_out, final_norm_g, norm_mix_g_2, w_in_2, b_gate_2, conv_w_2,
           conv_b_2, lru_lambda_2, lru_wa_2, lru_ba_2, lru_wx_2, lru_bx_2, attn_sink_2, w_out_2,
           norm_ffn_g_2, w_ffn_in_2, w_ffn_out_2, norm_final_g_2):
    def cols(v):
        return np.asarray(v).reshape(-1, 128).T

    def tiles(w, width=128):
        k, m = w.shape
        return np.ascontiguousarray(w.reshape(k // 128, 128, m // width, width).transpose(2, 1, 0, 3).reshape(m // width, 128, k // 128 * width))

    f = np.float32
    heads = np.array([h for a in range(2) for i in range(4) for h in (8 * a + i, 8 * a + 4 + i)])
    perm = (heads[:, None] * 64 + np.arange(64)).reshape(-1)
    D = {}
    D["xT"] = np.ascontiguousarray(x[0].T).reshape(8, 128, 1024)
    D["ctxT"] = np.ascontiguousarray(ctx[0].T.reshape(8, 128, 256).transpose(1, 0, 2))
    D["cc"] = np.ascontiguousarray(np.stack([c[0].reshape(8, 128), c_ctx.reshape(8, 128)], -1).transpose(1, 0, 2))
    D["crow"] = np.ascontiguousarray(np.broadcast_to(c[0], (128, 1024)))
    D["ada"] = np.ascontiguousarray(w_ada[0][:, 0:2048].reshape(8, 128, 2048))
    D["adaT"] = np.ascontiguousarray(w_ada[0][:, 2048:].T).reshape(32, 128, 1024)
    w = w_in[0]
    at = 0
    for name, n in (("u", 1024), ("v", 1024), ("q", 512), ("k", 512), ("vv", 1024), ("r", 1024), ("al", 32), ("ga", 1024), ("gb", 1024)):
        D["W" + name] = tiles(w[:, at:at + n], min(n, 128))
        at += n
    D["Wwa"], D["Wwb"], D["Wwo"] = tiles(w_branch_a[0]), tiles(w_branch_b[0]), tiles(w_out[0])
    D["Wf1"] = tiles(w_ffn_in[0])
    D["Wf2"] = np.ascontiguousarray(w_ffn_out[0]).reshape(22, 128, 1024)
    wal = np.zeros((32, 2, 512), f)
    wal[0:16, 0] = w_alpha_f[0]
    wal[16:32, 1] = w_alpha_b[0]
    D["walpha"] = wal
    D["wspT"] = np.ascontiguousarray(w_spatial[0].transpose(2, 0, 1)).reshape(128, 1024)
    D["bspb"] = np.ascontiguousarray(np.broadcast_to(b_spatial[0].reshape(1, 1024), (128, 1024)))
    D["lnvb"] = np.ascontiguousarray(np.broadcast_to(np.stack([ln_v_g[0], ln_v_b[0]]), (128, 2, 1024)))
    w = w_in_2[0]
    D["Wu2"], D["Wg2"] = tiles(w[:, 0:1024][:, perm]), tiles(w[:, 1024:2048][:, perm])
    D["Wq2"], D["Wk2"], D["Wv2"] = tiles(w[:, 2048:3072][:, perm]), tiles(w[:, 3072:3328]), tiles(w[:, 3328:3584])
    D["Wz0"], D["Wz1"] = tiles(w[:, 3584:4608][:, perm]), tiles(w[:, 4608:5632][:, perm])
    D["Wwo2"] = tiles(w_out_2[0][perm])
    D["Wf12"] = tiles(w_ffn_in_2[0])
    D["Wf22"] = np.ascontiguousarray(w_ffn_out_2[0]).reshape(22, 128, 1024)
    lw = np.zeros((8, 128, 4, 128), f)
    for m in range(8):
        for j in range(2):
            h = heads[2 * m + j]
            for d in range(2):
                for y, src in enumerate((lru_wa_2, lru_wx_2)):
                    lw[m, 64 * j:64 * j + 64, 2 * d + y, 64 * j:64 * j + 64] = src[0, d, h]
    D["lruw"] = lw.reshape(8, 128, 512)
    bg = b_gate_2[0].reshape(2, 1024)[:, perm]
    parts = {
        "b_ada": cols(b_ada[0]), "n1": cols(norm1_g[0]), "n2": cols(norm2_g[0]),
        "b_al": np.concatenate([cols(b_alpha_f[0]), cols(b_alpha_b[0])], 1), "gn": cols(gla_norm_g[0]),
        "nm2": None, "lam": cols(lru_lambda_2[0][:, perm]), "lba": cols(lru_ba_2[0][:, perm]), "lbx": cols(lru_bx_2[0][:, perm]),
        "cw": conv_w_2[0][:, perm].reshape(4, 8, 128).transpose(2, 1, 0).reshape(128, 32), "cb": cols(conv_b_2[0][perm]),
        "bg": cols(bg), "sink": np.broadcast_to(attn_sink_2[0], (128, 16)), "nf2": cols(norm_ffn_g_2[0]), "nfin": cols(norm_final_g_2), "fin1": cols(final_norm_g),
    }
    parts["nm2"] = cols(norm_mix_g_2[0])
    v = np.concatenate([parts[n] for n, _ in VECTORS], 1)
    D["vec"] = np.ascontiguousarray(np.concatenate([v, np.zeros((128, 240 - v.shape[1]), f)], 1))
    D["ident"] = np.eye(128, dtype=f)
    cm = np.ones((128, 512), f)
    cm[:, ::64] = 0
    D["cmask"] = cm
    j, i = np.arange(128)[:, None], np.arange(128)[None]
    D["amask0"] = ((j // 64 == i // 64) & (j <= i)).astype(np.int32)
    D["amask1"] = ((j // 64 == i // 64) & (j >= i)).astype(np.int32)
    s = np.arange(384)[None]
    dist = np.abs(j + 128 - s)
    D["alibi"] = np.where(dist <= 128, dist, 1e34).astype(f)
    return D


def kernel(**inputs):
    import concourse.bacc as bacc
    from concourse.bass_utils import run_bass_kernel_spmd

    D = layout(**{k: np.asarray(v) for k, v in inputs.items()})
    nc = bacc.Bacc("TRN2", target_bir_lowering=False, num_devices=1)
    aps = {n: nc.dram_tensor("i_" + n, a.shape, mybir.dt.from_np(a.dtype), kind="ExternalInput").ap() for n, a in D.items()}
    out = nc.dram_tensor("o_out", (8, 128, 1024), F, kind="ExternalOutput").ap()
    program(nc, aps, out)
    r = run_bass_kernel_spmd(nc, [{"i_" + n: a for n, a in D.items()}], core_ids=[0])
    y = np.asarray(r.results[0]["o_out"])
    return np.ascontiguousarray(y.reshape(1024, 1024).T)[None]
```

```python
from contextlib import ExitStack

import numpy as np

import concourse.bass as bass
from concourse import mybir

F = mybir.dt.float32
R = mybir.dt.float32r
I32 = mybir.dt.int32
ALU = mybir.AluOpType
ACT = mybir.ActivationFunctionType
AX = mybir.AxisListType

T = 1024
TC = 256
NF = 22
EPS = 1e-6
NW = 4
NS = 2
NT = 4


class Engine:

    def __init__(self, name, eng, sems):
        self.name, self.eng, self.sems, self.n, self.seen = name, eng, sems, 0, {}

    def wait(self, *tokens):
        for t in tokens:
            if t is None:
                continue
            if isinstance(t, list):
                self.wait(*t)
            elif self.seen.get(t[0], 0) < t[1]:
                self.seen[t[0]] = t[1]
                self.eng.wait_ge(self.sems(t[0]), t[1])

    def do(self, fn, *tokens):
        self.wait(*tokens)
        self.n += 1
        fn(self.eng).then_inc(self.sems(self.name), 1)
        return (self.name, self.n)

    def quiet(self, fn, *tokens):
        self.wait(*tokens)
        fn(self.eng)


class Dma:

    def __init__(self, eng):
        self.eng, self.n = eng, {}

    def __call__(self, key, out, in_, *tokens):
        self.eng.wait(*tokens)
        self.n[key] = self.n.get(key, 0) + 16
        self.eng.eng.dma_start(out, in_).then_inc(self.eng.sems(key), 16)
        return (key, self.n[key])


def weight_order():
    order = [("al", 0)]
    order += [("k", m) for m in range(4)] + [("vv", m) for m in range(8)] + [("q", m) for m in range(4)]
    for n in ("v", "u", "r", "ga", "gb"):
        order += [(n, m) for m in range(8)]
    for n in ("wa", "wb", "wo"):
        order += [(n, m) for m in range(8)]
    order += ffn_order("f1", "f2")
    for m in range(8):
        order += [("u2", m), ("g2", m), ("z0", m)]
    order += [("k2", 0), ("k2", 1), ("v2", 0), ("v2", 1)]
    order += [("q2", m) for m in range(8)] + [("z1", m) for m in range(8)]
    order += [("wo2", m) for m in range(8)]
    order += ffn_order("f12", "f22")
    return order


GROUPS = [(2 * i, 2 * i + 1) for i in range(NF // 2)]


def ffn_order(one, two):
    order = []
    for i, g in enumerate(GROUPS):
        for t in g:
            order += [(one, t), (one, NF + t)]
        if i:
            order += [(two, t) for t in GROUPS[i - 1]]
    return order + [(two, t) for t in GROUPS[-1]]


def program(nc, D, out):
    top = ExitStack()
    with top:
        held = {}

        def sems(key):
            if key not in held:
                held[key] = nc.alloc_semaphore("q_" + key)
            return held[key]

        PE, AC, DV, PO, SP = (Engine(n, e, sems) for n, e in (("pe", nc.tensor), ("ac", nc.scalar), ("dv", nc.vector), ("po", nc.gpsimd), ("sp", nc.sync)))
        dma = Dma(SP)
        cnt = [0]

        def alloc(stack, shape, dt, name="t"):
            cnt[0] += 1
            return stack.enter_context(nc.sbuf_tensor(f"s_{name}{cnt[0]}", shape, dt))

        def A(shape, dt, name="t"):
            return alloc(top, shape, dt, name)

        def scratch(name, shape):
            return nc.dram_tensor("d_" + name, shape, F, kind="Internal").ap()

        XH = A([128, 8, T], R, "xh")
        XL = A([128, 8, T], R, "xl")
        WH = A([128, NW, 1024], R, "wh")
        WL = A([128, NW, 1024], R, "wl")
        WS = A([128, NS, 1024], F, "ws")
        RES = A([128, 8, T], F, "res")
        TMP = A([128, NT, 512], F, "tmp")
        ACC = A([128, T], F, "acc")
        RB = A([128, T], F, "rb")
        ident = A([128, 128], F, "ident")
        ones = A([128, 128], F, "ones")
        MOD = A([128, 48], F, "mod")
        MODC = A([128, 16], F, "modc")
        VEC = A([128, 240], F, "vec")
        GS = A([128, 24], F, "gs")
        eps = A([128, 1], F, "eps")
        B = [top.enter_context(nc.psum_tensor(f"p_{i}", [128, 512], F)) for i in range(8)]
        bfree = [None] * 8

        t_vec = dma("vec", VEC[:], D["vec"])
        t_id = dma("ident", ident[:], D["ident"])
        t_ones = DV.do(lambda e: e.memset(ones[:], 1.0))
        t_eps = DV.do(lambda e: e.memset(eps[:], EPS))

        V = {}
        at = 0
        for name, n in VECTORS:
            V[name] = at
            at += n

        def vec(name, m):
            return VEC[:, V[name] + m:V[name] + m + 1]

        def barrier(skip=()):
            t = [(e.name, e.n) for e in (PE, AC, DV) if e.n]
            t += [(k, v) for k, v in dma.n.items() if not k.startswith(("ws",) + tuple(skip))]
            for e in (AC, DV, SP):
                e.wait(t)

        order = weight_order()
        wsplit, wfree, wload = {}, {}, {}
        state = {"next": 0, "loaded": 0, "split": 0}

        def wload_to(n):
            while state["loaded"] < min(n, len(order)):
                i = state["loaded"]
                name, m = order[i]
                src = D["W" + name][m]
                cols = src.shape[1]
                wload[i] = dma(f"ws{i % NS}", WS[:, i % NS, 0:cols], src, wsplit.get(i - NS))
                state["loaded"] += 1

        def wsplit_to(n):
            while state["split"] < min(n, len(order)):
                i = state["split"]
                wload_to(i + 1)
                s, w = i % NS, i % NW
                cols = D["W" + order[i][0]][order[i][1]].shape[1]
                hi, lo, src = WH[:, w, 0:cols], WL[:, w, 0:cols], WS[:, s, 0:cols]
                t1 = AC.do(lambda e: e.activation(hi, src, ACT.Copy), wload[i], wfree.get(i - NW))
                t2 = DV.do(lambda e: e.tensor_tensor(lo, src, hi.bitcast(F), ALU.subtract), wload[i], t1)
                wsplit[i] = [t1, t2]
                state["split"] += 1

        def wget(name, m):
            i = state["next"]
            assert order[i] == (name, m), (order[i], name, m)
            state["next"] += 1
            wsplit_to(i + 3)
            wload_to(i + 5)
            return i

        def wdone(i, token):
            wfree[i] = token

        banks = {"use": [0, 1, 2], "n": 0}

        def bank():
            b = banks["use"][banks["n"] % len(banks["use"])]
            banks["n"] += 1
            return b

        xtok = [[None] * 8, [None] * 8]

        def products(ws, half, M=128, X=None, n=512, tok=None, mid=None):
            H, L = X or (XH, XL)
            tok = tok or xtok[half]
            bs = [bank() for _ in ws]
            out = []
            for k in range(8):
                if k == 5 and mid:
                    mid()
                PE.wait(tok[k])
                xh, xl = H[:, k, half * n:half * n + n], L[:, k, half * n:half * n + n]
                for b, i in zip(bs, ws):
                    w = i % NW
                    o = B[b][0:M, 0:n]
                    wh, wl = WH[:, w, k * M:(k + 1) * M], WL[:, w, k * M:(k + 1) * M]
                    if k == 0:
                        PE.wait(bfree[b], wsplit[i])
                    PE.quiet(lambda e: e.matmul(o, wh, xh, start=(k == 0), stop=False))
                    PE.quiet(lambda e: e.matmul(o, wh, xl, start=False, stop=False))
                    f = (lambda e: e.matmul(o, wl, xh, start=False, stop=(k == 7)))
                    if k < 7:
                        PE.quiet(f)
                    else:
                        out.append((b, PE.do(f)))
            return out

        def product(i, half, **kw):
            return products([i], half, **kw)[0]

        def split_to(hi, lo, src, *tokens):
            t1 = AC.do(lambda e: e.activation(hi, src, ACT.Copy), *tokens)
            t2 = DV.do(lambda e: e.tensor_tensor(lo, src, hi.bitcast(F), ALU.subtract), t1, *tokens)
            return [t1, t2]

        later = []

        def run_later():
            todo, later[:] = later[:], []
            for f in todo:
                f()

        written = {}
        ring = {"i": 0, "free": [None] * NT}

        def take():
            s = ring["i"] % NT
            ring["i"] += 1
            return s, ring["free"][s]

        def store(s, dst, src, name, *tokens):
            t = dma(f"st{s}", dst, src, *tokens)
            ring["free"][s] = t
            written.setdefault(name, []).append(t)
            return t

        def square_sum(x, c, n, first, tx, tacc):
            a = ACC[:, c:c + n]
            if first:
                return AC.do(lambda e: e.activation(a, x, ACT.Square), tx, tacc)
            s, fr = take()
            q = TMP[:, s, 0:n]
            t1 = AC.do(lambda e: e.activation(q, x, ACT.Square), tx, fr)
            t2 = DV.do(lambda e: e.tensor_tensor(a, a, q, ALU.add), t1, tacc)
            ring["free"][s] = t2
            return t2

        def rms_sum(c, n, tacc):
            b = bank()
            t = PE.do(lambda e: e.matmul(B[b][:, 0:n], ones[:], ACC[:, c:c + n], start=True, stop=True), bfree[b], tacc, t_ones)
            return b, t

        def rms_scale(c, n, bt, trb):
            b, t = bt
            r = RB[:, c:c + n]
            t2 = AC.do(lambda e: e.activation(r, B[b][:, 0:n], ACT.Sqrt, bias=eps[:, 0:1], scale=1.0 / 1024), t, t_eps, trb)
            bfree[b] = t2
            return DV.do(lambda e: e.reciprocal(r, r), t2)

        def norm_tiles(src, c, n, trb, scale, shift, H, L, ready, free):
            outs, todo = [], None
            r = RB[:, c:c + n]
            for k in range(8):
                s, fr = take()
                q, x = TMP[:, s, 0:n], src[:, k, c:c + n]
                h, l = H[:, k, c:c + n], L[:, k, c:c + n]
                t1 = DV.do(lambda e: e.scalar_tensor_tensor(out=q, in0=x, scalar=scale(k), in1=r, op0=ALU.mult, op1=ALU.mult), trb, ready[k], fr)
                if shift:
                    t2 = AC.do(lambda e: e.activation(h, q, ACT.Identity, bias=shift(k)), t1, free)
                else:
                    t2 = AC.do(lambda e: e.activation(h, q, ACT.Copy), t1, free)
                if todo:
                    todo()

                def todo(s=s, q=q, h=h, l=l, k=k, t2=t2):
                    if shift:
                        t3 = DV.do(lambda e: e.scalar_tensor_tensor(out=l, in0=q, scalar=shift(k), in1=h.bitcast(F), op0=ALU.add, op1=ALU.subtract), t2, free)
                    else:
                        t3 = DV.do(lambda e: e.tensor_tensor(l, q, h.bitcast(F), ALU.subtract), t2, free)
                    ring["free"][s] = [t2, t3]
                    outs.append([t2, t3])
            todo()
            return outs

        def pe_now():
            return ("pe", PE.n)

        pc = ExitStack()
        CH = alloc(pc, [128, 8, TC], R, "ch")
        CL = alloc(pc, [128, 8, TC], R, "cl")
        p0 = ExitStack()
        sc2 = alloc(p0, [128, 8, 2], F, "sc2")
        AD = alloc(p0, [128, 2, 2048], F, "ad")
        XC = alloc(p0, [128, 8, TC], F, "xc")
        mrow = WS[0:2, :, :].rearrange("p s n -> p (s n)")

        t_cc = dma("cc", sc2[:], D["cc"])
        t_sc = AC.do(lambda e: e.activation(sc2[:, :, :], sc2[:, :, :], ACT.Silu), t_cc)
        banks["use"] = [4, 5, 6, 7]
        tad = [None, None]
        tx = [None] * 8
        tacc = [None, None]
        txc = dma("xc", XC[:], D["ctxT"])
        for k in range(8):
            t = dma(f"ad{k % 2}", AD[:, k % 2, :], D["ada"][k], tad[k % 2])
            tx[k] = dma(f"x{k}", RES[:, k, :], D["xT"][k])
            for c in range(4):
                f = (lambda e: e.matmul(B[c][0:2, :], sc2[:, k, :], AD[:, k % 2, c * 512:c * 512 + 512], start=(k == 0), stop=(k == 7)))
                if c < 3:
                    PE.quiet(f, t, t_sc)
                else:
                    tad[k % 2] = PE.do(f)
        tc_ = None
        for k in range(8):
            s, fr = take()
            q, x = TMP[:, s, 0:TC], XC[:, k, :]
            if k == 0:
                tc_ = AC.do(lambda e: e.activation(RB[:, 0:TC], x, ACT.Square), txc)
            else:
                t1 = AC.do(lambda e: e.activation(q, x, ACT.Square), txc, fr)
                tc_ = DV.do(lambda e: e.tensor_tensor(RB[:, 0:TC], RB[:, 0:TC], q, ALU.add), t1, tc_)
                ring["free"][s] = tc_
        for k in range(8):
            for h in range(2):
                tacc[h] = square_sum(RES[:, k, 512 * h:512 * h + 512], 512 * h, 512, k == 0, tx[k], tacc[h])
        tmr = None
        for c in range(4):
            tmr = AC.do(lambda e: e.activation(mrow[:, c * 512:c * 512 + 512], B[c][0:2, :], ACT.Copy), tad[0], tad[1])
        bfree[0:4] = [tmr] * 4
        for m in range(16):
            f = (lambda e: e.transpose(B[0][:, 2 * m:2 * m + 2], mrow[:, m * 128:m * 128 + 128], ident[0:2, 0:2]))
            if m < 15:
                PE.quiet(f, tmr, t_id)
            else:
                t = PE.do(f)
        mp = B[0][:, 0:32].rearrange("p (m j) -> p j m", j=2)
        bada = VEC[:, V["b_ada"]:V["b_ada"] + 16]
        t_m1 = DV.do(lambda e: e.tensor_tensor(MOD[:, 0:16], mp[:, 0, :], bada, ALU.add), t, t_vec)
        t_m2 = DV.do(lambda e: e.tensor_tensor(MODC[:, 0:16], mp[:, 1, :], bada, ALU.add))
        bfree[0] = t_m2
        n1 = VEC[:, V["n1"]:V["n1"] + 8]
        t_g1 = DV.do(lambda e: e.scalar_tensor_tensor(out=GS[:, 0:8], in0=MOD[:, 8:16], scalar=1.0, in1=n1, op0=ALU.add, op1=ALU.mult), t_m1)
        t_g2 = DV.do(lambda e: e.scalar_tensor_tensor(out=GS[:, 8:16], in0=MODC[:, 8:16], scalar=1.0, in1=n1, op0=ALU.add, op1=ALU.mult), t_m2)

        b = bank()
        t = PE.do(lambda e: e.matmul(B[b][:, 0:TC], ones[:], RB[:, 0:TC], start=True, stop=True), tc_, t_ones)
        trc = rms_scale(0, TC, (b, t), t)
        bt = [rms_sum(512 * h, 512, tacc[h]) for h in range(2)]
        ctok = norm_tiles(XC, 0, TC, [trc, t_g2], lambda k: GS[:, 8 + k:9 + k], lambda k: MODC[:, k:k + 1], CH, CL, [txc] * 8, None)
        for h in range(2):
            trb = rms_scale(512 * h, 512, bt[h], ctok[7] if h == 0 else None)
            xtok[h] = norm_tiles(RES, 512 * h, 512, [trb, t_g1], lambda k: GS[:, k:k + 1], lambda k: MOD[:, k:k + 1], XH, XL, tx, None)
        wload[-1] = t_m2
        barrier(("vec", "ident"))
        wsplit_to(2)
        wload_to(3)
        p0.close()

        dB = [scratch("bf", [4, 128, T + TC]), scratch("bb", [4, 128, T + TC])]
        dK = scratch("k", [4, 128, T + TC])
        dQ = scratch("q", [4, 128, T])
        dV = scratch("v", [10, 128, 1024])
        dVm = scratch("vm", [8, 128, 1024])
        dU = scratch("u", [8, 128, T])
        dR = scratch("r", [8, 128, T])
        dGA = scratch("ga", [8, 128, T])
        dGB = scratch("gb", [8, 128, T])
        dA = scratch("a", [8, 128, T])
        dBo = scratch("bo", [8, 128, T])

        p1 = ExitStack()
        banks["use"] = [0, 1, 2]

        def parts(ctx):
            p = [(TC, 0, 512, (XH, XL), None), (TC + 512, 1, 512, (XH, XL), None)]
            if ctx:
                p = [(0, 0, 256, (CH, CL), ctok)] + p
            return p

        AL = alloc(p1, [128, T + TC], R, "al")
        WAL = alloc(p1, [128, 2, 512], R, "wal")
        WA0 = alloc(p1, [128, 2, 512], F, "wa0")
        LG = alloc(p1, [128, 2, 2, 512], F, "lg")
        cmask = alloc(p1, [128, 512], F, "cmask")
        cb = alloc(p1, [128, 1024], F, "cb")
        aw = alloc(p1, [128, 1024], F, "aw")
        t_wal = dma("wal", WA0[:], D["walpha"])
        t_cm = dma("cmask", cmask[:], D["cmask"])
        t_cb = dma("cb", cb[:], D["crow"])
        t_cb = AC.do(lambda e: e.activation(cb[:, :], cb[:, :], ACT.Silu), t_cb)
        t1 = AC.do(lambda e: e.activation(WAL[:, :, :], WA0[:, :, :], ACT.Copy), t_wal)
        t_wal = DV.do(lambda e: e.tensor_tensor(WAL[64:96, :, :], WA0[64:96, :, :], WAL[64:96, :, :].bitcast(F), ALU.subtract), t1)

        def turned(src, n, col, m, dst, name, ts, tbank):
            c4 = n // 128
            for c in range(c4):
                f = (lambda e: e.transpose(B[tbank][:, c * 128:c * 128 + 128], src[:, c * 128:c * 128 + 128], ident[:]))
                if c < c4 - 1:
                    PE.quiet(f, bfree[tbank], ts, t_id)
                else:
                    t = PE.do(f, bfree[tbank], ts, t_id)
            s, fr = take()
            t2 = DV.do(lambda e: e.tensor_copy(TMP[:, s, 0:n], B[tbank][:, 0:n]), t, fr)
            bfree[tbank] = t2
            store(s, dst[col // 128:col // 128 + c4, :, m * 128:m * 128 + 128].rearrange("c p f -> p c f"),
                  TMP[:, s, 0:n].rearrange("p (c f) -> p c f", f=128), name, t2)
            return t

        VF = [ACC[:, 0:512], ACC[:, 512:1024], RB[:, 0:512], RB[:, 512:1024]]
        vf = {"i": 0, "free": [[xtok[0][7], xtok[1][7]]] * 4}

        def project(name, m, ctx, put):
            i = wget(name, m)
            for col, h, n, X, tok in parts(ctx):
                b, t = product(i, h, X=X, n=n, tok=tok)
                run_later()
                put(m, col, n, B[b][:, 0:n], b, t)
                yield
            wdone(i, t)

        def put_plain(dst, name, off, scale=1.0):
            def put(m, col, n, ps, b, t):
                s, fr = take()
                o = TMP[:, s, 0:n]
                t2 = AC.do(lambda e: e.activation(o, ps, ACT.Copy, scale=scale), t, fr)
                bfree[b] = t2
                store(s, dst[m][:, col - off:col - off + n], o, name, t2)
            return put

        def put_turned(dst, name, off, tbank):
            def put(m, col, n, ps, b, t):
                q = vf["i"] % 4
                vf["i"] += 1
                o = VF[q][:, 0:n]
                t2 = AC.do(lambda e: e.activation(o, ps, ACT.Copy), t, vf["free"][q])
                bfree[b] = t2

                def go():
                    vf["free"][q] = turned(o, n, col - off, m, dst, name, t2, tbank)
                later.append(go)
            return put

        def run(g):
            for _ in g:
                pass

        def beside(fill, work, rate):
            due = 0.0
            for _ in fill:
                due += rate
                while due >= 1:
                    due -= 1
                    next(work, 0)
                yield
            for _ in work:
                yield

        def projections():
            for m in range(4):
                yield from project("k", m, True, put_plain(dK, "k", 0))
            for m in range(8):
                yield from project("vv", m, True, put_turned(dV, "v", 0, 3))
            for m in range(4):
                yield from project("q", m, False, put_plain(dQ, "q", TC, scale=float(128 ** -0.5)))

        i = wget("al", 0)
        tal = []
        for col, h, n, X, tok in parts(True):
            b, t = product(i, h, X=X, n=n, tok=tok)
            o = AL[:, col:col + n]
            t2 = AC.do(lambda e: e.activation(o, B[b][:, 0:n], ACT.Copy), t)
            lo = AL[32:64, col:col + n]
            t3 = DV.do(lambda e: e.tensor_tensor(lo, B[b][32:64, 0:n], lo.bitcast(F), ALU.subtract), t2)
            bfree[b] = t3
            tal.append((col, n, [t2, t3]))
        wdone(i, t)

        def decays():
            tlg = [None, None]
            j = 0
            for d in range(2):
                for h in range(4):
                    for col, n, ta in tal:
                        b = 4 + j % 2
                        q = j % 2
                        j += 1
                        t = PE.do(lambda e: e.matmul(B[b][:, 0:n], WAL[:, d, h * 128:h * 128 + 128], AL[:, col:col + n], start=True, stop=True),
                                  bfree[b], ta, t_wal)
                        bias = vec("b_al", 4 * d + h)
                        g0, g1 = LG[:, q, 0, 0:n], LG[:, q, 1, 0:n]
                        ps = B[b][:, 0:n]
                        t1 = AC.do(lambda e: e.activation(g0, ps, ACT.Abs, bias=bias), t, tlg[q], t_vec)
                        t2 = DV.do(lambda e: e.tensor_scalar(g1, ps, bias, 0.0, ALU.add, ALU.min), t1, tlg[q], t_vec)
                        bfree[b] = t2
                        t3 = AC.do(lambda e: e.activation(g0, g0, ACT.Exp, scale=-1.0), t1)
                        t4 = AC.do(lambda e: e.activation(g0, g0, ACT.Ln, bias=ones[:, 0:1]), t3, t_ones)
                        yield
                        t5 = DV.do(lambda e: e.tensor_tensor(g1, g1, g0, ALU.subtract), t4, t2)
                        s, fr = take()
                        o = TMP[:, s, 0:n]
                        if d == 0:
                            t6 = DV.do(lambda e: e.tensor_tensor_scan(o, cmask[:, 0:n], g1, 0.0, ALU.mult, ALU.add), t5, t_cm, fr)
                        else:
                            t6 = DV.do(lambda e: e.tensor_tensor_scan(o[:, ::-1], cmask[:, 0:n], g1[:, ::-1], 0.0, ALU.mult, ALU.add), t5, t_cm, fr)
                        tlg[q] = [t5, t6]
                        store(s, dB[d][h][:, col:col + n], o, f"b{d}", t6)

        mt = {}

        def mods():
            for m in range(16, 48):
                t = dma("aw", aw[:], D["adaT"][m - 16], mt.get("ops"))
                yield
                mt["ops"] = DV.do(lambda e: e.tensor_tensor_reduce(out=aw[:], in0=aw[:], in1=cb[:], scale=1.0, scalar=0.0,
                                                                   op0=ALU.mult, op1=ALU.add, accum_out=MOD[:, m:m + 1]), t, t_cb)
            t = DV.do(lambda e: e.tensor_tensor(MOD[:, 16:48], MOD[:, 16:48], VEC[:, V["b_ada"] + 16:V["b_ada"] + 48], ALU.add), mt["ops"])
            n2 = VEC[:, V["n2"]:V["n2"] + 8]
            mt["gs"] = DV.do(lambda e: e.scalar_tensor_tensor(out=GS[:, 16:24], in0=MOD[:, 32:40], scalar=1.0, in1=n2, op0=ALU.add, op1=ALU.mult), t)

        def side():
            a, b = decays(), mods()
            for _ in range(60):
                next(a, 0)
                next(b, 0)
                yield

        run(beside(projections(), side(), 1))
        run_later()
        barrier(("st",))
        p1.close()
        pc.close()

        p2 = ExitStack()
        S2 = lambda shape, dt, name="t": [alloc(p2, shape, dt, name) for _ in range(2)]
        banks["use"] = [0, 1]
        TB, AB, KB, VB = 2, 3, 4, 5
        OB = [6, 7]
        gb, gk, gq = S2([128, 4, 128], F, "gb"), S2([128, 4, 128], F, "gk"), S2([128, 4, 128], F, "gq")
        gv = S2([128, 1024], F, "gv")
        ee_, ki_, ks_, kT_ = (S2([128, 4, 128], F, "e"), S2([128, 4, 128], F, "ki"), S2([128, 4, 128], F, "ks"), S2([128, 4, 128], F, "kt"))
        att = S2([128, 4, 128], F, "att")
        amask = S2([128, 128], I32, "am")
        SS = S2([128, 4, 256], F, "S")
        EB_ = S2([128, 4, 2], F, "eb")
        EP_ = S2([128, 4], F, "ep")
        t_am = [dma(f"am{d}", amask[d][:], D[f"amask{d}"]) for d in range(2)]
        t_att = [DV.do(lambda e: e.memset(att[d][:], 0.0)) for d in range(2)]
        t_S = [DV.do(lambda e: e.memset(SS[d][:], 0.0)) for d in range(2)]
        g_free = [{}, {}]
        o_tok = {}

        def gla(d, pair, ctx):
            col = pair * 128
            fr = g_free[d]
            b, k, q, v, ee, ki, ks, kT, EB, EP = (x[d] for x in (gb, gk, gq, gv, ee_, ki_, ks_, kT_, EB_, EP_))
            tb = dma(f"gb{d}", b[:], dB[d][:, :, col:col + 128].rearrange("h p t -> p h t"), written[f"b{d}"], fr.get("b"))
            tk = dma(f"gk{d}", k[:], dK[:, :, col:col + 128].rearrange("h p t -> p h t"), written["k"], fr.get("k"))
            tq = None
            if not ctx:
                tq = dma(f"gq{d}", q[:], dQ[:, :, col - TC:col - TC + 128].rearrange("h p t -> p h t"), written["q"], fr.get("q"))
            tv = dma(f"gv{d}", v[:], dV[pair], written["v"], fr.get("v"))
            yield
            first, second = (0, 1) if d == 0 else (1, 0)
            last = (lambda c: 64 * c + 63) if d == 0 else (lambda c: 64 * c)
            f0, s0 = 64 * first, 64 * second
            lastv = b[:, :, last(0):last(0) + 65:64]
            b2 = b[:, :, :].rearrange("p h (c t) -> p h c t", c=2)
            for c in range(2):
                td = DV.do(lambda e: e.tensor_tensor(ks[:, :, 64 * c:64 * c + 64], b[:, :, last(c):last(c) + 1].to_broadcast([128, 4, 64]), b2[:, :, c, :], ALU.subtract), tb, fr.get("ks"))
            te = AC.do(lambda e: e.activation(EB[:, :, :], lastv, ACT.Exp, scale=1 / 16), tb, fr.get("EB"))
            if not ctx:
                t1 = AC.do(lambda e: e.activation(ee[:, :, :], b[:, :, :], ACT.Exp, scale=1 / 16), tb, fr.get("ee"))
                tq1 = DV.do(lambda e: e.tensor_tensor(q[:, :, :], q[:, :, :], ee[:, :, :], ALU.mult), t1, tq)
                t2 = AC.do(lambda e: e.activation(ki[:, :, :], b[:, :, :], ACT.Exp, scale=-1 / 16), tb, fr.get("ki"))
                tki = DV.do(lambda e: e.tensor_tensor(ki[:, :, :], k[:, :, :], ki[:, :, :], ALU.mult), t2, tk)
                fr["ee"] = tq1
            t3 = AC.do(lambda e: e.activation(ks[:, :, :], ks[:, :, :], ACT.Exp, scale=1 / 16), td)
            fr["b"] = [t3, td]
            tks = DV.do(lambda e: e.tensor_tensor(ks[:, :, :], k[:, :, :], ks[:, :, :], ALU.mult), t3, tk)
            fr["k"] = tks
            tp = DV.do(lambda e: e.tensor_tensor(EP[:, :], EB[:, :, 0], EB[:, :, 1], ALU.mult), te, fr.get("EP"))
            yield
            tx1 = tks
            if not ctx:
                for h in range(4):
                    PE.quiet(lambda e: e.matmul(B[AB][:, h * 128:h * 128 + 128], ki[:, h, :], q[:, h, :], start=True, stop=True), tki, tq1, bfree[AB])
                for h in range(4):
                    f = (lambda e: e.matmul(B[KB][f0:f0 + 64, h * 64:h * 64 + 64], ks[:, h, f0:f0 + 64], q[:, h, s0:s0 + 64], start=True, stop=True))
                    if h < 3:
                        PE.quiet(f, tks, bfree[KB])
                    else:
                        ta = PE.do(f)
                fr["ki"] = ta
                tq2 = DV.do(lambda e: e.tensor_tensor(q[:, :, s0:s0 + 64], q[:, :, s0:s0 + 64], EB[:, :, first:first + 1].to_broadcast([128, 4, 64]), ALU.mult), ta)
                tx1 = ta
            tks2 = DV.do(lambda e: e.tensor_tensor(ks[:, :, f0:f0 + 64], ks[:, :, f0:f0 + 64], EB[:, :, second:second + 1].to_broadcast([128, 4, 64]), ALU.mult), tx1, te)
            fr["EB"] = [tks2, tp]
            if not ctx:
                tc = DV.do(lambda e: e.copy_predicated(att[d][:, :, :], amask[d][:].rearrange("p (o t) -> p o t", o=1).to_broadcast([128, 4, 128]),
                                                      B[AB][:, :].rearrange("p (h t) -> p h t", h=4)), ta, t_att[d], t_am[d])
                bfree[AB] = tc
                tc2 = DV.do(lambda e: e.tensor_copy(att[d][f0:f0 + 64, :, s0:s0 + 64], B[KB][f0:f0 + 64, 0:256].rearrange("p (h t) -> p h t", h=4)), tc)
                bfree[KB] = tc2
            yield
            for h in range(4):
                f = (lambda e: e.transpose(B[KB][:, h * 128:h * 128 + 128], ks[:, h, :], ident[:]))
                if h < 3:
                    PE.quiet(f, tks2, bfree[KB])
                else:
                    tt = PE.do(f)
            fr["ks"] = tt
            tkt = AC.do(lambda e: e.activation(kT[:, :, :], B[KB][:, :].rearrange("p (h t) -> p h t", h=4), ACT.Copy), tt, fr.get("kT"))
            bfree[KB] = tkt
            to = None
            if not ctx:
                for h in range(4):
                    bk = OB[h // 2]
                    o = B[bk][:, (h % 2) * 256:(h % 2) * 256 + 256]
                    PE.quiet(lambda e: e.matmul(o, q[:, h, :], SS[d][:, h, :], start=True, stop=False), tq2, t_S[d], bfree[bk])
                    f = (lambda e: e.matmul(o, att[d][:, h, :], v[:, h * 256:h * 256 + 256], start=False, stop=True))
                    if h % 2 == 0:
                        PE.quiet(f, tc2, tv)
                    else:
                        to = PE.do(f, tc2, tv)
                        key = (pair - 2, h // 2)
                        dst = RES[:, pair - 2, h // 2 * 512:h // 2 * 512 + 512]
                        if key not in o_tok:
                            o_tok[key] = AC.do(lambda e: e.activation(dst, B[bk][:, :], ACT.Copy), to)
                        else:
                            o_tok[key] = DV.do(lambda e: e.tensor_tensor(dst, B[bk][:, :], dst, ALU.add), to, o_tok[key])
                        bfree[bk] = o_tok[key]
                t_att[d] = to
                fr["q"] = to
            yield
            for hh in range(2):
                for h in (2 * hh, 2 * hh + 1):
                    f = (lambda e: e.matmul(B[VB][:, (h % 2) * 256:(h % 2) * 256 + 256], kT[:, h, :], v[:, h * 256:h * 256 + 256], start=True, stop=True))
                    if h % 2 == 0:
                        PE.quiet(f, tkt, bfree[VB], tv)
                    else:
                        tkv = PE.do(f)
                for h in (2 * hh, 2 * hh + 1):
                    ts = DV.do(lambda e: e.scalar_tensor_tensor(out=SS[d][:, h, :], in0=SS[d][:, h, :], scalar=EP[:, h:h + 1],
                                                                in1=B[VB][:, (h % 2) * 256:(h % 2) * 256 + 256], op0=ALU.mult, op1=ALU.add),
                               tkv, to, tp, t_S[d])
                bfree[VB] = ts
                if hh == 0:
                    yield
            t_S[d] = ts
            fr["EP"] = ts
            fr["kT"] = tkv
            fr["v"] = tkv

        def direction(d):
            for s in range(10):
                yield from gla(d, s if d == 0 else ((1 - s) if s < 2 else 11 - s), s < 2)

        def in_turn(a, b, lead):
            for _ in range(lead):
                next(a, 0)
                yield
            live = True
            while live:
                live = next(a, 0) is None
                if live:
                    yield
                live2 = next(b, 0) is None
                if live2:
                    yield
                live = live or live2

        def fill(names):
            table = {"v": (dVm, "vm"), "u": (dU, "u"), "r": (dR, "r"), "ga": (dGA, "ga"), "gb": (dGB, "gb")}
            for n in names:
                dst, key = table[n]
                put = put_turned(dst, key, TC, TB) if n == "v" else put_plain(dst, key, TC)
                for m in range(8):
                    yield from project(n, m, False, put)

        run(beside(fill(["v", "u", "r"]), in_turn(direction(0), direction(1), 2), 102 / 48))
        run_later()
        barrier(("st",))
        p2.close()

        p3 = ExitStack()
        S3 = lambda shape, dt, name="t": alloc(p3, shape, dt, name)
        vn = S3([128, 4, 1024], F, "vn")
        lg = S3([128, 2, 1024], F, "lng")
        bs = S3([128, 1024], F, "bs")
        wsp = S3([128, 1024], F, "wsp")
        ld = S3([128, 3, 512], F, "ld")
        st6 = S3([128, 4, 2, 6], F, "st6")
        mv = S3([128, 4, 2], F, "mv")
        ss = S3([128, 32], F, "ss")
        t_lg = dma("lg", lg[:], D["lnvb"])
        t_bs = dma("bs", bs[:], D["bspb"])
        t_wsp = dma("wsp", wsp[:], D["wspT"])

        def mlp():
            ldf = [None] * 3
            j = 0
            tvf = [None] * 4
            tms = None
            for half in range(2):
                tn = []
                tld = []
                for c in range(4):
                    tld.append(dma(f"vn{c}", vn[:, c, :], dVm[4 * half + c], written["vm"], tvf[c]))
                yield
                for c in range(4):
                    x = vn[:, c, :]
                    t = AC.do(lambda e: e.activation(x, x, ACT.Gelu), tld[c])
                    for s in range(2):
                        t1 = DV.do(lambda e: e.bn_stats(st6[:, c, s, :], x[:, s * 512:s * 512 + 512]), t, tms)
                    tms1 = DV.do(lambda e: e.bn_aggr(mv[:, c, :], st6[:, c, :, :].rearrange("p a b -> p (a b)")), t1)
                    if c % 2:
                        yield
                t3 = AC.do(lambda e: e.activation(mv[:, :, 1], mv[:, :, 1], ACT.Sqrt, bias=eps[:, 0:1]), tms1)
                tms = DV.do(lambda e: e.reciprocal(mv[:, :, 1], mv[:, :, 1]), t3)
                for c in range(4):
                    x = vn[:, c, :]
                    t5 = DV.do(lambda e: e.tensor_scalar(x, x, mv[:, c, 0:1], mv[:, c, 1:2], ALU.subtract, ALU.mult), tms)
                    t6 = DV.do(lambda e: e.tensor_tensor(x, x, lg[:, 0, :], ALU.mult), t5, t_lg)
                    t7 = DV.do(lambda e: e.tensor_tensor(x, x, lg[:, 1, :], ALU.add), t6)
                    tn.append(t7)
                    yield
                tms = t7
                for g in range(8):
                    q = j % 3
                    j += 1
                    tu = dma(f"ld{q}", ld[:, q, :], dU[g][:, half * 512:half * 512 + 512], written["u"], ldf[q])
                    bk = [3, 4][g % 2]
                    for c in range(4):
                        f = (lambda e: e.matmul(B[bk][:, c * 128:c * 128 + 128], vn[:, c, g * 128:g * 128 + 128], wsp[:, g * 128:g * 128 + 128], start=True, stop=True))
                        if c < 3:
                            PE.quiet(f, tn[c], t_wsp, bfree[bk])
                        else:
                            t = PE.do(f, tn[c])
                    tg = AC.do(lambda e: e.activation(ld[:, q, :], ld[:, q, :], ACT.Gelu), tu)
                    s, fr = take()
                    o = TMP[:, s, :]
                    bsg = bs[:, g * 128:g * 128 + 128].rearrange("p (o t) -> p o t", o=1).to_broadcast([128, 4, 128])
                    t1 = DV.do(lambda e: e.tensor_tensor(o.rearrange("p (c t) -> p c t", c=4), B[bk][:, :].rearrange("p (c t) -> p c t", c=4), bsg, ALU.add), t, t_bs, fr)
                    bfree[bk] = t1
                    t2 = DV.do(lambda e: e.tensor_tensor(o, o, ld[:, q, :], ALU.mult), t1, tg)
                    ldf[q] = t2
                    store(s, dA[g][:, half * 512:half * 512 + 512], o, "a", t2)
                    yield
                tvf = [t] * 4

            for p8 in range(8):
                for h in range(4):
                    o = RES[:, p8, h * 256:h * 256 + 256]
                    c = 4 * p8 + h
                    q = h % 3
                    t1 = AC.do(lambda e: e.activation(ld[:, q, 0:256], o, ACT.Square, accum_out=ss[:, c:c + 1]), o_tok[(p8, 0)], o_tok[(p8, 1)], ldf[q])
                    ldf[q] = t1
                if p8 % 2:
                    yield
            t2 = AC.do(lambda e: e.activation(ss[:, :], ss[:, :], ACT.Sqrt, bias=eps[:, 0:1], scale=1 / 256), t1)
            t3 = DV.do(lambda e: e.reciprocal(ss[:, :], ss[:, :]), t2)
            tr = []
            for p8 in range(8):
                for h in range(4):
                    o = RES[:, p8, h * 256:h * 256 + 256]
                    c = 4 * p8 + h
                    t4 = DV.do(lambda e: e.tensor_scalar(o, o, ss[:, c:c + 1], None, ALU.mult), t3)
                tr.append(t4)
                if p8 % 2:
                    yield
            for half in range(2):
                for m in range(8):
                    q = j % 3
                    j += 1
                    tu = dma(f"ld{q}", ld[:, q, :], dR[m][:, half * 512:half * 512 + 512], written["r"], ldf[q])
                    bk = [3, 4][m % 2]
                    for c in range(4):
                        p8 = 4 * half + c
                        f = (lambda e: e.transpose(B[bk][:, c * 128:c * 128 + 128], RES[:, p8, m * 128:m * 128 + 128], ident[:]))
                        if c < 3:
                            PE.quiet(f, tr[p8], bfree[bk])
                        else:
                            t = PE.do(f, tr[p8])
                    tg = AC.do(lambda e: e.activation(ld[:, q, :], ld[:, q, :], ACT.Silu), tu)
                    s, fr = take()
                    o = TMP[:, s, :]
                    t1 = DV.do(lambda e: e.scalar_tensor_tensor(out=o, in0=B[bk][:, :], scalar=vec("gn", m), in1=ld[:, q, :], op0=ALU.mult, op1=ALU.mult), t, tg, fr)
                    bfree[bk] = t1
                    ldf[q] = t1
                    store(s, dBo[m][:, half * 512:half * 512 + 512], o, "bo", t1)
                    yield
            mt["oT"] = t

        run(beside(fill(["ga", "gb"]), mlp(), 56 / 30))
        run_later()
        barrier(("st",))
        p3.close()

        p4 = ExitStack()
        NQ = 4
        lq = alloc(p4, [128, NQ, 512], F, "lq")
        FH = alloc(p4, [128, 4, T], R, "fh")
        FL = alloc(p4, [128, 4, T], R, "fl")
        lqs = {"i": 0, "free": [None] * NQ}

        def fetch(src, name, *tokens):
            q = lqs["i"] % NQ
            lqs["i"] += 1
            t = dma(f"lq{q}", lq[:, q, :], src, written[name] if name else None, lqs["free"][q], *tokens)
            return q, t

        def load_split(src, name, half, free):
            outs = []
            for k in range(8):
                s, fr = take()
                c = 512 * half
                t = dma(f"st{s}", TMP[:, s, :], src[k][:, c:c + 512], written[name], fr)
                o = split_to(XH[:, k, c:c + 512], XL[:, k, c:c + 512], TMP[:, s, :], t, free)
                ring["free"][s] = o
                outs.append(o)
            xtok[half] = outs

        def pairs(name, after, then=None):
            for p in range(4):
                ws = [wget(name, 2 * p), wget(name, 2 * p + 1)]
                for h in range(2):
                    r = products(ws, h)
                    for x, (b, t) in enumerate(r):
                        after(2 * p + x, h, b, t)
                    if p == 3 and then:
                        then(h, t)
                for i in ws:
                    wdone(i, t)

        banks["use"] = list(range(8))
        for h in range(2):
            load_split(dA, "a", h, pe_now())

        def gated(gate, key, add, toks):
            def after(m, h, b, t):
                q, tl = fetch(gate[m][:, h * 512:h * 512 + 512], key)
                y = RES[:, m, h * 512:h * 512 + 512]
                g = lq[:, q, :]
                ts = AC.do(lambda e: e.activation(g, g, ACT.Sigmoid), tl)
                if not add:
                    t1 = DV.do(lambda e: e.tensor_tensor(y, B[b][:, :], g, ALU.mult), t, ts, mt["oT"])
                    bfree[b] = t1
                else:
                    t0 = DV.do(lambda e: e.tensor_tensor(g, B[b][:, :], g, ALU.mult), t, ts)
                    bfree[b] = t0
                    t1 = DV.do(lambda e: e.tensor_tensor(y, y, g, ALU.add), t0)
                lqs["free"][q] = t1
                toks[(m, h)] = t1
            return after

        pairs("wa", gated(dGA, "ga", False, {}), lambda h, t: load_split(dBo, "bo", h, t))
        ty = {}
        ygone = {}

        def y_split(h, t):
            c = 512 * h
            outs = []
            for k in range(8):
                outs.append(split_to(XH[:, k, c:c + 512], XL[:, k, c:c + 512], RES[:, k, c:c + 512], ty[(k, h)], t))
                ygone[(k, h)] = outs[-1]
            xtok[h] = outs

        pairs("wb", gated(dGB, "gb", True, ty), y_split)

        def residual(gain, xsrc, key, tr, tacc):
            def after(m, h, b, t):
                q, tl = fetch(xsrc[m][:, h * 512:h * 512 + 512], key)
                y = RES[:, m, h * 512:h * 512 + 512]
                t1 = DV.do(lambda e: e.scalar_tensor_tensor(out=y, in0=B[b][:, :], scalar=gain(m), in1=lq[:, q, :], op0=ALU.mult, op1=ALU.add), t, tl, ygone.get((m, h)))
                bfree[b] = t1
                lqs["free"][q] = t1
                tr[(m, h)] = t1
                tacc[h] = square_sum(y, 512 * h, 512, m == 0, t1, tacc[h])
            return after

        def normed(scale, shift, tr, tacc):
            def then(h, t):
                bt = rms_sum(512 * h, 512, tacc[h]) if h else None
                if h == 0:
                    pend["mid"] = lambda: pend.update(bt=rms_sum(0, 512, tacc[0]), done=None)
                    pend["fin"] = lambda: finish(0, pend["bt"], t)
                else:
                    finish(1, bt, t)

            def finish(h, bt, t):
                trb = rms_scale(512 * h, 512, bt, None)
                xtok[h] = norm_tiles(RES, 512 * h, 512, trb, scale, shift, XH, XL, [tr[(k, h)] for k in range(8)], t)
            return then

        pend = {}

        def pairs_normed(name, after, scale, shift, tr, tacc):
            for p in range(4):
                ws = [wget(name, 2 * p), wget(name, 2 * p + 1)]
                for h in range(2):
                    mid = None
                    if p == 3 and h == 1:
                        mid = lambda: pend.update(bt=rms_sum(0, 512, tacc[0]))
                    r = products(ws, h, mid=mid)
                    if mid:
                        first_half(scale, shift, tr, t0)
                    for x, (b, t) in enumerate(r):
                        after(2 * p + x, h, b, t)
                    if h == 0:
                        t0 = t
                for i in ws:
                    wdone(i, t)
            second_half(scale, shift, tr, tacc, t)

        def first_half(scale, shift, tr, t):
            trb = rms_scale(0, 512, pend["bt"], None)
            xtok[0] = norm_tiles(RES, 0, 512, trb, scale, shift, XH, XL, [tr[(k, 0)] for k in range(8)], t)

        def second_half(scale, shift, tr, tacc, t):
            trb = rms_scale(512, 512, rms_sum(512, 512, tacc[1]), None)
            xtok[1] = norm_tiles(RES, 512, 512, trb, scale, shift, XH, XL, [tr[(k, 1)] for k in range(8)], t)

        tr, tacc = {}, [None, None]
        pairs_normed("wo", residual(lambda m: MOD[:, 16 + m:17 + m], D["xT"], None, tr, tacc),
                     lambda k: GS[:, 16 + k:17 + k], lambda k: MOD[:, 24 + k:25 + k], tr, tacc)

        def ffn(one, two, gate_first, gain, tr, tacc, mid_last):
            ffree = [None] * 4
            ftok = {}

            def second(g, last):
                ws = [wget(two, t) for t in g]
                for h in range(2):
                    for m in range(8):
                        b = bank()
                        o = B[b][:, :]
                        for x, (i, tt) in enumerate(zip(ws, g)):
                            s, w = tt % 4, i % NW
                            wh, wl = WH[:, w, m * 128:m * 128 + 128], WL[:, w, m * 128:m * 128 + 128]
                            xh, xl = FH[:, s, h * 512:h * 512 + 512], FL[:, s, h * 512:h * 512 + 512]
                            PE.quiet(lambda e: e.matmul(o, wh, xh, start=(x == 0), stop=False), bfree[b], wsplit[i], ftok[(tt, h)])
                            PE.quiet(lambda e: e.matmul(o, wh, xl, start=False, stop=False))
                            f = (lambda e: e.matmul(o, wl, xh, start=False, stop=(x == 1)))
                            if x < 1:
                                PE.quiet(f)
                            else:
                                t = PE.do(f)
                        y = RES[:, m, h * 512:h * 512 + 512]
                        tr[(m, h)] = DV.do(lambda e: e.scalar_tensor_tensor(out=y, in0=B[b][:, :], scalar=gain(m), in1=y, op0=ALU.mult, op1=ALU.add), t, tr.get((m, h)))
                        bfree[b] = tr[(m, h)]
                        if last:
                            tacc[h] = square_sum(y, 512 * h, 512, m == 0, tr[(m, h)], tacc[h])
                            if h == 1 and m == 2:
                                mid_last()
                for i in ws:
                    wdone(i, t)
                for tt in g:
                    ffree[tt % 4] = t

            for gi, g in enumerate(GROUPS):
                for tt in g:
                    ws = [wget(one, tt), wget(one, NF + tt)]
                    s = tt % 4
                    for h in range(2):
                        r = products(ws, h)
                        (bg, tg), (bu, tu) = r if gate_first else r[::-1]
                        q, fr = take()
                        y = TMP[:, q, :]
                        t2 = AC.do(lambda e: e.activation(y, B[bg][:, :], ACT.Silu), tg, fr)
                        t3 = DV.do(lambda e: e.tensor_tensor(y, B[bu][:, :], y, ALU.mult), tu, t2)
                        bfree[bg], bfree[bu] = t2, t3
                        ftok[(tt, h)] = split_to(FH[:, s, h * 512:h * 512 + 512], FL[:, s, h * 512:h * 512 + 512], y, t3, ffree[s])
                        ring["free"][q] = ftok[(tt, h)]
                    for i in ws:
                        wdone(i, r[1][1])
                    ffn_x["last"] = r[1][1]
                if gi:
                    second(GROUPS[gi - 1], False)
            second(GROUPS[-1], True)

        ffn_x = {}
        dX = scratch("x2", [8, 128, T])
        xst = {}
        tacc = [None, None]
        tfin = {}

        def between(h):
            c = 512 * h
            trb = rms_scale(c, 512, rms_sum(c, 512, tacc[h]), None)
            ta = None
            for k in range(8):
                x = RES[:, k, c:c + 512]
                t = DV.do(lambda e: e.scalar_tensor_tensor(out=x, in0=x, scalar=vec("fin1", k), in1=RB[:, c:c + 512], op0=ALU.mult, op1=ALU.mult), trb)
                tfin[(k, h)] = t
                ta = square_sum(x, c, 512, k == 0, t, ta or trb)
                xst[(k, h)] = dma(f"x{k}", dX[k][:, c:c + 512], x, t)
                written.setdefault("x2", []).append(xst[(k, h)])
            return ta

        def again(h, ta, free):
            c = 512 * h
            trb = rms_scale(c, 512, rms_sum(c, 512, ta), None)
            xtok[h] = norm_tiles(RES, c, 512, trb, lambda k: vec("nm2", k), None, XH, XL, [tfin[(k, h)] for k in range(8)], free)

        def mid1():
            ta = between(0)
            pend["again"] = lambda: again(0, ta, ffn_x["last"])

        ffn("f1", "f2", False, lambda m: MOD[:, 40 + m:41 + m], tr, tacc, mid1)
        pend["again"]()
        again(1, between(1), ffn_x["last"])
        wsplit_to(state["next"] + 2)
        barrier(("x",))
        p4.close()

        dU2 = scratch("u2", [8, 128, T])
        dG2 = scratch("g2", [8, 128, T])
        dZ0 = scratch("z0", [8, 128, T])
        dZ1 = scratch("z1", [8, 128, T])
        dM = scratch("mg", [8, 128, T])
        dQ2 = scratch("q2", [8, 128, T])
        dK2 = scratch("k2", [2, 128, T])
        dV2 = scratch("v2", [8, 128, 256])
        dY = scratch("y", [8, 128, T])

        p5 = ExitStack()
        S5 = lambda shape, dt, name="t": alloc(p5, shape, dt, name)
        UC, HH, SQ = RES[:, 1, :], RES[:, 6, :], RES[:, 7, :]
        Rg = [RES[:, 2, :], RES[:, 3, :]]
        Ig = [RES[:, 4, :], RES[:, 5, :]]
        UP = S5([128, T + 3], F, "up")
        UH = S5([128, T], R, "uh")
        UL = S5([128, T], R, "ul")
        GL = S5([128, T], F, "gl")
        Z0 = S5([128, T], F, "z0")
        BD = S5([128, 512], F, "bd")
        BH = S5([128, 512], R, "bh")
        BL = S5([128, 512], R, "bl")
        SPL = S5([128, 16], F, "spl")
        s12 = S5([128, 2, 16], F, "s12")
        tm = S5([128, 4, T], F, "tm")
        lam = VEC[:, V["lam"]:V["lam"] + 16]
        s1, s2 = s12[:, 0, :], s12[:, 1, :]
        t1 = AC.do(lambda e: e.activation(s1, lam, ACT.Abs))
        t1 = AC.do(lambda e: e.activation(s1, s1, ACT.Exp, scale=-1.0), t1)
        t1 = AC.do(lambda e: e.activation(s1, s1, ACT.Ln, bias=ones[:, 0:1]), t1)
        t2 = DV.do(lambda e: e.tensor_scalar(s2, lam, -1.0, 0.0, ALU.mult, ALU.max))
        t2 = DV.do(lambda e: e.tensor_tensor(s2, s2, s1, ALU.add), t1, t2)
        t_spl = DV.do(lambda e: e.tensor_scalar(SPL[:, :], s2, -8.0, None, ALU.mult), t2)
        t_up = DV.do(lambda e: e.memset(UP[:], 0.0))
        banks["use"] = [0, 1]
        fr = {}
        xs = list(xst.values())
        for k in ("UC", "HH", "SQ", ("G", 0), ("G", 1)):
            fr[k] = xs
        mid = {"n": 0}

        def lru_tile(m):
            tu = dma("up", UP[:, 2:T + 2], dU2[m], written["u2"], fr.get("UP"), t_up)
            tb = dma("bd", BD[:], D["lruw"][m], fr.get("BD"))
            tg = dma("gl", GL[:], dG2[m], written["g2"], fr.get("GL"))
            tz = dma("z0", Z0[:], dZ0[m], written["z0"], fr.get("GL"))
            yield
            tbs = split_to(BH[:, :], BL[:, :], BD[:, :], tb, fr.get("BH"))
            fr["BD"] = tbs
            t = DV.do(lambda e: e.tensor_scalar(UC, UP[:, 0:T], vec("cw", 4 * m), None, ALU.mult), tu, fr.get("UC"))
            for c in range(1, 4):
                t = DV.do(lambda e: e.scalar_tensor_tensor(out=UC, in0=UP[:, c:c + T], scalar=vec("cw", 4 * m + c), in1=UC, op0=ALU.mult, op1=ALU.add), t)
                if c == 2:
                    yield
            fr["UP"] = t
            tuc = DV.do(lambda e: e.tensor_scalar(UC, UC, vec("cb", m), None, ALU.add), t)
            tsp = split_to(UH[:, :], UL[:, :], UC, tuc, fr.get("UH"))
            yield
            yield
            gt = {}
            tz = AC.do(lambda e: e.activation(Z0[:, :], Z0[:, :], ACT.Sigmoid, bias=vec("bg", m)), tz)
            for d in range(2):
                for w in range(2):
                    for h in range(2):
                        b = 4 + mid["n"] % 4
                        mid["n"] += 1
                        c = (2 * d + w) * 128
                        o = B[b][:, :]
                        xh, xl = UH[:, h * 512:h * 512 + 512], UL[:, h * 512:h * 512 + 512]
                        PE.quiet(lambda e: e.matmul(o, BH[:, c:c + 128], xh, start=True, stop=False), bfree[b], tsp, tbs)
                        PE.quiet(lambda e: e.matmul(o, BH[:, c:c + 128], xl, start=False, stop=False))
                        t = PE.do(lambda e: e.matmul(o, BL[:, c:c + 128], xh, start=False, stop=True))
                        dst = (Rg if w == 0 else Ig)[d][:, h * 512:h * 512 + 512]
                        bias = vec("lba" if w == 0 else "lbx", 8 * d + m)
                        gt[(d, w, h)] = AC.do(lambda e: e.activation(dst, o, ACT.Sigmoid, bias=bias), t, fr.get(("G", d)))
                        bfree[b] = gt[(d, w, h)]
                yield
            fr["UH"] = t
            fr["BH"] = t
            tt, ta, ti = {}, {}, {}
            for d in range(2):
                r, w0, w1 = Rg[d], tm[:, 2 * d, :], tm[:, 2 * d + 1, :]
                tla = DV.do(lambda e: e.tensor_scalar(r, r, SPL[:, 8 * d + m:8 * d + m + 1], None, ALU.mult), gt[(d, 0, 0)], gt[(d, 0, 1)], t_spl)
                tt[d] = AC.do(lambda e: e.activation(w0, r, ACT.Tanh, scale=-0.5), tla, fr.get(("tm", d)))
                ta[d] = AC.do(lambda e: e.activation(r, r, ACT.Exp), tt[d])
            for d in range(2):
                i, w1 = Ig[d], tm[:, 2 * d + 1, :]
                ti[d] = DV.do(lambda e: e.tensor_tensor(i, i, UC, ALU.mult), gt[(d, 1, 0)], gt[(d, 1, 1)], tuc)
            fr["UC"] = ti[1]
            yield
            ts, tin = {}, {}
            for d in range(2):
                w0 = tm[:, 2 * d, :]
                ts[d] = AC.do(lambda e: e.activation(w0, w0, ACT.Sqrt), tt[d])
            for d in range(2):
                r, i, w0, w1 = Rg[d], Ig[d], tm[:, 2 * d, :], tm[:, 2 * d + 1, :]
                tb3 = DV.do(lambda e: e.scalar_tensor_tensor(out=w1, in0=r, scalar=1.0, in1=w0, op0=ALU.add, op1=ALU.mult), ta[d], ts[d], fr.get(("tm", d)))
                tin[d] = DV.do(lambda e: e.tensor_tensor(i, i, w1, ALU.mult), ti[d], tb3)
                fr[("tm", d)] = tin[d]
                if d == 0:
                    yield
            tg = AC.do(lambda e: e.activation(GL[:, :], GL[:, :], ACT.Gelu_apprx_tanh), tg)
            th = DV.do(lambda e: e.tensor_tensor_scan(HH, Rg[0], Ig[0], 0.0, ALU.mult, ALU.add), tin[0], fr.get("HH"))
            fr[("G", 0)] = th
            yield
            th2 = DV.do(lambda e: e.tensor_tensor_scan(SQ[:, ::-1], Rg[1][:, ::-1], Ig[1][:, ::-1], 0.0, ALU.mult, ALU.add), tin[1], fr.get("SQ"))
            fr[("G", 1)] = th2
            t = DV.do(lambda e: e.tensor_tensor(HH, HH, SQ, ALU.add), th, th2)
            fr["SQ"] = t
            t = DV.do(lambda e: e.tensor_tensor(HH, HH, GL[:, :], ALU.mult), t, tg)
            t = DV.do(lambda e: e.tensor_tensor(HH, HH, Z0[:, :], ALU.mult), t, tz)
            fr["GL"] = t
            t = dma("mg", dM[m], HH, t)
            fr["HH"] = t
            written.setdefault("mg", []).append(t)
            yield

        def lru():
            for m in range(8):
                yield from lru_tile(m)

        def fill_pair(a, b, ka, kb, pa, pb):
            ws = [wget(ka, a), wget(kb, b)]
            for h in range(2):
                r = products(ws, h)
                pa(a, TC + 512 * h, 512, B[r[0][0]][:, :], *r[0])
                pb(b, TC + 512 * h, 512, B[r[1][0]][:, :], *r[1])
            for i in ws:
                wdone(i, r[1][1])

        pu, pg, pz0 = put_plain(dU2, "u2", TC), put_plain(dG2, "g2", TC), put_plain(dZ0, "z0", TC)
        banks["use"] = [0, 1, 2, 3]
        fill_pair(0, 0, "u2", "g2", pu, pg)
        run(project("z0", 0, False, pz0))
        banks["use"] = [0, 1]

        def fill_b():
            for m in range(1, 8):
                yield from project("u2", m, False, pu)
                yield from project("g2", m, False, pg)
                yield from project("z0", m, False, pz0)
            for m in range(2):
                yield from project("k2", m, False, put_plain(dK2, "k2", TC))
            for m in range(2):
                yield from project("v2", m, False, put_turned(dV2, "v2", TC, 2))
            for m in range(8):
                yield from project("q2", m, False, put_plain(dQ2, "q2", TC, scale=0.125))

        vf["free"] = [xtok[0][7] + xtok[1][7]] * 4
        run(beside(fill_b(), lru(), 80 / 64))
        run_later()
        barrier(("st",))
        p5.close()

        p6 = ExitStack()
        S6 = lambda shape, dt, name="t": alloc(p6, shape, dt, name)
        K1 = S6([128, 2, T], R, "k1")
        K2 = S6([128, 2, T], R, "k2")
        QS = [S6([128, 8, 128], R, "qs") for _ in range(2)]
        PT = S6([128, 8, 3, 128], F, "pt")
        PR = [RES[:, 0:3, :].rearrange("p a t -> p (a t)").rearrange("p (h s) -> p h s", h=8), S6([128, 8, 384], F, "pr")]
        Vt = RES[:, 3:6, :].rearrange("p a t -> p (a t)").rearrange("p (c q f) -> p c q f", c=8, q=2)
        QD = [ACC[:, :].rearrange("p (h t) -> p h t", h=8), RB[:, :].rearrange("p (h t) -> p h t", h=8)]
        KD = RES[:, 7, :]
        ZB = RES[:, 6, 0:512].rearrange("p (a t) -> p a t", a=4)
        MB = RES[:, 6, 512:1024].rearrange("p (a t) -> p a t", a=4)
        ADD = S6([128, 384], F, "ad")
        mx_ = [S6([128, 8], F, "mx") for _ in range(2)]
        es_ = [S6([128, 8], F, "es") for _ in range(2)]
        dn_ = [S6([128, 8], F, "dn") for _ in range(2)]
        t_v0 = DV.do(lambda e: e.memset(RES[:, 3:6, :], 0.0))
        t_k0 = DV.do(lambda e: e.memset(K2[64:128, :, :].bitcast(F), 0.0))
        t_ad = dma("adb", ADD[:], D["alibi"])
        tV = []
        for q in range(2):
            for x in range(2):
                tV.append(dma(f"vt{q}{x}", Vt[:, :, q, 128 * x:128 * x + 64], dV2[:, :, 128 * q + 64 * x:128 * q + 64 * x + 64].rearrange("c p f -> p c f"), written["v2"], t_v0))
        banks["use"] = [0, 1]
        slopes = [float(2.0 ** (-8.0 * (h + 1) / 16)) for h in range(16)]
        af = [{}, {}]
        one = {}

        def keys(pair):
            tk = one.get("kd")
            toks = []
            for x in range(2):
                src = dK2[pair][64 * x:64 * x + 64, :]
                t1 = dma("kd0", KD[0:64, :], src, written["k2"], tk)
                t2 = dma("kd1", KD[64:128, :], src, tk)
                hi = K1[:, x, :]
                t3 = AC.do(lambda e: e.activation(hi, KD, ACT.Copy), t1, t2, one.get("scores"))
                t4 = DV.do(lambda e: e.tensor_tensor(K2[0:64, x, :], KD[0:64, :], K1[0:64, x, :].bitcast(F), ALU.subtract), t3, one.get("scores"))
                tk = [t3, t4]
                toks += tk
            one["kd"] = tk
            one["K"] = toks + [t_k0]

        def attend(pair, blk, z):
            f = af[z]
            mx, es, dn, P, Q, qd = mx_[z], es_[z], dn_[z], PR[z], QS[z], QD[z]
            c0 = blk * 128
            tiles = slice(4 * pair, 4 * pair + 4)
            tq = []
            for kv in range(2):
                src = dQ2[tiles, 64 * kv:64 * kv + 64, c0:c0 + 128].rearrange("a p t -> p a t")
                for y in range(2):
                    tq.append(dma(f"qd{z}{kv}{y}", qd[64 * y:64 * y + 64, 4 * kv:4 * kv + 4, :], src, written["q2"], f.get("qd")))
            k0, k1 = max(0, blk - 1), min(8, blk + 2)
            n = (k1 - k0) * 128
            a0 = (k0 - blk + 1) * 128
            yield
            t1 = AC.do(lambda e: e.activation(Q[:, :, :], qd, ACT.Copy), tq, f.get("Q"))
            t2 = DV.do(lambda e: e.tensor_tensor(Q[64:128, :, :], qd[64:128, :, :], Q[64:128, :, :].bitcast(F), ALU.subtract), t1)
            f["qd"] = [t1, t2]
            yield
            tx_ = []
            for x in range(8):
                kv, a = x // 4, x % 4
                b = 3 + x % 2
                head = 4 * (2 * pair + kv) + a
                o = B[b][:, 0:n]
                PE.quiet(lambda e: e.matmul(o, Q[:, x, :], K1[:, kv, k0 * 128:k0 * 128 + n], start=True, stop=False), bfree[b], t2, one["K"])
                t = PE.do(lambda e: e.matmul(o, Q[:, x, :], K2[:, kv, k0 * 128:k0 * 128 + n], start=False, stop=True))
                t1 = DV.do(lambda e: e.scalar_tensor_tensor(out=P[:, x, 0:n], in0=ADD[:, a0:a0 + n], scalar=-slopes[head], in1=o, op0=ALU.mult, op1=ALU.add),
                           t, t_ad, f.get("P"))
                bfree[b] = t1
                if x == 3:
                    yield
            f["Q"] = t
            one["scores"] = t
            sink = VEC[:, V["sink"] + 8 * pair:V["sink"] + 8 * pair + 8]
            t2 = DV.do(lambda e: e.tensor_reduce(mx[:, :], P[:, :, 0:n], AX.X, ALU.max), t1, f.get("mx"))
            t3 = DV.do(lambda e: e.tensor_tensor(mx[:, :], mx[:, :], sink, ALU.max), t2)
            t4 = DV.do(lambda e: e.tensor_tensor(es[:, :], sink, mx[:, :], ALU.subtract), t3, f.get("es"))
            t5 = DV.do(lambda e: e.tensor_scalar(mx[:, :], mx[:, :], -1.0, None, ALU.mult), t4)
            yield
            t6 = AC.do(lambda e: e.activation(es[:, :], es[:, :], ACT.Exp), t4)
            for x in range(8):
                t7 = AC.do(lambda e: e.activation(P[:, x, 0:n], P[:, x, 0:n], ACT.Exp, bias=mx[:, x:x + 1], accum_out=dn[:, x:x + 1]), t5, f.get("dn"))
            f["mx"] = t7
            yield
            t8 = DV.do(lambda e: e.tensor_tensor(dn[:, :], dn[:, :], es[:, :], ALU.add), t6, t7)
            f["es"] = t8
            t9 = DV.do(lambda e: e.reciprocal(dn[:, :], dn[:, :]), t8)
            tn = []
            for x in range(8):
                tn.append(DV.do(lambda e: e.tensor_scalar(P[:, x, 0:n], P[:, x, 0:n], dn[:, x:x + 1], None, ALU.mult), t9))
            f["dn"] = tn[-1]
            yield
            tpt = []
            for x in range(8):
                b = 5 + x % 2
                for c in range(n // 128):
                    g = (lambda e: e.transpose(B[b][:, c * 128:c * 128 + 128], P[:, x, c * 128:c * 128 + 128], ident[:]))
                    if c < n // 128 - 1:
                        PE.quiet(g, tn[x], bfree[b])
                    else:
                        t = PE.do(g, tn[x], bfree[b])
                dst = PT[:, x, 0:n // 128, :]
                src = B[b][:, 0:n].rearrange("p (c t) -> p c t", t=128)
                if x % 4 == 3:
                    tc = DV.do(lambda e: e.tensor_copy(dst, src), t, one.get("pt"))
                else:
                    tc = AC.do(lambda e: e.activation(dst, src, ACT.Copy), t, one.get("pt"))
                bfree[b] = tc
                tpt.append(tc)
                if x == 3:
                    yield
            f["P"] = t
            tz = dma("zb", ZB, dZ1[tiles, :, c0:c0 + 128].rearrange("a p t -> p a t"), written["z1"], one.get("z"))
            tm_ = dma("mb", MB, dM[tiles, :, c0:c0 + 128].rearrange("a p t -> p a t"), written["mg"], one.get("z"))
            yield
            mms = [(kv, c) for kv in range(2) for c in range(n // 128)]
            o = B[7][:, :].rearrange("p (a t) -> p a t", a=4)
            for x, (kv, c) in enumerate(mms):
                g = (lambda e: e.matmul(o, Vt[:, k0 + c, pair, 64 * kv:64 * kv + 128], PT[:, 4 * kv:4 * kv + 4, c, :], start=(x == 0), stop=(x == len(mms) - 1)))
                if x < len(mms) - 1:
                    PE.quiet(g, tpt, tV, bfree[7])
                else:
                    t = PE.do(g)
            one["pt"] = t
            tz = [AC.do(lambda e: e.activation(ZB[:, a, :], ZB[:, a, :], ACT.Sigmoid, bias=vec("bg", 8 + 4 * pair + a)), tz) for a in range(4)]
            t1 = DV.do(lambda e: e.tensor_tensor(ZB, o, ZB, ALU.mult), t, tz)
            bfree[7] = t1
            s, fs = take()
            so = TMP[:, s, :].rearrange("p (a t) -> p a t", a=4)
            t2 = DV.do(lambda e: e.tensor_tensor(so, ZB, MB, ALU.add), t1, tm_, fs)
            one["z"] = t2
            store(s, dY[tiles, :, c0:c0 + 128].rearrange("a p t -> p a t"), so, "y", t2)
            yield

        def attend_line(z):
            for pair in range(2):
                if z == 0:
                    keys(pair)
                for blk in range(z, 8, 2):
                    yield from attend(pair, blk, z)

        def fill_c():
            for m in range(8):
                yield from project("z1", m, False, put_plain(dZ1, "z1", TC))

        fc = fill_c()
        for _ in range(8):
            next(fc)
        run(beside(fc, in_turn(attend_line(0), attend_line(1), 5), 10))
        run_later()
        barrier()
        p6.close()

        p4 = ExitStack()
        lq = alloc(p4, [128, NQ, 512], F, "lq")
        FH = alloc(p4, [128, 4, T], R, "fh")
        FL = alloc(p4, [128, 4, T], R, "fl")
        lqs["free"] = [None] * NQ
        banks["use"] = list(range(8))
        for h in range(2):
            load_split(dY, "y", h, pe_now())
        ygone.clear()
        tr, tacc = {}, [None, None]
        pairs_normed("wo2", residual(lambda m: ones[:, 0:1], dX, "x2", tr, tacc), lambda k: vec("nf2", k), None, tr, tacc)
        tacc = [None, None]

        def last_norm(h):
            c = 512 * h
            trb = rms_scale(c, 512, rms_sum(c, 512, tacc[h]), None)
            for k in range(8):
                x = RES[:, k, c:c + 512]
                t = DV.do(lambda e: e.scalar_tensor_tensor(out=x, in0=x, scalar=vec("nfin", k), in1=RB[:, c:c + 512], op0=ALU.mult, op1=ALU.mult), trb)
                dma(f"x{k}", out[k][:, c:c + 512], x, t)

        ffn("f12", "f22", True, lambda m: ones[:, 0:1], tr, tacc, lambda: last_norm(0))
        last_norm(1)
        assert state["next"] == len(order)
        SP.wait([(k, v) for k, v in dma.n.items()])
        p4.close()


VECTORS = [("b_ada", 48), ("n1", 8), ("n2", 8), ("b_al", 8), ("gn", 8), ("nm2", 8), ("lam", 16), ("lba", 16), ("lbx", 16),
           ("cw", 32), ("cb", 8), ("bg", 16), ("sink", 16), ("nf2", 8), ("nfin", 8), ("fin1", 8)]
assert sum(n for _, n in VECTORS) <= 240


def layout(x, c, ctx, c_ctx, w_ada, b_ada, norm1_g, w_in, ln_v_g, ln_v_b, w_spatial, b_spatial,
           w_alpha_f, b_alpha_f, w_alpha_b, b_alpha_b, gla_norm_g, w_branch_a, w_branch_b, w_out,
           norm2_g, w_ffn_in, w_ffn_out, final_norm_g, norm_mix_g_2, w_in_2, b_gate_2, conv_w_2,
           conv_b_2, lru_lambda_2, lru_wa_2, lru_ba_2, lru_wx_2, lru_bx_2, attn_sink_2, w_out_2,
           norm_ffn_g_2, w_ffn_in_2, w_ffn_out_2, norm_final_g_2):
    def cols(v):
        return np.asarray(v).reshape(-1, 128).T

    def tiles(w, width=128):
        k, m = w.shape
        return np.ascontiguousarray(w.reshape(k // 128, 128, m // width, width).transpose(2, 1, 0, 3).reshape(m // width, 128, k // 128 * width))

    f = np.float32
    heads = np.array([h for a in range(2) for i in range(4) for h in (8 * a + i, 8 * a + 4 + i)])
    perm = (heads[:, None] * 64 + np.arange(64)).reshape(-1)
    D = {}
    D["xT"] = np.ascontiguousarray(x[0].T).reshape(8, 128, 1024)
    D["ctxT"] = np.ascontiguousarray(ctx[0].T.reshape(8, 128, 256).transpose(1, 0, 2))
    D["cc"] = np.ascontiguousarray(np.stack([c[0].reshape(8, 128), c_ctx.reshape(8, 128)], -1).transpose(1, 0, 2))
    D["crow"] = np.ascontiguousarray(np.broadcast_to(c[0], (128, 1024)))
    D["ada"] = np.ascontiguousarray(w_ada[0][:, 0:2048].reshape(8, 128, 2048))
    D["adaT"] = np.ascontiguousarray(w_ada[0][:, 2048:].T).reshape(32, 128, 1024)
    w = w_in[0]
    at = 0
    for name, n in (("u", 1024), ("v", 1024), ("q", 512), ("k", 512), ("vv", 1024), ("r", 1024), ("al", 32), ("ga", 1024), ("gb", 1024)):
        part = w[:, at:at + n]
        D["W" + name] = tiles(np.tile(part, (1, 4)) if name == "al" else part)
        at += n
    D["Wwa"], D["Wwb"], D["Wwo"] = tiles(w_branch_a[0]), tiles(w_branch_b[0]), tiles(w_out[0])
    D["Wf1"] = tiles(w_ffn_in[0])
    D["Wf2"] = np.ascontiguousarray(w_ffn_out[0]).reshape(22, 128, 1024)
    wal = np.zeros((128, 2, 512), f)
    for i in range(3):
        wal[32 * i:32 * i + 16, 0] = w_alpha_f[0]
        wal[32 * i + 16:32 * i + 32, 1] = w_alpha_b[0]
    D["walpha"] = wal
    D["wspT"] = np.ascontiguousarray(w_spatial[0].transpose(2, 0, 1)).reshape(128, 1024)
    D["bspb"] = np.ascontiguousarray(np.broadcast_to(b_spatial[0].reshape(1, 1024), (128, 1024)))
    D["lnvb"] = np.ascontiguousarray(np.broadcast_to(np.stack([ln_v_g[0], ln_v_b[0]]), (128, 2, 1024)))
    w = w_in_2[0]
    D["Wu2"], D["Wg2"] = tiles(w[:, 0:1024][:, perm]), tiles(w[:, 1024:2048][:, perm])
    D["Wq2"], D["Wk2"], D["Wv2"] = tiles(w[:, 2048:3072][:, perm]), tiles(w[:, 3072:3328]), tiles(w[:, 3328:3584])
    D["Wz0"], D["Wz1"] = tiles(w[:, 3584:4608][:, perm]), tiles(w[:, 4608:5632][:, perm])
    D["Wwo2"] = tiles(w_out_2[0][perm])
    D["Wf12"] = tiles(w_ffn_in_2[0])
    D["Wf22"] = np.ascontiguousarray(w_ffn_out_2[0]).reshape(22, 128, 1024)
    lw = np.zeros((8, 128, 4, 128), f)
    for m in range(8):
        for j in range(2):
            h = heads[2 * m + j]
            for d in range(2):
                for y, src in enumerate((lru_wa_2, lru_wx_2)):
                    lw[m, 64 * j:64 * j + 64, 2 * d + y, 64 * j:64 * j + 64] = src[0, d, h]
    D["lruw"] = lw.reshape(8, 128, 512)
    bg = b_gate_2[0].reshape(2, 1024)[:, perm]
    parts = {
        "b_ada": cols(b_ada[0]), "n1": cols(norm1_g[0]), "n2": cols(norm2_g[0]),
        "b_al": np.concatenate([cols(b_alpha_f[0]), cols(b_alpha_b[0])], 1), "gn": cols(gla_norm_g[0]),
        "nm2": None, "lam": cols(lru_lambda_2[0][:, perm]), "lba": cols(lru_ba_2[0][:, perm]), "lbx": cols(lru_bx_2[0][:, perm]),
        "cw": conv_w_2[0][:, perm].reshape(4, 8, 128).transpose(2, 1, 0).reshape(128, 32), "cb": cols(conv_b_2[0][perm]),
        "bg": cols(bg), "sink": np.broadcast_to(attn_sink_2[0], (128, 16)), "nf2": cols(norm_ffn_g_2[0]), "nfin": cols(norm_final_g_2), "fin1": cols(final_norm_g),
    }
    parts["nm2"] = cols(norm_mix_g_2[0])
    v = np.concatenate([parts[n] for n, _ in VECTORS], 1)
    D["vec"] = np.ascontiguousarray(np.concatenate([v, np.zeros((128, 240 - v.shape[1]), f)], 1))
    D["ident"] = np.eye(128, dtype=f)
    cm = np.ones((128, 512), f)
    cm[:, ::64] = 0
    D["cmask"] = cm
    j, i = np.arange(128)[:, None], np.arange(128)[None]
    D["amask0"] = ((j // 64 == i // 64) & (j <= i)).astype(np.int32)
    D["amask1"] = ((j // 64 == i // 64) & (j >= i)).astype(np.int32)
    s = np.arange(384)[None]
    dist = np.abs(j + 128 - s)
    D["alibi"] = np.where(dist <= 128, dist, 1e34).astype(f)
    return D


def kernel(**inputs):
    import concourse.bacc as bacc
    from concourse.bass_utils import run_bass_kernel_spmd

    D = layout(**{k: np.asarray(v) for k, v in inputs.items()})
    nc = bacc.Bacc("TRN2", target_bir_lowering=False, num_devices=1)
    aps = {n: nc.dram_tensor("i_" + n, a.shape, mybir.dt.from_np(a.dtype), kind="ExternalInput").ap() for n, a in D.items()}
    out = nc.dram_tensor("o_out", (8, 128, 1024), F, kind="ExternalOutput").ap()
    program(nc, aps, out)
    r = run_bass_kernel_spmd(nc, [{"i_" + n: a for n, a in D.items()}], core_ids=[0])
    y = np.asarray(r.results[0]["o_out"])
    return np.ascontiguousarray(y.reshape(1024, 1024).T)[None]
```

```python
from contextlib import ExitStack

import numpy as np

import concourse.bass as bass
from concourse import mybir

F = mybir.dt.float32
R = mybir.dt.float32r
I32 = mybir.dt.int32
ALU = mybir.AluOpType
ACT = mybir.ActivationFunctionType
AX = mybir.AxisListType

T = 1024
TC = 256
NF = 22
EPS = 1e-6
NW = 4
NS = 2
NT = 4


class Engine:

    def __init__(self, name, eng, sems):
        self.name, self.eng, self.sems, self.n, self.seen = name, eng, sems, 0, {}

    def wait(self, *tokens):
        for t in tokens:
            if t is None:
                continue
            if isinstance(t, list):
                self.wait(*t)
            elif self.seen.get(t[0], 0) < t[1]:
                self.seen[t[0]] = t[1]
                self.eng.wait_ge(self.sems(t[0]), t[1])

    def do(self, fn, *tokens):
        self.wait(*tokens)
        self.n += 1
        fn(self.eng).then_inc(self.sems(self.name), 1)
        return (self.name, self.n)

    def quiet(self, fn, *tokens):
        self.wait(*tokens)
        fn(self.eng)


class Dma:

    def __init__(self, eng, n):
        self.eng, self.n = eng, n

    def __call__(self, key, out, in_, *tokens):
        self.eng.wait(*tokens)
        self.n[key] = self.n.get(key, 0) + 16
        self.eng.eng.dma_start(out, in_).then_inc(self.eng.sems(key), 16)
        return (key, self.n[key])


def weight_order():
    order = [("al", 0)]
    order += [("k", m) for m in range(4)] + [("vv", m) for m in range(8)] + [("q", m) for m in range(4)]
    for n in ("v", "u", "r", "ga", "gb"):
        order += [(n, m) for m in range(8)]
    for n in ("wa", "wb", "wo"):
        order += [(n, m) for m in range(8)]
    order += ffn_order("f1", "f2")
    for m in range(8):
        order += [("u2", m), ("g2", m), ("z0", m)]
    order += [("k2", 0), ("k2", 1), ("v2", 0), ("v2", 1)]
    order += [("q2", m) for m in range(4)] + [("z1", m) for m in range(4)]
    order += [("q2", m) for m in range(4, 8)] + [("z1", m) for m in range(4, 8)]
    order += [("wo2", m) for m in range(8)]
    order += ffn_order("f12", "f22")
    return order


GROUPS = [(2 * i, 2 * i + 1) for i in range(NF // 2)]


def ffn_order(one, two):
    order = []
    for i, g in enumerate(GROUPS):
        for t in g:
            order += [(one, t), (one, NF + t)]
        if i:
            order += [(two, t) for t in GROUPS[i - 1]]
    return order + [(two, t) for t in GROUPS[-1]]


def program(nc, D, out):
    top = ExitStack()
    with top:
        held = {}

        def sems(key):
            if key not in held:
                held[key] = nc.alloc_semaphore("q_" + key)
            return held[key]

        PE, AC, DV, PO, SP = (Engine(n, e, sems) for n, e in (("pe", nc.tensor), ("ac", nc.scalar), ("dv", nc.vector), ("po", nc.gpsimd), ("sp", nc.sync)))
        dma = Dma(SP, {})
        dma_out = Dma(PO, dma.n)
        cnt = [0]

        def alloc(stack, shape, dt, name="t"):
            cnt[0] += 1
            return stack.enter_context(nc.sbuf_tensor(f"s_{name}{cnt[0]}", shape, dt))

        def A(shape, dt, name="t"):
            return alloc(top, shape, dt, name)

        def scratch(name, shape):
            return nc.dram_tensor("d_" + name, shape, F, kind="Internal").ap()

        XH = A([128, 8, T], R, "xh")
        XL = A([128, 8, T], R, "xl")
        WH = A([128, NW, 1024], R, "wh")
        WL = A([128, NW, 1024], R, "wl")
        WS = A([128, NS, 1024], F, "ws")
        RES = A([128, 8, T], F, "res")
        TMP = A([128, NT, 512], F, "tmp")
        ACC = A([128, T], F, "acc")
        RB = A([128, T], F, "rb")
        ident = A([128, 128], F, "ident")
        ones = A([128, 128], F, "ones")
        MOD = A([128, 48], F, "mod")
        MODC = A([128, 16], F, "modc")
        VEC = A([128, 240], F, "vec")
        GS = A([128, 24], F, "gs")
        eps = A([128, 1], F, "eps")
        BG2 = A([128, 8], F, "bg2")
        RC = A([128, 3, 4], F, "rc")
        R12 = A([128, 2, 4], F, "r12")
        FN = A([128, 8], F, "fn")
        B = [top.enter_context(nc.psum_tensor(f"p_{i}", [128, 512], F)) for i in range(8)]
        bfree = [None] * 8

        t_vec = dma("vec", VEC[:], D["vec"])
        t_id = dma("ident", ident[:], D["ident"])
        t_ones = DV.do(lambda e: e.memset(ones[:], 1.0))
        t_eps = DV.do(lambda e: e.memset(eps[:], EPS))

        V = {}
        at = 0
        for name, n in VECTORS:
            V[name] = at
            at += n

        t_bg2 = DV.do(lambda e: e.tensor_scalar(BG2[:, :], VEC[:, V["bg"] + 8:V["bg"] + 16], 0.5, None, ALU.mult), t_vec)

        def vec(name, m):
            return VEC[:, V[name] + m:V[name] + m + 1]

        def so_far(skip=()):
            t = [(e.name, e.n) for e in (PE, AC, DV, PO) if e.n]
            return t + [(k, v) for k, v in dma.n.items() if not k.startswith(("ws",) + tuple(skip))]

        def join(tokens):
            for e in (AC, DV, PO, SP):
                e.wait(tokens)

        def barrier(skip=()):
            join(so_far(skip))

        order = weight_order()
        wsplit, wfree, wload = {}, {}, {}
        state = {"next": 0, "loaded": 0, "split": 0}

        def wload_to(n):
            while state["loaded"] < min(n, len(order)):
                i = state["loaded"]
                name, m = order[i]
                src = D["W" + name][m]
                cols = src.shape[1]
                wload[i] = dma(f"ws{i % NS}", WS[:, i % NS, 0:cols], src, wsplit.get(i - NS))
                state["loaded"] += 1

        def wsplit_to(n):
            while state["split"] < min(n, len(order)) and (state["split"] < NW or state["split"] - NW in wfree):
                i = state["split"]
                wload_to(i + 1)
                s, w = i % NS, i % NW
                cols = D["W" + order[i][0]][order[i][1]].shape[1]
                hi, lo, src = WH[:, w, 0:cols], WL[:, w, 0:cols], WS[:, s, 0:cols]
                t1 = AC.do(lambda e: e.activation(hi, src, ACT.Copy), wload[i], wfree.get(i - NW))
                t2 = DV.do(lambda e: e.tensor_tensor(lo, src, hi.bitcast(F), ALU.subtract), wload[i], t1)
                wsplit[i] = [t1, t2]
                state["split"] += 1

        def wget(name, m):
            i = state["next"]
            assert order[i] == (name, m), (order[i], name, m)
            state["next"] += 1
            wsplit_to(i + 3)
            wload_to(state["split"] + NS)
            assert i in wsplit
            return i

        def wdone(i, token):
            wfree[i] = token
            wsplit_to(state["next"] + 2)

        banks = {"use": [0, 1, 2], "n": 0}

        def bank():
            b = banks["use"][banks["n"] % len(banks["use"])]
            banks["n"] += 1
            return b

        xtok = [[None] * 8, [None] * 8]
        defer = {}

        def products(ws, half, M=128, X=None, n=512, tok=None, mids=None):
            H, L = X or (XH, XL)
            tok = tok or xtok[half]
            bs = [bank() for _ in ws]
            mids = dict(mids or {})
            mids.update(defer)
            defer.clear()
            out = []
            for k in range(8):
                if k in mids:
                    mids[k]()
                PE.wait(tok[k])
                xh, xl = H[:, k, half * n:half * n + n], L[:, k, half * n:half * n + n]
                for b, i in zip(bs, ws):
                    w = i % NW
                    o = B[b][0:M, 0:n]
                    wh, wl = WH[:, w, k * M:(k + 1) * M], WL[:, w, k * M:(k + 1) * M]
                    if k == 0:
                        PE.wait(bfree[b], wsplit[i])
                    PE.quiet(lambda e: e.matmul(o, wh, xh, start=(k == 0), stop=False))
                    PE.quiet(lambda e: e.matmul(o, wh, xl, start=False, stop=False))
                    f = (lambda e: e.matmul(o, wl, xh, start=False, stop=(k == 7)))
                    if k < 7:
                        PE.quiet(f)
                    else:
                        out.append((b, PE.do(f)))
            return out

        def product(i, half, **kw):
            return products([i], half, **kw)[0]

        def split_to(hi, lo, src, *tokens):
            t1 = AC.do(lambda e: e.activation(hi, src, ACT.Copy), *tokens)
            t2 = DV.do(lambda e: e.tensor_tensor(lo, src, hi.bitcast(F), ALU.subtract), t1, *tokens)
            return [t1, t2]

        later = []

        def run_later():
            todo, later[:] = later[:], []
            for f in todo:
                f()

        written = {}
        ring = {"i": 0, "free": [None] * NT}
        pinned = set()

        def take():
            while ring["i"] % NT in pinned:
                ring["i"] += 1
            s = ring["i"] % NT
            ring["i"] += 1
            return s, ring["free"][s]

        def store(s, dst, src, name, *tokens):
            t = dma_out(f"so{s}", dst, src, *tokens)
            ring["free"][s] = t
            for key in {name, name[0] if isinstance(name, tuple) else name}:
                written.setdefault(key, []).append(t)
            return t

        def square_sum(x, c, n, first, tx, tacc, eng=None, acc=None, scale=1.0):
            a = (acc if acc is not None else ACC)[:, c:c + n]
            if first:
                return AC.do(lambda e: e.activation(a, x, ACT.Square, scale=scale), tx, tacc)
            s, fr = take()
            q = TMP[:, s, 0:n]
            t1 = AC.do(lambda e: e.activation(q, x, ACT.Square, scale=scale), tx, fr)
            t2 = (eng or DV).do(lambda e: e.tensor_tensor(a, a, q, ALU.add), t1, tacc)
            ring["free"][s] = t2
            return t2

        rc = {"i": 0, "free": [None] * 3}

        def rms_cols(c, n, tacc, acc=None):
            a = acc if acc is not None else ACC
            b = bank()
            for j in range(n // 128):
                f = (lambda e: e.matmul(B[b][:, j:j + 1], a[:, c + 128 * j:c + 128 * j + 128], ones[:, 0:1], start=True, stop=True))
                if j < n // 128 - 1:
                    PE.quiet(f, bfree[b], tacc, t_ones)
                else:
                    t = PE.do(f, bfree[b], tacc, t_ones)
            return b, t

        def root(r, ps, t, *more):
            t1 = AC.do(lambda e: e.activation(r, ps, ACT.Sqrt, bias=eps[:, 0:1], scale=1.0 / 1024), t, t_eps, *more)
            return t1, DV.do(lambda e: e.reciprocal(r, r), t1)

        def diagonal(r, n, t):
            s, fr = take()
            pinned.add(s)
            m = n // 128
            o = TMP[:, s, 0:n].rearrange("p (c t) -> p c t", c=m)
            return s, DV.do(lambda e: e.tensor_tensor(o, ident[:, :].rearrange("p (o t) -> p o t", o=1).to_broadcast([128, m, 128]),
                                                      r.rearrange("p (c o) -> p c o", o=1).to_broadcast([128, m, 128]), ALU.mult), t, t_id, fr)

        def spread(st, n):
            s, t = st
            b = bank()
            t2 = PE.do(lambda e: e.matmul(B[b][:, 0:n], ones[:], TMP[:, s, 0:n], start=True, stop=True), t, bfree[b])
            ring["free"][s] = t2
            pinned.discard(s)
            return b, t2

        def rms_root(bt, n):
            b, t = bt
            q = rc["i"] % 3
            rc["i"] += 1
            r = RC[:, q, 0:n // 128]
            t1, t2 = root(r, B[b][:, 0:n // 128], t, rc["free"][q])
            bfree[b] = t1
            return q, r, t2

        def rms_diagonal(qrt, n):
            q, r, t = qrt
            st = diagonal(r, n, t)
            rc["free"][q] = st[1]
            return st

        def rms_scale(bt, n):
            return rms_diagonal(rms_root(bt, n), n)

        def norm_tiles(src, c, n, bt, scale, shift, H, L, ready, free, tg=None, hooks=None):
            outs, todo = [], None
            b, trb = bt
            r = B[b][:, 0:n]
            for k in range(8):
                if hooks and k in hooks:
                    hooks[k]()
                s, fr = take()
                q, x = TMP[:, s, 0:n], src[:, k, c:c + n]
                h, l = H[:, k, c:c + n], L[:, k, c:c + n]
                t1 = DV.do(lambda e: e.scalar_tensor_tensor(out=q, in0=x, scalar=scale(k), in1=r, op0=ALU.mult, op1=ALU.mult), trb, tg, ready[k], fr)
                if shift:
                    t2 = AC.do(lambda e: e.activation(h, q, ACT.Identity, bias=shift(k)), t1, free)
                else:
                    t2 = AC.do(lambda e: e.activation(h, q, ACT.Copy), t1, free)
                if todo:
                    todo()

                def todo(s=s, q=q, h=h, l=l, k=k, t2=t2):
                    if shift:
                        t3 = DV.do(lambda e: e.scalar_tensor_tensor(out=l, in0=q, scalar=shift(k), in1=h.bitcast(F), op0=ALU.add, op1=ALU.subtract), t2, free)
                    else:
                        t3 = DV.do(lambda e: e.tensor_tensor(l, q, h.bitcast(F), ALU.subtract), t2, free)
                    ring["free"][s] = [t2, t3]
                    outs.append([t2, t3])
            todo()
            bfree[b] = t1
            return outs

        def load_tile(src, k, half, tw, free):
            return split_tile(k, half, load_raw(src, k, half, tw), free)

        def load_raw(src, k, half, tw):
            s, fr = take()
            pinned.add(s)
            return s, dma(f"st{s}", TMP[:, s, :], src[k][:, 512 * half:512 * half + 512], tw, fr)

        def split_tile(k, half, st, free):
            s, t = st
            c = 512 * half
            ring["free"][s] = split_to(XH[:, k, c:c + 512], XL[:, k, c:c + 512], TMP[:, s, :], t, free)
            pinned.discard(s)
            return ring["free"][s]

        def pe_now():
            return ("pe", PE.n)

        pc = ExitStack()
        CH = alloc(pc, [128, 8, TC], R, "ch")
        CL = alloc(pc, [128, 8, TC], R, "cl")
        p0 = ExitStack()
        sc2 = alloc(p0, [128, 8, 2], F, "sc2")
        AD = alloc(p0, [128, 2, 2048], F, "ad")
        XC = alloc(p0, [128, 8, TC], F, "xc")
        mrow = alloc(p0, [2, 2048], F, "mrow")

        t_cc = dma("cc", sc2[:], D["cc"])
        t_sc = AC.do(lambda e: e.activation(sc2[:, :, :], sc2[:, :, :], ACT.Silu), t_cc)
        banks["use"] = [4, 5, 6, 7]
        tad = [None, None]
        tx = [None] * 8
        tacc = [None, None]
        txc = dma("xc", XC[:], D["ctxT"])

        def ada(k):
            t = dma(f"ad{k % 2}", AD[:, k % 2, :], D["ada"][k], tad[k % 2])
            for c in range(4):
                f = (lambda e: e.matmul(B[c][0:2, :], sc2[:, k, :], AD[:, k % 2, c * 512:c * 512 + 512], start=(k == 0), stop=(k == 7)))
                if c < 3:
                    PE.quiet(f, t, t_sc)
                else:
                    tad[k % 2] = PE.do(f)

        wload_to(NS)
        for k in range(4):
            ada(k)
            for x in (2 * k, 2 * k + 1):
                tx[x] = dma(f"x{x}", RES[:, x, :], D["xT"][x])
        ada(4)
        ada(5)
        tc_ = None
        for k in range(8):
            s, fr = take()
            q, x = TMP[:, s, 0:TC], XC[:, k, :]
            if k == 0:
                tc_ = AC.do(lambda e: e.activation(RB[:, 0:TC], x, ACT.Square), txc)
            else:
                t1 = AC.do(lambda e: e.activation(q, x, ACT.Square), txc, fr)
                tc_ = DV.do(lambda e: e.tensor_tensor(RB[:, 0:TC], RB[:, 0:TC], q, ALU.add), t1, tc_)
                ring["free"][s] = tc_
        wsplit_to(NS)
        wload_to(NW)
        for k in range(8):
            for h in range(2):
                tacc[h] = square_sum(RES[:, k, 512 * h:512 * h + 512], 512 * h, 512, k == 0, tx[k], tacc[h])

        def rooted(src, c, n, qrt, ready):
            b, t = spread(rms_diagonal(qrt, n), n)
            out = [DV.do(lambda e: e.tensor_tensor(src[:, k, c:c + n], src[:, k, c:c + n], B[b][:, 0:n], ALU.mult), t, ready[k]) for k in range(8)]
            bfree[b] = out[-1]
            return out

        st = [rms_root(rms_cols(0, TC, tc_, RB), TC)]
        for h in range(2):
            st.append(rms_root(rms_cols(512 * h, 512, tacc[h]), 512))
        ada(6)
        txc = rooted(XC, 0, TC, st[0], [txc] * 8)
        ready = [[tx[k], tacc] for k in range(8)]
        ada(7)
        txh = rooted(RES, 0, 512, st[1], ready)
        tmr = None
        for c in range(4):
            tmr = AC.do(lambda e: e.activation(mrow[:, c * 512:c * 512 + 512], B[c][0:2, :], ACT.Copy), tad[0], tad[1])
        bfree[0:4] = [tmr] * 4
        for m in range(16):
            f = (lambda e: e.transpose(B[0][:, 2 * m:2 * m + 2], mrow[:, m * 128:m * 128 + 128], ident[0:2, 0:2]))
            if m < 15:
                PE.quiet(f, tmr, t_id)
            else:
                t = PE.do(f)
        mp = B[0][:, 0:32].rearrange("p (m j) -> p j m", j=2)
        bada = VEC[:, V["b_ada"]:V["b_ada"] + 16]
        t_m1 = DV.do(lambda e: e.tensor_tensor(MOD[:, 0:16], mp[:, 0, :], bada, ALU.add), t, t_vec)
        t_m2 = DV.do(lambda e: e.tensor_tensor(MODC[:, 0:16], mp[:, 1, :], bada, ALU.add))
        bfree[0] = t_m2
        n1 = VEC[:, V["n1"]:V["n1"] + 8]
        t_g1 = DV.do(lambda e: e.scalar_tensor_tensor(out=GS[:, 0:8], in0=MOD[:, 8:16], scalar=1.0, in1=n1, op0=ALU.add, op1=ALU.mult), t_m1)
        t_g2 = DV.do(lambda e: e.scalar_tensor_tensor(out=GS[:, 8:16], in0=MODC[:, 8:16], scalar=1.0, in1=n1, op0=ALU.add, op1=ALU.mult), t_m2)

        def modulated(src, c, n, scale, shift, H, L, ready):
            outs, todo = [], None
            for k in range(8):
                s, fr = take()
                q = TMP[:, s, 0:n]
                h, l = H[:, k, c:c + n], L[:, k, c:c + n]
                t1 = DV.do(lambda e: e.tensor_scalar(q, src[:, k, c:c + n], scale[:, k:k + 1], shift[:, k:k + 1], ALU.mult, ALU.add), ready[k], t_g1, t_g2, fr)
                t2 = AC.do(lambda e: e.activation(h, q, ACT.Copy), t1)
                if todo:
                    todo()

                def todo(s=s, q=q, h=h, l=l, t2=t2):
                    t3 = DV.do(lambda e: e.tensor_tensor(l, q, h.bitcast(F), ALU.subtract), t2)
                    ring["free"][s] = t3
                    outs.append([t2, t3])
            todo()
            return outs

        wsplit_to(NW)
        ctok = modulated(XC, 0, TC, GS[:, 8:16], MODC, CH, CL, txc)
        xtok[0] = modulated(RES, 0, 512, GS[:, 0:8], MOD, XH, XL, txh)
        free0 = so_far(("vec", "ident"))

        def second_half():
            xtok[1] = modulated(RES, 512, 512, GS[:, 0:8], MOD, XH, XL, rooted(RES, 512, 512, st[2], ready))


        dB = [scratch("bf", [4, 128, T + TC]), scratch("bb", [4, 128, T + TC])]
        dK = scratch("k", [4, 128, T + TC])
        dQ = scratch("q", [4, 128, T])
        dV = scratch("v", [10, 128, 1024])
        dVm = scratch("vm", [8, 128, 1024])
        dU = scratch("u", [8, 128, T])
        dR = scratch("r", [8, 128, T])
        dGA = scratch("ga", [8, 128, T])
        dGB = scratch("gb", [8, 128, T])
        dA = scratch("a", [8, 128, T])
        dBo = scratch("bo", [8, 128, T])

        p1 = ExitStack()
        banks["use"] = [0, 1, 2]

        def parts(ctx):
            p = [(TC, 0, 512, (XH, XL), None), (TC + 512, 1, 512, (XH, XL), None)]
            if ctx:
                p = [(0, 0, 256, (CH, CL), ctok)] + p
            return p

        p0.close()
        join(free0)
        AL = alloc(p1, [128, T + TC], R, "al")
        WAL = alloc(p1, [128, 2, 512], R, "wal")
        WA0 = alloc(p1, [128, 2, 512], F, "wa0")
        LG = alloc(p1, [128, 2, 2, 512], F, "lg")
        cmask = alloc(p1, [128, 512], F, "cmask")
        cb = alloc(p1, [128, 1024], F, "cb")
        aw = alloc(p1, [128, 1024], F, "aw")
        t_wal = dma("wal", WA0[:], D["walpha"])
        t_cm = dma("cmask", cmask[:], D["cmask"])
        t_cb = dma("cb", cb[:], D["crow"])
        t_cb = AC.do(lambda e: e.activation(cb[:, :], cb[:, :], ACT.Silu), t_cb)
        t1 = AC.do(lambda e: e.activation(WAL[:, :, :], WA0[:, :, :], ACT.Copy), t_wal)
        t_wal = DV.do(lambda e: e.tensor_tensor(WAL[64:96, :, :], WA0[64:96, :, :], WAL[64:96, :, :].bitcast(F), ALU.subtract), t1)

        def turned(src, n, col, m, dst, name, ts, tbank):
            c4 = n // 128
            for c in range(c4):
                f = (lambda e: e.transpose(B[tbank][:, c * 128:c * 128 + 128], src[:, c * 128:c * 128 + 128], ident[:]))
                if c < c4 - 1:
                    PE.quiet(f, bfree[tbank], ts, t_id)
                else:
                    t = PE.do(f, bfree[tbank], ts, t_id)
            s, fr = take()
            t2 = DV.do(lambda e: e.tensor_copy(TMP[:, s, 0:n], B[tbank][:, 0:n]), t, fr)
            bfree[tbank] = t2
            store(s, dst[col // 128:col // 128 + c4, :, m * 128:m * 128 + 128].rearrange("c p f -> p c f"),
                  TMP[:, s, 0:n].rearrange("p (c f) -> p c f", f=128), name, t2)
            return t

        VF = [ACC[:, 0:512], ACC[:, 512:1024], RB[:, 0:512], RB[:, 512:1024]]
        vf = {"i": 0, "free": [[xtok[0][7], xtok[1][7]]] * 4}

        def project(name, m, ctx, put):
            i = wget(name, m)
            for col, h, n, X, tok in parts(ctx):
                b, t = product(i, h, X=X, n=n, tok=tok)
                run_later()
                put(m, col, n, B[b][:, 0:n], b, t)
                yield
            wdone(i, t)

        def put_plain(dst, name, off, scale=1.0):
            def put(m, col, n, ps, b, t):
                s, fr = take()
                o = TMP[:, s, 0:n]
                t2 = AC.do(lambda e: e.activation(o, ps, ACT.Copy, scale=scale), t, fr)
                bfree[b] = t2
                store(s, dst[m][:, col - off:col - off + n], o, (name, m), t2)
            return put

        def put_turned(dst, name, off, tbank):
            def put(m, col, n, ps, b, t):
                q = vf["i"] % 4
                vf["i"] += 1
                o = VF[q][:, 0:n]
                t2 = AC.do(lambda e: e.activation(o, ps, ACT.Copy), t, vf["free"][q])
                bfree[b] = t2

                def go():
                    vf["free"][q] = turned(o, n, col - off, m, dst, name, t2, tbank)
                later.append(go)
            return put

        def run(g):
            for _ in g:
                pass

        def beside(fill, work, rate, due=0.0):
            for _ in fill:
                due += rate
                while due >= 1:
                    due -= 1
                    next(work, 0)
                yield
            for _ in work:
                yield

        def projections():
            yield from project("k", 3, True, putk)
            for m in range(8):
                yield from project("vv", m, True, put_turned(dV, "v", 0, 3))
            for m in range(4):
                yield from project("q", m, False, put_plain(dQ, "q", TC, scale=float(128 ** -0.5)))

        banks["use"] = list(range(8))
        ws = [wget("al", 0)] + [wget("k", m) for m in range(3)]
        tal = []
        putk = put_plain(dK, "k", 0)
        for col, h, n, X, tok in parts(True):
            r = products(ws, h, X=X, n=n, tok=tok, mids={3: second_half} if col == TC else None)
            b, t = r[0]
            o = AL[:, col:col + n]
            t2 = AC.do(lambda e: e.activation(o, B[b][:, 0:n], ACT.Copy), t)
            lo = AL[32:64, col:col + n]
            t3 = DV.do(lambda e: e.tensor_tensor(lo, B[b][32:64, 0:n], lo.bitcast(F), ALU.subtract), t2)
            bfree[b] = t3
            tal.append((col, n, [t2, t3]))
            for m in range(3):
                putk(m, col, n, B[r[1 + m][0]][:, 0:n], *r[1 + m])
        for i in ws:
            wdone(i, r[-1][1])
        banks["use"] = [0, 1, 2]

        def decays():
            tlg = [None, None]
            j = 0
            for d in range(2):
                for h in range(4):
                    for col, n, ta in tal:
                        b = 4 + j % 2
                        q = j % 2
                        j += 1
                        t = PE.do(lambda e: e.matmul(B[b][:, 0:n], WAL[:, d, h * 128:h * 128 + 128], AL[:, col:col + n], start=True, stop=True),
                                  bfree[b], ta, t_wal)
                        bias = vec("b_al", 4 * d + h)
                        g0, g1 = LG[:, q, 0, 0:n], LG[:, q, 1, 0:n]
                        ps = B[b][:, 0:n]
                        t1 = AC.do(lambda e: e.activation(g0, ps, ACT.Abs, bias=bias), t, tlg[q], t_vec)
                        t2 = DV.do(lambda e: e.tensor_scalar(g1, ps, bias, 0.0, ALU.add, ALU.min), t1, tlg[q], t_vec)
                        bfree[b] = t2
                        t3 = AC.do(lambda e: e.activation(g0, g0, ACT.Exp, scale=-1.0), t1)
                        t4 = AC.do(lambda e: e.activation(g0, g0, ACT.Ln, bias=ones[:, 0:1]), t3, t_ones)
                        yield
                        t5 = DV.do(lambda e: e.tensor_tensor(g1, g1, g0, ALU.subtract), t4, t2)
                        s, fr = take()
                        o = TMP[:, s, 0:n]
                        if d == 0:
                            t6 = DV.do(lambda e: e.tensor_tensor_scan(o, cmask[:, 0:n], g1, 0.0, ALU.mult, ALU.add), t5, t_cm, fr)
                        else:
                            t6 = DV.do(lambda e: e.tensor_tensor_scan(o[:, ::-1], cmask[:, 0:n], g1[:, ::-1], 0.0, ALU.mult, ALU.add), t5, t_cm, fr)
                        tlg[q] = [t5, t6]
                        store(s, dB[d][h][:, col:col + n], o, f"b{d}", t6)

        mt = {}

        def mods():
            for m in range(16, 48):
                t = dma("aw", aw[:], D["adaT"][m - 16], mt.get("ops"))
                yield
                mt["ops"] = DV.do(lambda e: e.tensor_tensor_reduce(out=aw[:], in0=aw[:], in1=cb[:], scale=1.0, scalar=0.0,
                                                                   op0=ALU.mult, op1=ALU.add, accum_out=MOD[:, m:m + 1]), t, t_cb)
            t = DV.do(lambda e: e.tensor_tensor(MOD[:, 16:48], MOD[:, 16:48], VEC[:, V["b_ada"] + 16:V["b_ada"] + 48], ALU.add), mt["ops"])
            n2 = VEC[:, V["n2"]:V["n2"] + 8]
            mt["gs"] = DV.do(lambda e: e.scalar_tensor_tensor(out=GS[:, 16:24], in0=MOD[:, 32:40], scalar=1.0, in1=n2, op0=ALU.add, op1=ALU.mult), t)

        def side():
            a, b = decays(), mods()
            for _ in range(60):
                next(a, 0)
                next(b, 0)
                yield

        run(beside(projections(), side(), 1))
        run_later()
        barrier(("st", "so"))
        p1.close()
        pc.close()

        p2 = ExitStack()
        S2 = lambda shape, dt, name="t": [alloc(p2, shape, dt, name) for _ in range(2)]
        banks["use"] = [0, 1]
        TB, AB, KB, VB = 2, 3, 4, 5
        OB = [6, 7]
        gb, gk, gq = S2([128, 4, 128], F, "gb"), S2([128, 4, 128], F, "gk"), S2([128, 4, 128], F, "gq")
        gv = S2([128, 1024], F, "gv")
        ee_, ki_, ks_, kT_ = (S2([128, 4, 128], F, "e"), S2([128, 4, 128], F, "ki"), S2([128, 4, 128], F, "ks"), S2([128, 4, 128], F, "kt"))
        att = S2([128, 4, 128], F, "att")
        amask = S2([128, 128], I32, "am")
        SS = S2([128, 4, 256], F, "S")
        EB_ = S2([128, 4, 2], F, "eb")
        EP_ = S2([128, 4], F, "ep")
        t_am = [dma(f"am{d}", amask[d][:], D[f"amask{d}"]) for d in range(2)]
        t_att = [DV.do(lambda e: e.memset(att[d][:], 0.0)) for d in range(2)]
        t_S = [DV.do(lambda e: e.memset(SS[d][:], 0.0)) for d in range(2)]
        g_free = [{}, {}]
        o_tok = {}

        def gla(d, pair, ctx):
            col = pair * 128
            fr = g_free[d]
            b, k, q, v, ee, ki, ks, kT, EB, EP = (x[d] for x in (gb, gk, gq, gv, ee_, ki_, ks_, kT_, EB_, EP_))
            tb = dma(f"gb{d}", b[:], dB[d][:, :, col:col + 128].rearrange("h p t -> p h t"), written[f"b{d}"], fr.get("b"))
            tk = dma(f"gk{d}", k[:], dK[:, :, col:col + 128].rearrange("h p t -> p h t"), written["k"], fr.get("k"))
            tq = None
            if not ctx:
                tq = dma(f"gq{d}", q[:], dQ[:, :, col - TC:col - TC + 128].rearrange("h p t -> p h t"), written["q"], fr.get("q"))
            tv = dma(f"gv{d}", v[:], dV[pair], written["v"], fr.get("v"))
            yield
            first, second = (0, 1) if d == 0 else (1, 0)
            last = (lambda c: 64 * c + 63) if d == 0 else (lambda c: 64 * c)
            f0, s0 = 64 * first, 64 * second
            lastv = b[:, :, last(0):last(0) + 65:64]
            b2 = b[:, :, :].rearrange("p h (c t) -> p h c t", c=2)
            for c in range(2):
                td = DV.do(lambda e: e.tensor_tensor(ks[:, :, 64 * c:64 * c + 64], b[:, :, last(c):last(c) + 1].to_broadcast([128, 4, 64]), b2[:, :, c, :], ALU.subtract), tb, fr.get("ks"))
            te = AC.do(lambda e: e.activation(EB[:, :, :], lastv, ACT.Exp, scale=1 / 16), tb, fr.get("EB"))
            if not ctx:
                t1 = AC.do(lambda e: e.activation(ee[:, :, :], b[:, :, :], ACT.Exp, scale=1 / 16), tb, fr.get("ee"))
                tq1 = DV.do(lambda e: e.tensor_tensor(q[:, :, :], q[:, :, :], ee[:, :, :], ALU.mult), t1, tq)
                t2 = AC.do(lambda e: e.activation(ki[:, :, :], b[:, :, :], ACT.Exp, scale=-1 / 16), tb, fr.get("ki"))
                tki = DV.do(lambda e: e.tensor_tensor(ki[:, :, :], k[:, :, :], ki[:, :, :], ALU.mult), t2, tk)
                fr["ee"] = tq1
            t3 = AC.do(lambda e: e.activation(ks[:, :, :], ks[:, :, :], ACT.Exp, scale=1 / 16), td)
            fr["b"] = [t3, td]
            tks = DV.do(lambda e: e.tensor_tensor(ks[:, :, :], k[:, :, :], ks[:, :, :], ALU.mult), t3, tk)
            fr["k"] = tks
            tp = DV.do(lambda e: e.tensor_tensor(EP[:, :], EB[:, :, 0], EB[:, :, 1], ALU.mult), te, fr.get("EP"))
            yield
            tx1 = tks
            if not ctx:
                for h in range(4):
                    PE.quiet(lambda e: e.matmul(B[AB][:, h * 128:h * 128 + 128], ki[:, h, :], q[:, h, :], start=True, stop=True), tki, tq1, bfree[AB])
                for h in range(4):
                    f = (lambda e: e.matmul(B[KB][f0:f0 + 64, h * 64:h * 64 + 64], ks[:, h, f0:f0 + 64], q[:, h, s0:s0 + 64], start=True, stop=True))
                    if h < 3:
                        PE.quiet(f, tks, bfree[KB])
                    else:
                        ta = PE.do(f)
                fr["ki"] = ta
                tq2 = DV.do(lambda e: e.tensor_tensor(q[:, :, s0:s0 + 64], q[:, :, s0:s0 + 64], EB[:, :, first:first + 1].to_broadcast([128, 4, 64]), ALU.mult), ta)
                tx1 = ta
            tks2 = DV.do(lambda e: e.tensor_tensor(ks[:, :, f0:f0 + 64], ks[:, :, f0:f0 + 64], EB[:, :, second:second + 1].to_broadcast([128, 4, 64]), ALU.mult), tx1, te)
            fr["EB"] = [tks2, tp]
            if not ctx:
                tc = DV.do(lambda e: e.copy_predicated(att[d][:, :, :], amask[d][:].rearrange("p (o t) -> p o t", o=1).to_broadcast([128, 4, 128]),
                                                      B[AB][:, :].rearrange("p (h t) -> p h t", h=4)), ta, t_att[d], t_am[d])
                bfree[AB] = tc
                tc2 = DV.do(lambda e: e.tensor_copy(att[d][f0:f0 + 64, :, s0:s0 + 64], B[KB][f0:f0 + 64, 0:256].rearrange("p (h t) -> p h t", h=4)), tc)
                bfree[KB] = tc2
            yield
            for h in range(4):
                f = (lambda e: e.transpose(B[KB][:, h * 128:h * 128 + 128], ks[:, h, :], ident[:]))
                if h < 3:
                    PE.quiet(f, tks2, bfree[KB])
                else:
                    tt = PE.do(f)
            fr["ks"] = tt
            tkt = AC.do(lambda e: e.activation(kT[:, :, :], B[KB][:, :].rearrange("p (h t) -> p h t", h=4), ACT.Copy), tt, fr.get("kT"))
            bfree[KB] = tkt
            to = None
            if not ctx:
                for h in range(4):
                    bk = OB[h // 2]
                    o = B[bk][:, (h % 2) * 256:(h % 2) * 256 + 256]
                    PE.quiet(lambda e: e.matmul(o, q[:, h, :], SS[d][:, h, :], start=True, stop=False), tq2, t_S[d], bfree[bk])
                    f = (lambda e: e.matmul(o, att[d][:, h, :], v[:, h * 256:h * 256 + 256], start=False, stop=True))
                    if h % 2 == 0:
                        PE.quiet(f, tc2, tv)
                    else:
                        to = PE.do(f, tc2, tv)
                        key = (pair - 2, h // 2)
                        dst = RES[:, pair - 2, h // 2 * 512:h // 2 * 512 + 512]
                        if key not in o_tok:
                            o_tok[key] = AC.do(lambda e: e.activation(dst, B[bk][:, :], ACT.Copy), to)
                        else:
                            o_tok[key] = DV.do(lambda e: e.tensor_tensor(dst, B[bk][:, :], dst, ALU.add), to, o_tok[key])
                        bfree[bk] = o_tok[key]
                t_att[d] = to
                fr["q"] = to
            yield
            for hh in range(2):
                for h in (2 * hh, 2 * hh + 1):
                    f = (lambda e: e.matmul(B[VB][:, (h % 2) * 256:(h % 2) * 256 + 256], kT[:, h, :], v[:, h * 256:h * 256 + 256], start=True, stop=True))
                    if h % 2 == 0:
                        PE.quiet(f, tkt, bfree[VB], tv)
                    else:
                        tkv = PE.do(f)
                for h in (2 * hh, 2 * hh + 1):
                    ts = DV.do(lambda e: e.scalar_tensor_tensor(out=SS[d][:, h, :], in0=SS[d][:, h, :], scalar=EP[:, h:h + 1],
                                                                in1=B[VB][:, (h % 2) * 256:(h % 2) * 256 + 256], op0=ALU.mult, op1=ALU.add),
                               tkv, to, tp, t_S[d])
                bfree[VB] = ts
                if hh == 0:
                    yield
            t_S[d] = ts
            fr["EP"] = ts
            fr["kT"] = tkv
            fr["v"] = tkv

        def direction(d):
            for s in range(10):
                yield from gla(d, s if d == 0 else ((1 - s) if s < 2 else 11 - s), s < 2)

        def in_turn(a, b, lead):
            for _ in range(lead):
                next(a, 0)
                yield
            live = True
            while live:
                live = next(a, 0) is None
                if live:
                    yield
                live2 = next(b, 0) is None
                if live2:
                    yield
                live = live or live2

        def fill(names):
            table = {"v": (dVm, "vm"), "u": (dU, "u"), "r": (dR, "r"), "ga": (dGA, "ga"), "gb": (dGB, "gb")}
            for n in names:
                dst, key = table[n]
                put = put_turned(dst, key, TC, TB) if n == "v" else put_plain(dst, key, TC)
                for m in range(8):
                    yield from project(n, m, False, put)

        run(beside(fill(["v", "u", "r"]), in_turn(direction(0), direction(1), 2), 98 / 48))
        run_later()
        barrier(("st", "so"))
        p2.close()

        p3 = ExitStack()
        S3 = lambda shape, dt, name="t": alloc(p3, shape, dt, name)
        vn = S3([128, 4, 1024], F, "vn")
        lg = S3([128, 2, 1024], F, "lng")
        bs = S3([128, 1024], F, "bs")
        wsp = S3([128, 1024], F, "wsp")
        ld = S3([128, 3, 512], F, "ld")
        st6 = S3([128, 4, 2, 6], F, "st6")
        mv = S3([128, 4, 2], F, "mv")
        ss = S3([128, 32], F, "ss")
        t_lg = dma("lg", lg[:], D["lnvb"])
        t_bs = dma("bs", bs[:], D["bspb"])
        t_wsp = dma("wsp", wsp[:], D["wspT"])

        def mlp():
            ldf = [None] * 3
            j = 0
            tvf = [None] * 4
            tms = None
            for half in range(2):
                tn = []
                tld = []
                for c in range(4):
                    tld.append(dma(f"vn{c}", vn[:, c, :], dVm[4 * half + c], written["vm"], tvf[c]))
                yield
                for c in range(4):
                    x = vn[:, c, :]
                    t = AC.do(lambda e: e.activation(x, x, ACT.Gelu), tld[c])
                    for s in range(2):
                        t1 = DV.do(lambda e: e.bn_stats(st6[:, c, s, :], x[:, s * 512:s * 512 + 512]), t, tms)
                    tms1 = DV.do(lambda e: e.bn_aggr(mv[:, c, :], st6[:, c, :, :].rearrange("p a b -> p (a b)")), t1)
                    if c % 2:
                        yield
                t3 = AC.do(lambda e: e.activation(mv[:, :, 1], mv[:, :, 1], ACT.Sqrt, bias=eps[:, 0:1]), tms1)
                tms = DV.do(lambda e: e.reciprocal(mv[:, :, 1], mv[:, :, 1]), t3)
                for c in range(4):
                    x = vn[:, c, :]
                    t5 = DV.do(lambda e: e.tensor_scalar(x, x, mv[:, c, 0:1], mv[:, c, 1:2], ALU.subtract, ALU.mult), tms)
                    t6 = DV.do(lambda e: e.tensor_tensor(x, x, lg[:, 0, :], ALU.mult), t5, t_lg)
                    t7 = DV.do(lambda e: e.tensor_tensor(x, x, lg[:, 1, :], ALU.add), t6)
                    tn.append(t7)
                    yield
                tms = t7
                for g in range(8):
                    q = j % 3
                    j += 1
                    tu = dma(f"ld{q}", ld[:, q, :], dU[g][:, half * 512:half * 512 + 512], written[("u", g)], ldf[q])
                    bk = [3, 4][g % 2]
                    for c in range(4):
                        f = (lambda e: e.matmul(B[bk][:, c * 128:c * 128 + 128], vn[:, c, g * 128:g * 128 + 128], wsp[:, g * 128:g * 128 + 128], start=True, stop=True))
                        if c < 3:
                            PE.quiet(f, tn[c], t_wsp, bfree[bk])
                        else:
                            t = PE.do(f, tn[c])
                    tg = AC.do(lambda e: e.activation(ld[:, q, :], ld[:, q, :], ACT.Gelu), tu)
                    s, fr = take()
                    o = TMP[:, s, :]
                    bsg = bs[:, g * 128:g * 128 + 128].rearrange("p (o t) -> p o t", o=1).to_broadcast([128, 4, 128])
                    t1 = DV.do(lambda e: e.tensor_tensor(o.rearrange("p (c t) -> p c t", c=4), B[bk][:, :].rearrange("p (c t) -> p c t", c=4), bsg, ALU.add), t, t_bs, fr)
                    bfree[bk] = t1
                    t2 = DV.do(lambda e: e.tensor_tensor(o, o, ld[:, q, :], ALU.mult), t1, tg)
                    ldf[q] = t2
                    store(s, dA[g][:, half * 512:half * 512 + 512], o, ("a", g), t2)
                    yield
                tvf = [t] * 4

            for p8 in range(8):
                for h in range(4):
                    o = RES[:, p8, h * 256:h * 256 + 256]
                    c = 4 * p8 + h
                    q = h % 3
                    t1 = AC.do(lambda e: e.activation(ld[:, q, 0:256], o, ACT.Square, accum_out=ss[:, c:c + 1]), o_tok[(p8, 0)], o_tok[(p8, 1)], ldf[q])
                    ldf[q] = t1
                if p8 % 2:
                    yield
            t2 = AC.do(lambda e: e.activation(ss[:, :], ss[:, :], ACT.Sqrt, bias=eps[:, 0:1], scale=1 / 256), t1)
            t3 = DV.do(lambda e: e.reciprocal(ss[:, :], ss[:, :]), t2)
            tr = []
            for p8 in range(8):
                for h in range(4):
                    o = RES[:, p8, h * 256:h * 256 + 256]
                    c = 4 * p8 + h
                    t4 = DV.do(lambda e: e.tensor_scalar(o, o, ss[:, c:c + 1], None, ALU.mult), t3)
                tr.append(t4)
                if p8 % 2:
                    yield
            for half in range(2):
                for m in range(8):
                    q = j % 3
                    j += 1
                    tu = dma(f"ld{q}", ld[:, q, :], dR[m][:, half * 512:half * 512 + 512], written[("r", m)], ldf[q])
                    bk = [3, 4][m % 2]
                    for c in range(4):
                        p8 = 4 * half + c
                        f = (lambda e: e.transpose(B[bk][:, c * 128:c * 128 + 128], RES[:, p8, m * 128:m * 128 + 128], ident[:]))
                        if c < 3:
                            PE.quiet(f, tr[p8], bfree[bk])
                        else:
                            t = PE.do(f, tr[p8])
                    tg = AC.do(lambda e: e.activation(ld[:, q, :], ld[:, q, :], ACT.Silu), tu)
                    s, fr = take()
                    o = TMP[:, s, :]
                    t1 = DV.do(lambda e: e.scalar_tensor_tensor(out=o, in0=B[bk][:, :], scalar=vec("gn", m), in1=ld[:, q, :], op0=ALU.mult, op1=ALU.mult), t, tg, fr)
                    bfree[bk] = t1
                    ldf[q] = t1
                    store(s, dBo[m][:, half * 512:half * 512 + 512], o, ("bo", m), t1)
                    yield
            mt["oT"] = t

        run(beside(fill(["ga", "gb"]), mlp(), 57 / 30))
        run_later()
        barrier(("st", "so"))
        p3.close()

        p4 = ExitStack()
        NQ = 4
        lq = alloc(p4, [128, NQ, 512], F, "lq")
        FH = alloc(p4, [128, 4, T], R, "fh")
        FL = alloc(p4, [128, 4, T], R, "fl")
        lqs = {"i": 0, "free": [None] * NQ}

        def fetch(src, name, *tokens):
            q = lqs["i"] % NQ
            lqs["i"] += 1
            t = dma(f"lq{q}", lq[:, q, :], src, written[name] if name else None, lqs["free"][q], *tokens)
            return q, t

        def load_split(src, name, half, free):
            xtok[half] = [load_tile(src, k, half, written[(name, k)], free) for k in range(8)]

        def pairs(name, after, then=None):
            for p in range(4):
                ws = [wget(name, 2 * p), wget(name, 2 * p + 1)]
                for h in range(2):
                    r = products(ws, h)
                    for x, (b, t) in enumerate(r):
                        after(2 * p + x, h, b, t)
                    if p == 3 and then:
                        then(h, t)
                for i in ws:
                    wdone(i, t)

        banks["use"] = list(range(8))
        for h in range(2):
            load_split(dA, "a", h, pe_now())

        def gated(gate, key, add, toks):
            def after(m, h, b, t):
                q, tl = fetch(gate[m][:, h * 512:h * 512 + 512], key)
                y = RES[:, m, h * 512:h * 512 + 512]
                g = lq[:, q, :]
                ts = AC.do(lambda e: e.activation(g, g, ACT.Sigmoid), tl)
                if not add:
                    t1 = DV.do(lambda e: e.tensor_tensor(y, B[b][:, :], g, ALU.mult), t, ts, mt["oT"])
                    bfree[b] = t1
                else:
                    t0 = DV.do(lambda e: e.tensor_tensor(g, B[b][:, :], g, ALU.mult), t, ts)
                    bfree[b] = t0
                    t1 = DV.do(lambda e: e.tensor_tensor(y, y, g, ALU.add), t0)
                lqs["free"][q] = t1
                toks[(m, h)] = t1
            return after

        pairs("wa", gated(dGA, "ga", False, {}), lambda h, t: load_split(dBo, "bo", h, t))
        ty = {}
        ygone = {}

        def y_split(h, t):
            c = 512 * h
            outs = []
            for k in range(8):
                outs.append(split_to(XH[:, k, c:c + 512], XL[:, k, c:c + 512], RES[:, k, c:c + 512], ty[(k, h)], t))
                ygone[(k, h)] = outs[-1]
            xtok[h] = outs

        pairs("wb", gated(dGB, "gb", True, ty), y_split)

        def residual(gain, xsrc, key, tr, tacc):
            def after(m, h, b, t):
                q, tl = fetch(xsrc[m][:, h * 512:h * 512 + 512], key)
                y = RES[:, m, h * 512:h * 512 + 512]
                t1 = DV.do(lambda e: e.scalar_tensor_tensor(out=y, in0=B[b][:, :], scalar=gain(m), in1=lq[:, q, :], op0=ALU.mult, op1=ALU.add), t, tl, ygone.get((m, h)))
                bfree[b] = t1
                lqs["free"][q] = t1
                tr[(m, h)] = t1
                tacc[h] = square_sum(y, 512 * h, 512, m == 0, t1, tacc[h], eng=PO)
            return after

        def pairs_normed(name, after, scale, shift, tr, tacc):
            st = {}

            def norm(h, free, hooks=None):
                xtok[h] = norm_tiles(RES, 512 * h, 512, spread(st[h], 512), scale, shift, XH, XL, [tr[(k, h)] for k in range(8)], free, hooks=hooks)

            def sums(h):
                st[h] = rms_scale(rms_cols(512 * h, 512, tacc[h]), 512)

            for p in range(4):
                ws = [wget(name, 2 * p), wget(name, 2 * p + 1)]
                for h in range(2):
                    last = p == 3 and h == 1
                    r = products(ws, h, mids={4: lambda: sums(0)} if last else None)

                    def rest():
                        for x, (b, t) in enumerate(r):
                            after(2 * p + x, h, b, t)
                    if last:
                        norm(0, t0, {3: rest})
                    else:
                        rest()
                    if h == 0:
                        t0 = r[1][1]
                for i in ws:
                    wdone(i, r[1][1])
            t1 = r[1][1]
            defer[3] = lambda: sums(1)
            defer[6] = lambda: norm(1, t1)

        tr, tacc = {}, [None, None]
        pairs_normed("wo", residual(lambda m: MOD[:, 16 + m:17 + m], D["xT"], None, tr, tacc),
                     lambda k: GS[:, 16 + k:17 + k], lambda k: MOD[:, 24 + k:25 + k], tr, tacc)

        def ffn(one, two, gate_first, gain, tr, tacc, mid_last, sums):
            ffree = [None] * 4
            ftok = {}

            def second(g, last):
                ws = [wget(two, t) for t in g]
                for h in range(2):
                    for m in range(8):
                        b = bank()
                        o = B[b][:, :]
                        for x, (i, tt) in enumerate(zip(ws, g)):
                            s, w = tt % 4, i % NW
                            wh, wl = WH[:, w, m * 128:m * 128 + 128], WL[:, w, m * 128:m * 128 + 128]
                            xh, xl = FH[:, s, h * 512:h * 512 + 512], FL[:, s, h * 512:h * 512 + 512]
                            PE.quiet(lambda e: e.matmul(o, wh, xh, start=(x == 0), stop=False), bfree[b], wsplit[i], ftok[(tt, h)])
                            PE.quiet(lambda e: e.matmul(o, wh, xl, start=False, stop=False))
                            f = (lambda e: e.matmul(o, wl, xh, start=False, stop=(x == 1)))
                            if x < 1:
                                PE.quiet(f)
                            else:
                                t = PE.do(f)
                        y = RES[:, m, h * 512:h * 512 + 512]
                        tr[(m, h)] = DV.do(lambda e: e.scalar_tensor_tensor(out=y, in0=B[b][:, :], scalar=gain(m), in1=y, op0=ALU.mult, op1=ALU.add), t, tr.get((m, h)))
                        bfree[b] = tr[(m, h)]
                        if last:
                            sums(m, h, y)
                            if h == 1 and m in mid_last:
                                mid_last[m]()
                for i in ws:
                    wdone(i, t)
                for tt in g:
                    ffree[tt % 4] = t

            def first(tt, ws, h):
                s = tt % 4
                r = products(ws, h)
                (bg, tg), (bu, tu) = r if gate_first else r[::-1]
                q, fr = take()
                y = TMP[:, q, :]
                t2 = AC.do(lambda e: e.activation(y, B[bg][:, :], ACT.Silu), tg, fr)
                t3 = DV.do(lambda e: e.tensor_tensor(y, B[bu][:, :], y, ALU.mult), tu, t2)
                bfree[bg], bfree[bu] = t2, t3
                ftok[(tt, h)] = split_to(FH[:, s, h * 512:h * 512 + 512], FL[:, s, h * 512:h * 512 + 512], y, t3, ffree[s])
                ring["free"][q] = ftok[(tt, h)]
                ffn_x[h] = r[1][1]

            for gi, g in enumerate(GROUPS):
                if gi == 0:
                    ws = {tt: [wget(one, tt), wget(one, NF + tt)] for tt in g}
                    for tt in g:
                        first(tt, ws[tt], 0)
                    for tt in g:
                        first(tt, ws[tt], 1)
                        for i in ws[tt]:
                            wdone(i, ffn_x[1])
                else:
                    for tt in g:
                        ws = [wget(one, tt), wget(one, NF + tt)]
                        for h in range(2):
                            first(tt, ws, h)
                        for i in ws:
                            wdone(i, ffn_x[1])
                if gi:
                    second(GROUPS[gi - 1], False)
            second(GROUPS[-1], True)

        ffn_x = {}
        dX = scratch("x2", [8, 128, T])
        xst = {}
        tacc = [None, None]
        tfin = {}

        t_fn = DV.do(lambda e: e.tensor_tensor(FN[:, :], VEC[:, V["fin1"]:V["fin1"] + 8], VEC[:, V["nm2"]:V["nm2"] + 8], ALU.mult), t_vec)
        tacc2 = [None, None]
        two = {}

        def sums1(m, h, y):
            tacc2[h] = square_sum(y, 512 * h, 512, m == 0, tr[(m, h)], tacc2[h], acc=RB, scale=vec("fin1", m))
            tacc[h] = square_sum(y, 512 * h, 512, m == 0, tr[(m, h)], tacc[h], eng=PO)

        def cols2(h):
            b1, t1 = rms_cols(512 * h, 512, tacc[h])
            b2, t2 = rms_cols(512 * h, 512, tacc2[h], RB)
            r, r12 = RC[:, h, :], R12[:, h, :]
            ta, tb = root(r, B[b1][:, 0:4], t1, rc["free"])
            bfree[b1] = ta
            t = DV.do(lambda e: e.tensor_tensor(r12, B[b2][:, 0:4], r, ALU.mult), t2, tb)
            bfree[b2] = t
            t = DV.do(lambda e: e.tensor_tensor(r12, r12, r, ALU.mult), t)
            ta, t = root(r12, r12, t)
            t = DV.do(lambda e: e.tensor_tensor(r12, r12, r, ALU.mult), t)
            two[h] = [diagonal(r12, 512, t), diagonal(r, 512, tb)]
            rc["free"][h] = two[h][1][1]

        def spread2(h):
            two[h][0] = spread(two[h][0], 512)

        def norm2(h, free):
            xtok[h] = norm_tiles(RES, 512 * h, 512, two[h][0], lambda k: FN[:, k:k + 1], None, XH, XL, [tr[(k, h)] for k in range(8)], free, t_fn)

        def input2(h):
            c = 512 * h
            b, t1 = spread(two[h][1], 512)
            for k in range(8):
                x = RES[:, k, c:c + 512]
                t = DV.do(lambda e: e.scalar_tensor_tensor(out=x, in0=x, scalar=vec("fin1", k), in1=B[b][:, :], op0=ALU.mult, op1=ALU.mult), t1)
                xst[(k, h)] = dma_out(f"xo{k}", dX[k][:, c:c + 512], x, t)
                written.setdefault("x2", []).append(xst[(k, h)])
            bfree[b] = t

        ffn("f1", "f2", False, lambda m: MOD[:, 40 + m:41 + m], tr, tacc, {2: lambda: cols2(0), 5: lambda: spread2(0)}, sums1)
        free_ffn = so_far(("xo",))
        norm2(0, ffn_x[0])
        defer[2] = lambda: cols2(1)
        defer[4] = lambda: (spread2(1), norm2(1, ffn_x[1]))

        dU2 = scratch("u2", [8, 128, T])
        dG2 = scratch("g2", [8, 128, T])
        dZ0 = scratch("z0", [8, 128, T])
        dZ1 = scratch("z1", [8, 128, T])
        dM = scratch("mg", [8, 128, T])
        dQ2 = scratch("q2", [8, 128, T])
        dK2 = scratch("k2", [2, 128, T])
        dV2 = scratch("v2", [8, 128, 256])
        dY = scratch("y", [8, 128, T])

        pu, pg, pz0 = put_plain(dU2, "u2", TC), put_plain(dG2, "g2", TC), put_plain(dZ0, "z0", TC)
        ws = [wget(n, 0) for n in ("u2", "g2", "z0")]
        for h in range(2):
            r = products(ws, h)
            for put, (b, t) in zip((pu, pg, pz0), r):
                put(0, TC + 512 * h, 512, B[b][:, :], b, t)
            input2(h)
        for i in ws:
            wdone(i, r[2][1])
        p4.close()
        join(free_ffn)
        p5 = ExitStack()
        S5 = lambda shape, dt, name="t": alloc(p5, shape, dt, name)
        UCs, HH, SQ = [RES[:, 0, :], RES[:, 1, :]], RES[:, 6, :], RES[:, 7, :]
        Rg = [RES[:, 2, :], RES[:, 3, :]]
        Ig = [RES[:, 4, :], RES[:, 5, :]]
        UP = S5([128, T + 3], F, "up")
        UH = S5([128, T], R, "uh")
        UL = S5([128, T], R, "ul")
        GL = S5([128, T], F, "gl")
        Z0 = S5([128, T], F, "z0")
        BD = S5([128, 512], F, "bd")
        BH = S5([128, 512], R, "bh")
        BL = S5([128, 512], R, "bl")
        SPL = S5([128, 16], F, "spl")
        s12 = S5([128, 2, 16], F, "s12")
        tm = S5([128, 4, T], F, "tm")
        lam = VEC[:, V["lam"]:V["lam"] + 16]
        s1, s2 = s12[:, 0, :], s12[:, 1, :]
        t1 = AC.do(lambda e: e.activation(s1, lam, ACT.Abs))
        t1 = AC.do(lambda e: e.activation(s1, s1, ACT.Exp, scale=-1.0), t1)
        t1 = AC.do(lambda e: e.activation(s1, s1, ACT.Ln, bias=ones[:, 0:1]), t1)
        t2 = DV.do(lambda e: e.tensor_scalar(s2, lam, -1.0, 0.0, ALU.mult, ALU.max))
        t2 = DV.do(lambda e: e.tensor_tensor(s2, s2, s1, ALU.add), t1, t2)
        t_spl = DV.do(lambda e: e.tensor_scalar(SPL[:, :], s2, -8.0, None, ALU.mult), t2)
        t_up = DV.do(lambda e: e.memset(UP[:], 0.0))
        banks["use"] = [0, 1]
        fr = {}
        xs = list(xst.values()) + xtok[0] + xtok[1]
        for k in (("UC", 0), ("UC", 1), "HH", "SQ", ("G", 0), ("G", 1)):
            fr[k] = xs
        mid = {"n": 0}

        def conv(m):
            UC = UCs[m % 2]
            tu = dma("up", UP[:, 2:T + 2], dU2[m], written[("u2", m)], fr.get("UP"), t_up)
            tb = dma("bd", BD[:], D["lruw"][m], fr.get("BD"))
            yield
            yield
            tbs = split_to(BH[:, :], BL[:, :], BD[:, :], tb, fr.get("BH"))
            fr["BD"] = tbs
            t = DV.do(lambda e: e.tensor_scalar(UC, UP[:, 0:T], vec("cw", 4 * m), None, ALU.mult), tu, fr.get(("UC", m % 2)))
            for c in range(1, 4):
                t = DV.do(lambda e: e.scalar_tensor_tensor(out=UC, in0=UP[:, c:c + T], scalar=vec("cw", 4 * m + c), in1=UC, op0=ALU.mult, op1=ALU.add), t)
                if c == 2:
                    yield
            fr["UP"] = t
            tuc = DV.do(lambda e: e.tensor_scalar(UC, UC, vec("cb", m), None, ALU.add), t)
            cv[m] = (tuc, tbs, split_to(UH[:, :], UL[:, :], UC, tuc, fr.get("UH")))
            yield

        def lru_tile(m):
            UC = UCs[m % 2]
            tuc, tbs, tsp = cv[m]
            tg = dma("gl", GL[:], dG2[m], written[("g2", m)], fr.get("GL"))
            tz = dma("z0", Z0[:], dZ0[m], written[("z0", m)], fr.get("GL"))
            gt = {}
            for d in range(2):
                for w in range(2):
                    for h in range(2):
                        b = 4 + mid["n"] % 4
                        mid["n"] += 1
                        c = (2 * d + w) * 128
                        o = B[b][:, :]
                        xh, xl = UH[:, h * 512:h * 512 + 512], UL[:, h * 512:h * 512 + 512]
                        PE.quiet(lambda e: e.matmul(o, BH[:, c:c + 128], xh, start=True, stop=False), bfree[b], tsp, tbs)
                        PE.quiet(lambda e: e.matmul(o, BH[:, c:c + 128], xl, start=False, stop=False))
                        t = PE.do(lambda e: e.matmul(o, BL[:, c:c + 128], xh, start=False, stop=True))
                        dst = (Rg if w == 0 else Ig)[d][:, h * 512:h * 512 + 512]
                        bias = vec("lba" if w == 0 else "lbx", 8 * d + m)
                        gt[(d, w, h)] = AC.do(lambda e: e.activation(dst, o, ACT.Sigmoid, bias=bias), t, fr.get(("G", d)))
                        bfree[b] = gt[(d, w, h)]
                yield
            fr["UH"] = t
            fr["BH"] = t
            tz = AC.do(lambda e: e.activation(Z0[:, :], Z0[:, :], ACT.Sigmoid, bias=vec("bg", m)), tz)
            tt, ta, ti = {}, {}, {}
            for d in range(2):
                r, w0, w1 = Rg[d], tm[:, 2 * d, :], tm[:, 2 * d + 1, :]
                tla = DV.do(lambda e: e.tensor_scalar(r, r, SPL[:, 8 * d + m:8 * d + m + 1], None, ALU.mult), gt[(d, 0, 0)], gt[(d, 0, 1)], t_spl)
                tt[d] = AC.do(lambda e: e.activation(w0, r, ACT.Tanh, scale=-0.5), tla, fr.get(("tm", d)))
                ta[d] = AC.do(lambda e: e.activation(r, r, ACT.Exp), tt[d])
            yield
            for d in range(2):
                i, w1 = Ig[d], tm[:, 2 * d + 1, :]
                ti[d] = DV.do(lambda e: e.tensor_tensor(i, i, UC, ALU.mult), gt[(d, 1, 0)], gt[(d, 1, 1)], tuc)
            fr[("UC", m % 2)] = ti[1]
            ts, tin = {}, {}
            for d in range(2):
                w0 = tm[:, 2 * d, :]
                ts[d] = AC.do(lambda e: e.activation(w0, w0, ACT.Sqrt), tt[d])
            yield
            for d in range(2):
                r, i, w0, w1 = Rg[d], Ig[d], tm[:, 2 * d, :], tm[:, 2 * d + 1, :]
                tb3 = DV.do(lambda e: e.scalar_tensor_tensor(out=w1, in0=r, scalar=1.0, in1=w0, op0=ALU.add, op1=ALU.mult), ta[d], ts[d], fr.get(("tm", d)))
                tin[d] = DV.do(lambda e: e.tensor_tensor(i, i, w1, ALU.mult), ti[d], tb3)
                fr[("tm", d)] = tin[d]
                if d == 0:
                    yield
            tg = AC.do(lambda e: e.activation(GL[:, :], GL[:, :], ACT.Gelu_apprx_tanh), tg)
            th = DV.do(lambda e: e.tensor_tensor_scan(HH, Rg[0], Ig[0], 0.0, ALU.mult, ALU.add), tin[0], fr.get("HH"))
            fr[("G", 0)] = th
            th2 = DV.do(lambda e: e.tensor_tensor_scan(SQ[:, ::-1], Rg[1][:, ::-1], Ig[1][:, ::-1], 0.0, ALU.mult, ALU.add), tin[1], fr.get("SQ"))
            fr[("G", 1)] = th2
            yield
            t = DV.do(lambda e: e.tensor_tensor(HH, HH, SQ, ALU.add), th, th2)
            fr["SQ"] = t
            t = DV.do(lambda e: e.tensor_tensor(HH, HH, GL[:, :], ALU.mult), t, tg)
            t = DV.do(lambda e: e.tensor_tensor(HH, HH, Z0[:, :], ALU.mult), t, tz)
            fr["GL"] = t
            t = dma_out("mg", dM[m], HH, t)
            fr["HH"] = t
            written.setdefault("mg", []).append(t)
            yield

        def put_tanh(m, col, n, ps, b, t):
            s, fr = take()
            o = TMP[:, s, 0:n]
            t2 = AC.do(lambda e: e.activation(o, ps, ACT.Tanh, bias=BG2[:, m:m + 1], scale=0.5), t, fr, t_bg2)
            bfree[b] = t2
            store(s, dZ1[m][:, col - TC:col - TC + n], o, ("z1", m), t2)

        cv = {}

        def lru():
            yield from conv(0)
            yield
            for m in range(8):
                back = lru_tile(m)
                next(back)
                yield
                next(back)
                yield
                front = conv(m + 1) if m < 7 else iter(())
                live = True
                while live:
                    live = next(front, 0) is None
                    live2 = next(back, 0) is None
                    live = live or live2
                    if live:
                        yield

        def fill_b():
            for m in range(1, 8):
                yield from project("u2", m, False, pu)
                yield from project("g2", m, False, pg)
                yield from project("z0", m, False, pz0)
            for m in range(2):
                yield from project("k2", m, False, put_plain(dK2, "k2", TC))
            for m in range(2):
                yield from project("v2", m, False, put_turned(dV2, "v2", TC, 2))
            for m in range(4):
                yield from project("q2", m, False, put_plain(dQ2, "q2", TC, scale=0.125))
            for m in range(4):
                yield from project("z1", m, False, put_tanh)

        vf["free"] = [xtok[0][7] + xtok[1][7]] * 4
        run(beside(fill_b(), lru(), 1))
        run_later()
        barrier(("st", "so"))
        p5.close()

        p6 = ExitStack()
        S6 = lambda shape, dt, name="t": alloc(p6, shape, dt, name)
        K1 = S6([128, 2, T], R, "k1")
        K2 = S6([128, 2, T], R, "k2")
        QS = [S6([128, 4, 128], R, "qs") for _ in range(3)]
        PT = [S6([128, 4, 3, 128], F, "pt") for _ in range(2)]
        PR = [RES[:, 0:2, :].rearrange("p a t -> p (a t)")[:, 0:1536].rearrange("p (h s) -> p h s", h=4), S6([128, 4, 384], F, "pr"), S6([128, 4, 384], F, "pr")]
        Vt = RES[:, 3:6, :].rearrange("p a t -> p (a t)").rearrange("p (c q f) -> p c q f", c=8, q=2)
        QD = [ACC[:, 0:512].rearrange("p (h t) -> p h t", h=4), ACC[:, 512:1024].rearrange("p (h t) -> p h t", h=4),
              RB[:, 0:512].rearrange("p (h t) -> p h t", h=4)]
        KD = [RES[:, 7, :], RES[:, 2, :]]
        ZB = RES[:, 6, 0:512].rearrange("p (a t) -> p a t", a=4)
        MB = RES[:, 6, 512:1024].rearrange("p (a t) -> p a t", a=4)
        ADD = S6([128, 384], F, "ad")
        mx_ = [S6([128, 4], F, "mx") for _ in range(2)]
        es_ = [S6([128, 4], F, "es") for _ in range(2)]
        dn_ = [S6([128, 4], F, "dn") for _ in range(2)]
        banks["use"] = [0, 1]
        slopes = [float(2.0 ** (-8.0 * (h + 1) / 16)) for h in range(16)]
        one = {}
        units = [(pair, blk, kv) for pair in range(2) for blk in range(8) for kv in range(2)]

        def key_load(pair, x):
            src = dK2[pair][64 * x:64 * x + 64, :]
            one[("kd", x)] = [dma(f"kd{x}{y}", KD[x][64 * y:64 * y + 64, :], src, written[("k2", pair)], one.get(("kfree", x))) for y in range(2)]

        def key_split(x):
            t3 = AC.do(lambda e: e.activation(K1[:, x, :], KD[x], ACT.Copy), one[("kd", x)], one.get(("scores", x)))
            t4 = DV.do(lambda e: e.tensor_tensor(K2[0:64, x, :], KD[x][0:64, :], K1[0:64, x, :].bitcast(F), ALU.subtract), t3, one.get(("scores", x)))
            one[("kfree", x)] = [t3, t4]
            one[("K", x)] = [t3, t4, t_k0]

        def q_load(u):
            pair, blk, kv = units[u]
            src = dQ2[4 * pair:4 * pair + 4, 64 * kv:64 * kv + 64, blk * 128:blk * 128 + 128].rearrange("a p t -> p a t")
            one[("q", u)] = [dma(f"qd{u % 3}{y}", QD[u % 3][64 * y:64 * y + 64, :, :], src, [written[("q2", 4 * pair + a)] for a in range(4)], one.get(("qfree", u - 3)))
                             for y in range(2)]

        def q_high(u):
            Q, qd = QS[u % 3], QD[u % 3]
            one[("qh", u)] = AC.do(lambda e: e.activation(Q[:, :, :], qd, ACT.Copy), one[("q", u)], one.get(("sc", u - 3)))

        def q_low(u):
            Q, qd = QS[u % 3], QD[u % 3]
            t1 = one[("qh", u)]
            t2 = DV.do(lambda e: e.tensor_tensor(Q[64:128, :, :], qd[64:128, :, :], Q[64:128, :, :].bitcast(F), ALU.subtract), t1)
            one[("qfree", u)] = [t1, t2]

        def span(u):
            blk = units[u][1]
            k0, k1 = max(0, blk - 1), min(8, blk + 2)
            return k0, (k1 - k0) * 128, (k0 - blk + 1) * 128

        def scores(u):
            pair, blk, kv = units[u]
            k0, n, a0 = span(u)
            P, Q = PR[u % 3], QS[u % 3]
            for a in range(4):
                b = 2 + one["sb"] % 3
                one["sb"] += 1
                head = 4 * (2 * pair + kv) + a
                o = B[b][:, 0:n]
                PE.quiet(lambda e: e.matmul(o, Q[:, a, :], K1[:, kv, k0 * 128:k0 * 128 + n], start=True, stop=False), bfree[b], one[("qfree", u)], one[("K", kv)])
                t = PE.do(lambda e: e.matmul(o, Q[:, a, :], K2[:, kv, k0 * 128:k0 * 128 + n], start=False, stop=True))
                t1 = DV.do(lambda e: e.scalar_tensor_tensor(out=P[:, a, 0:n], in0=ADD[:, a0:a0 + n], scalar=-slopes[head], in1=o, op0=ALU.mult, op1=ALU.add),
                           t, t_ad, one.get(("P", u - 3)))
                bfree[b] = t1
            one[("sc", u)] = t
            one[("scores", kv)] = t
            one[("s", u)] = t1

        def exps(u):
            pair, blk, kv = units[u]
            k0, n, a0 = span(u)
            P, mx, es, dn = PR[u % 3], mx_[u % 2], es_[u % 2], dn_[u % 2]
            t1 = one[("s", u)]
            c = V["sink"] + 8 * pair + 4 * kv
            sink = VEC[:, c:c + 4]
            t2 = DV.do(lambda e: e.tensor_reduce(mx[:, :], P[:, :, 0:n], AX.X, ALU.max), t1, one.get(("mx", u - 2)))
            t3 = DV.do(lambda e: e.tensor_tensor(mx[:, :], mx[:, :], sink, ALU.max), t2)
            t4 = DV.do(lambda e: e.tensor_tensor(es[:, :], sink, mx[:, :], ALU.subtract), t3, one.get(("es", u - 2)))
            t5 = DV.do(lambda e: e.tensor_scalar(mx[:, :], mx[:, :], -1.0, None, ALU.mult), t4)
            t6 = AC.do(lambda e: e.activation(es[:, :], es[:, :], ACT.Exp), t4)
            for a in range(4):
                t7 = AC.do(lambda e: e.activation(P[:, a, 0:n], P[:, a, 0:n], ACT.Exp, bias=mx[:, a:a + 1], accum_out=dn[:, a:a + 1]), t5, one.get(("dn", u - 2)))
            one[("mx", u)] = t7
            one[("e", u)] = (t6, t7)

        def divide(u):
            k0, n, a0 = span(u)
            P, es, dn = PR[u % 3], es_[u % 2], dn_[u % 2]
            t8 = DV.do(lambda e: e.tensor_tensor(dn[:, :], dn[:, :], es[:, :], ALU.add), *one[("e", u)])
            one[("es", u)] = t8
            t9 = DV.do(lambda e: e.reciprocal(dn[:, :], dn[:, :]), t8)
            one[("d", u)] = [DV.do(lambda e: e.tensor_scalar(P[:, a, 0:n], P[:, a, 0:n], dn[:, a:a + 1], 0.5, ALU.mult, ALU.mult), t9) for a in range(4)]
            one[("dn", u)] = one[("d", u)][-1]

        def turn(u):
            k0, n, a0 = span(u)
            P, pt = PR[u % 3], PT[u % 2]
            one[("pt", u)] = []
            for a in range(4):
                b = 5 + a % 2
                for c in range(n // 128):
                    g = (lambda e: e.transpose(B[b][:, c * 128:c * 128 + 128], P[:, a, c * 128:c * 128 + 128], ident[:]))
                    if c < n // 128 - 1:
                        PE.quiet(g, one[("d", u)][a], bfree[b])
                    else:
                        t = PE.do(g)
                dst = pt[:, a, 0:n // 128, :]
                src = B[b][:, 0:n].rearrange("p (c t) -> p c t", t=128)
                tc = AC.do(lambda e: e.activation(dst, src, ACT.Copy), t, one.get(("pv", u - 2)))
                bfree[b] = tc
                one[("pt", u)].append(tc)
            one[("P", u)] = t

        def weigh(u):
            pair, blk, kv = units[u]
            k0, n, a0 = span(u)
            o = B[7][:, :].rearrange("p (a t) -> p a t", a=4)
            for c in range(n // 128):
                g = (lambda e: e.matmul(o, Vt[:, k0 + c, pair, 64 * kv:64 * kv + 128], PT[u % 2][:, :, c, :], start=(kv == 0 and c == 0), stop=(kv == 1 and c == n // 128 - 1)))
                if c < n // 128 - 1:
                    PE.quiet(g, one[("pt", u)], tV, bfree[7])
                else:
                    t = PE.do(g)
            one[("pv", u)] = t
            if kv == 1:
                tz, tm_ = one["zm"]
                t1 = DV.do(lambda e: e.scalar_tensor_tensor(out=ZB, in0=ZB, scalar=1.0, in1=o, op0=ALU.add, op1=ALU.mult), t, tz)
                bfree[7] = t1
                s, fs = take()
                so = TMP[:, s, :].rearrange("p (a t) -> p a t", a=4)
                t2 = PO.do(lambda e: e.tensor_tensor(so, ZB, MB, ALU.add), t1, tm_, fs)
                one["z"] = t2
                store(s, dY[4 * pair:4 * pair + 4, :, blk * 128:blk * 128 + 128].rearrange("a p t -> p a t"), so, ("y", pair, blk), t2)

        def gate_load(u):
            pair, blk, kv = units[u]
            tiles, c0 = slice(4 * pair, 4 * pair + 4), blk * 128
            tz = dma("zb", ZB, dZ1[tiles, :, c0:c0 + 128].rearrange("a p t -> p a t"), [written[("z1", 4 * pair + a)] for a in range(4)], one.get("z"))
            tm_ = dma("mb", MB, dM[tiles, :, c0:c0 + 128].rearrange("a p t -> p a t"), written["mg"], one.get("z"))
            one["zm"] = (tz, tm_)

        def y_load(k, h):
            yraw.append((k, h, load_raw(dY, k, h, [written[("y", k // 4, blk)] for blk in range(4 * h, 4 * h + 4)])))

        def y_split():
            k, h, st = yraw.pop(0)
            ynew[h][k] = split_tile(k, h, st, one["x"])

        yraw = []

        ynew = [[None] * 8, [None] * 8]

        def attention():
            n = len(units)
            todo = [(k, h) for k in range(4) for h in range(2)] + [(k, 0) for k in range(4, 8)] + [(k, 1) for k in range(4, 8)]
            for u in range(n + 3):
                if u + 2 < n:
                    q_load(u + 2)
                if u == 8:
                    key_load(1, 0)
                    key_load(1, 1)
                if u < n:
                    scores(u)
                if u + 1 < n:
                    q_high(u + 1)
                if 2 <= u <= n + 1:
                    turn(u - 2)
                if u == 15:
                    key_split(0)
                if u == 16:
                    key_split(1)
                if u < n:
                    exps(u)
                if 1 <= u <= n:
                    divide(u - 1)
                if u + 1 < n:
                    q_low(u + 1)
                if u >= 3:
                    weigh(u - 3)
                if 2 <= u <= n + 1 and units[u - 2][2] == 0:
                    gate_load(u - 2)
                if u == 19:
                    one["x"] = pe_now()
                if yraw:
                    y_split()
                if u >= 20 and (todo[0][0] < 4 or (u >= 27 and todo[0][1] == 0)):
                    y_load(*todo.pop(0))
                yield
            for k, h in todo:
                y_load(k, h)
                if len(yraw) > 2:
                    y_split()
            while yraw:
                y_split()

        def fill_c():
            for m in range(4, 8):
                yield from project("q2", m, False, put_plain(dQ2, "q2", TC, scale=0.125))
            for m in range(4, 8):
                yield from project("z1", m, False, put_tanh)

        key_load(0, 0)
        q_load(0)
        t_k0 = DV.do(lambda e: e.memset(K2[64:128, :, :].bitcast(F), 0.0))
        key_load(0, 1)
        q_load(1)
        key_split(0)
        q_high(0)
        q_low(0)
        key_split(1)
        t_v0 = DV.do(lambda e: e.memset(RES[:, 3:6, :], 0.0))
        t_ad = dma("adb", ADD[:], D["alibi"])
        tV = []
        for q in range(2):
            for x in range(2):
                tV.append(dma(f"vt{q}{x}", Vt[:, :, q, 128 * x:128 * x + 64], dV2[:, :, 128 * q + 64 * x:128 * q + 64 * x + 64].rearrange("c p f -> p c f"), written["v2"], t_v0))
        one["sb"] = 0
        run(beside(fill_c(), attention(), 1, -1))
        run_later()
        barrier()
        p6.close()

        p4 = ExitStack()
        lq = alloc(p4, [128, NQ, 512], F, "lq")
        FH = alloc(p4, [128, 4, T], R, "fh")
        FL = alloc(p4, [128, 4, T], R, "fl")
        lqs["free"] = [None] * NQ
        banks["use"] = list(range(8))
        xtok[0], xtok[1] = ynew
        ygone.clear()
        tr, tacc = {}, [None, None]
        pairs_normed("wo2", residual(lambda m: ones[:, 0:1], dX, "x2", tr, tacc), lambda k: vec("nf2", k), None, tr, tacc)
        tacc = [None, None]

        def sums2(m, h, y):
            tacc[h] = square_sum(y, 512 * h, 512, m == 0, tr[(m, h)], tacc[h], eng=PO)

        fin = {}

        def last_sums(h):
            fin[h] = rms_scale(rms_cols(512 * h, 512, tacc[h]), 512)

        def last_spread(h):
            fin[h] = spread(fin[h], 512)

        def last_tiles(h):
            c = 512 * h
            b, trb = fin[h]
            for k in range(8):
                x = RES[:, k, c:c + 512]
                t = DV.do(lambda e: e.scalar_tensor_tensor(out=x, in0=x, scalar=vec("nfin", k), in1=B[b][:, :], op0=ALU.mult, op1=ALU.mult), trb)
                dma(f"x{k}", out[k][:, c:c + 512], x, t)
                yield
            bfree[b] = t

        half0 = last_tiles(0)
        some = lambda: next(half0)
        ffn("f12", "f22", True, lambda m: ones[:, 0:1], tr, tacc, {2: lambda: last_sums(0), 4: lambda: last_spread(0), 5: some, 6: some, 7: some}, sums2)
        last_sums(1)
        run(half0)
        last_spread(1)
        run(last_tiles(1))
        assert state["next"] == len(order)
        SP.wait([(k, v) for k, v in dma.n.items()])
        p4.close()


VECTORS = [("b_ada", 48), ("n1", 8), ("n2", 8), ("b_al", 8), ("gn", 8), ("nm2", 8), ("lam", 16), ("lba", 16), ("lbx", 16),
           ("cw", 32), ("cb", 8), ("bg", 16), ("sink", 16), ("nf2", 8), ("nfin", 8), ("fin1", 8)]
assert sum(n for _, n in VECTORS) <= 240


def layout(x, c, ctx, c_ctx, w_ada, b_ada, norm1_g, w_in, ln_v_g, ln_v_b, w_spatial, b_spatial,
           w_alpha_f, b_alpha_f, w_alpha_b, b_alpha_b, gla_norm_g, w_branch_a, w_branch_b, w_out,
           norm2_g, w_ffn_in, w_ffn_out, final_norm_g, norm_mix_g_2, w_in_2, b_gate_2, conv_w_2,
           conv_b_2, lru_lambda_2, lru_wa_2, lru_ba_2, lru_wx_2, lru_bx_2, attn_sink_2, w_out_2,
           norm_ffn_g_2, w_ffn_in_2, w_ffn_out_2, norm_final_g_2):
    def cols(v):
        return np.asarray(v).reshape(-1, 128).T

    def tiles(w, width=128):
        k, m = w.shape
        return np.ascontiguousarray(w.reshape(k // 128, 128, m // width, width).transpose(2, 1, 0, 3).reshape(m // width, 128, k // 128 * width))

    f = np.float32
    heads = np.array([h for a in range(2) for i in range(4) for h in (8 * a + i, 8 * a + 4 + i)])
    perm = (heads[:, None] * 64 + np.arange(64)).reshape(-1)
    D = {}
    D["xT"] = np.ascontiguousarray(x[0].T).reshape(8, 128, 1024)
    D["ctxT"] = np.ascontiguousarray(ctx[0].T.reshape(8, 128, 256).transpose(1, 0, 2))
    D["cc"] = np.ascontiguousarray(np.stack([c[0].reshape(8, 128), c_ctx.reshape(8, 128)], -1).transpose(1, 0, 2))
    D["crow"] = np.ascontiguousarray(np.broadcast_to(c[0], (128, 1024)))
    D["ada"] = np.ascontiguousarray(w_ada[0][:, 0:2048].reshape(8, 128, 2048))
    D["adaT"] = np.ascontiguousarray(w_ada[0][:, 2048:].T).reshape(32, 128, 1024)
    w = w_in[0]
    at = 0
    for name, n in (("u", 1024), ("v", 1024), ("q", 512), ("k", 512), ("vv", 1024), ("r", 1024), ("al", 32), ("ga", 1024), ("gb", 1024)):
        part = w[:, at:at + n]
        D["W" + name] = tiles(np.tile(part, (1, 4)) if name == "al" else part)
        at += n
    D["Wwa"], D["Wwb"], D["Wwo"] = tiles(w_branch_a[0]), tiles(w_branch_b[0]), tiles(w_out[0])
    D["Wf1"] = tiles(w_ffn_in[0])
    D["Wf2"] = np.ascontiguousarray(w_ffn_out[0]).reshape(22, 128, 1024)
    wal = np.zeros((128, 2, 512), f)
    for i in range(3):
        wal[32 * i:32 * i + 16, 0] = w_alpha_f[0]
        wal[32 * i + 16:32 * i + 32, 1] = w_alpha_b[0]
    D["walpha"] = wal
    D["wspT"] = np.ascontiguousarray(w_spatial[0].transpose(2, 0, 1)).reshape(128, 1024)
    D["bspb"] = np.ascontiguousarray(np.broadcast_to(b_spatial[0].reshape(1, 1024), (128, 1024)))
    D["lnvb"] = np.ascontiguousarray(np.broadcast_to(np.stack([ln_v_g[0], ln_v_b[0]]), (128, 2, 1024)))
    w = w_in_2[0]
    D["Wu2"], D["Wg2"] = tiles(w[:, 0:1024][:, perm]), tiles(w[:, 1024:2048][:, perm])
    D["Wq2"], D["Wk2"], D["Wv2"] = tiles(w[:, 2048:3072][:, perm]), tiles(w[:, 3072:3328]), tiles(w[:, 3328:3584])
    D["Wz0"], D["Wz1"] = tiles(w[:, 3584:4608][:, perm]), tiles(w[:, 4608:5632][:, perm])
    D["Wwo2"] = tiles(w_out_2[0][perm])
    D["Wf12"] = tiles(w_ffn_in_2[0])
    D["Wf22"] = np.ascontiguousarray(w_ffn_out_2[0]).reshape(22, 128, 1024)
    lw = np.zeros((8, 128, 4, 128), f)
    for m in range(8):
        for j in range(2):
            h = heads[2 * m + j]
            for d in range(2):
                for y, src in enumerate((lru_wa_2, lru_wx_2)):
                    lw[m, 64 * j:64 * j + 64, 2 * d + y, 64 * j:64 * j + 64] = src[0, d, h]
    D["lruw"] = lw.reshape(8, 128, 512)
    bg = b_gate_2[0].reshape(2, 1024)[:, perm]
    parts = {
        "b_ada": cols(b_ada[0]), "n1": cols(norm1_g[0]), "n2": cols(norm2_g[0]),
        "b_al": np.concatenate([cols(b_alpha_f[0]), cols(b_alpha_b[0])], 1), "gn": cols(gla_norm_g[0]),
        "nm2": None, "lam": cols(lru_lambda_2[0][:, perm]), "lba": cols(lru_ba_2[0][:, perm]), "lbx": cols(lru_bx_2[0][:, perm]),
        "cw": conv_w_2[0][:, perm].reshape(4, 8, 128).transpose(2, 1, 0).reshape(128, 32), "cb": cols(conv_b_2[0][perm]),
        "bg": cols(bg), "sink": np.broadcast_to(attn_sink_2[0], (128, 16)), "nf2": cols(norm_ffn_g_2[0]), "nfin": cols(norm_final_g_2), "fin1": cols(final_norm_g),
    }
    parts["nm2"] = cols(norm_mix_g_2[0])
    v = np.concatenate([parts[n] for n, _ in VECTORS], 1)
    D["vec"] = np.ascontiguousarray(np.concatenate([v, np.zeros((128, 240 - v.shape[1]), f)], 1))
    D["ident"] = np.eye(128, dtype=f)
    cm = np.ones((128, 512), f)
    cm[:, ::64] = 0
    D["cmask"] = cm
    j, i = np.arange(128)[:, None], np.arange(128)[None]
    D["amask0"] = ((j // 64 == i // 64) & (j <= i)).astype(np.int32)
    D["amask1"] = ((j // 64 == i // 64) & (j >= i)).astype(np.int32)
    s = np.arange(384)[None]
    dist = np.abs(j + 128 - s)
    D["alibi"] = np.where(dist <= 128, dist, 1e34).astype(f)
    return D


def kernel(**inputs):
    import concourse.bacc as bacc
    from concourse.bass_utils import run_bass_kernel_spmd

    D = layout(**{k: np.asarray(v) for k, v in inputs.items()})
    nc = bacc.Bacc("TRN2", target_bir_lowering=False, num_devices=1)
    aps = {n: nc.dram_tensor("i_" + n, a.shape, mybir.dt.from_np(a.dtype), kind="ExternalInput").ap() for n, a in D.items()}
    out = nc.dram_tensor("o_out", (8, 128, 1024), F, kind="ExternalOutput").ap()
    program(nc, aps, out)
    r = run_bass_kernel_spmd(nc, [{"i_" + n: a for n, a in D.items()}], core_ids=[0])
    y = np.asarray(r.results[0]["o_out"])
    return np.ascontiguousarray(y.reshape(1024, 1024).T)[None]
```
